# Optimizing a Trainium2 kernel written in Bass

```python
import jax, jax.numpy as jnp
from jax import lax
import numpy as np

D_MODEL = 1024
BATCH = 1
SEQ = 512
DEPTH = 2

N_META = 16
EPS = 1e-6
D_FF = 11 * D_MODEL // 4
BRANCH_W = D_MODEL // 2
N_BRANCH = 3
CONV_W = BRANCH_W
CONV_K = 3
ATT_HEAD_DIM = 64
ATT_HEADS = BRANCH_W // ATT_HEAD_DIM
ATT_KV_HEADS = 2
ATT_W = ATT_HEADS * ATT_HEAD_DIM
IDX_HEADS = 4
IDX_HEAD_DIM = ATT_HEAD_DIM
IDX_TOPK_MAX = 256
Q_BLOCK = 128
MLSTM_HEADS = 4
MLSTM_HEAD_DIM = BRANCH_W // MLSTM_HEADS
MLSTM_W = MLSTM_HEADS * MLSTM_HEAD_DIM
MLSTM_CHUNK = 64
ROPE_THETA = 10000.0

SPLIT_SIZES = (CONV_W, CONV_W, CONV_W,
               ATT_W, ATT_KV_HEADS * ATT_HEAD_DIM, ATT_KV_HEADS * ATT_HEAD_DIM,
               IDX_HEADS * IDX_HEAD_DIM, IDX_HEAD_DIM, IDX_HEADS,
               MLSTM_W, MLSTM_W, MLSTM_W, MLSTM_W, MLSTM_HEADS, MLSTM_HEADS,
               N_BRANCH * D_MODEL)
IN_W = sum(SPLIT_SIZES)

kernel_name = 'hybrid_conv_dsa_mlstm_macaron_trunk'

def rmsnorm(x, g):
    xf = x.astype(jnp.float32)
    y = xf * lax.rsqrt(jnp.mean(xf * xf, axis=-1, keepdims=True) + EPS)
    return (y * g).astype(x.dtype)

def headwise_rmsnorm(h, g):
    hf = h.astype(jnp.float32)
    y = hf * lax.rsqrt(jnp.mean(hf * hf, axis=-1, keepdims=True) + EPS)
    return (y.reshape(h.shape[:2] + (-1,)) * g).astype(h.dtype)

def swiglu(u, w_gu, w_down):
    gate, up = jnp.split(u @ w_gu, 2, axis=-1)
    return (jax.nn.silu(gate) * up) @ w_down

def rope_tables(T, dim):
    inv = 1.0 / (ROPE_THETA ** (jnp.arange(0, dim, 2, dtype=jnp.float32) / dim))
    ang = jnp.arange(T, dtype=jnp.float32)[:, None] * inv[None, :]
    return jnp.cos(ang), jnp.sin(ang)

def rope(x, cos, sin):
    xf = x.astype(jnp.float32)
    x1, x2 = jnp.split(xf, 2, axis=-1)
    c = cos[None, :, None, :]
    s = sin[None, :, None, :]
    return jnp.concatenate([x1 * c - x2 * s, x1 * s + x2 * c], axis=-1).astype(x.dtype)

def causal_dwconv(u, w):
    T = u.shape[1]
    up = jnp.pad(u, ((0, 0), (CONV_K - 1, 0), (0, 0)))
    out = w[0] * up[:, 0:T]
    for j in range(1, CONV_K):
        out = out + w[j] * up[:, j:j + T]
    return out

def indexed_sparse_attention(q, k, v, qi, ki, wi, topk):
    f32 = jnp.float32
    B, T = q.shape[:2]
    nblk = -(-T // Q_BLOCK)
    pad = nblk * Q_BLOCK - T

    def blocks(a):
        a = jnp.pad(a, [(0, 0), (0, pad)] + [(0, 0)] * (a.ndim - 2))
        return jnp.moveaxis(a.reshape((B, nblk, Q_BLOCK) + a.shape[2:]), 1, 0)

    starts = jnp.arange(nblk, dtype=jnp.int32) * Q_BLOCK
    key_pos = jnp.arange(T, dtype=jnp.int32)
    kif = ki.astype(f32)
    gather = jax.vmap(lambda a, i: a[i])

    def one_block(args):
        qb, qib, wib, start = args
        q_pos = start + jnp.arange(Q_BLOCK, dtype=jnp.int32)
        causal = key_pos[None, :] <= q_pos[:, None]
        rel = jax.nn.relu(jnp.einsum('bqhd,bsd->bqhs', qib.astype(f32), kif) * IDX_HEAD_DIM ** -0.5)
        score = jnp.einsum('bqh,bqhs->bqs', wib.astype(f32) * IDX_HEADS ** -0.5, rel)
        score = jnp.where(causal[None], score, -jnp.inf)
        top_val, top_idx = lax.top_k(score, topk)
        valid = top_val > -jnp.inf
        k_sel = gather(k, top_idx)
        v_sel = gather(v, top_idx)
        qg = qb.reshape(B, Q_BLOCK, ATT_KV_HEADS, ATT_HEADS // ATT_KV_HEADS, ATT_HEAD_DIM)
        s = jnp.einsum('bqgrd,bqkgd->bqgrk', qg, k_sel).astype(f32) * ATT_HEAD_DIM ** -0.5
        s = jnp.where(valid[:, :, None, None, :], s, -jnp.inf)
        p = jax.nn.softmax(s, axis=-1).astype(v.dtype)
        o = jnp.einsum('bqgrk,bqkgd->bqgrd', p, v_sel)
        return o.reshape(B, Q_BLOCK, ATT_W)

    out = lax.map(one_block, (blocks(q), blocks(qi), blocks(wi), starts))
    return jnp.moveaxis(out, 0, 1).reshape(B, nblk * Q_BLOCK, ATT_W)[:, :T].astype(q.dtype)

def mlstm_chunkwise(q, k, v, i_pre, f_pre):
    f32 = jnp.float32
    B, T, H, Dh = q.shape
    L = MLSTM_CHUNK
    pad = (-N_META) % L

    def seq_chunks(a):
        a = jnp.pad(a.astype(f32), ((0, 0), (pad, 0), (0, 0), (0, 0)))
        return jnp.transpose(a.reshape(B, -1, L, H, Dh), (1, 0, 3, 2, 4))

    def gate_chunks(a, fill):
        a = jnp.pad(a, ((0, 0), (pad, 0), (0, 0)), constant_values=fill)
        return jnp.transpose(a.reshape(B, -1, L, H), (1, 0, 3, 2))

    qs = seq_chunks(q)
    ks = seq_chunks(k) * Dh ** -0.5
    vs = seq_chunks(v)
    logi = gate_chunks(i_pre.astype(f32), -jnp.inf)
    logf = gate_chunks(jax.nn.log_sigmoid(f_pre.astype(f32)), 0.0)
    tril = jnp.tril(jnp.ones((L, L), dtype=bool))

    def step(carry, xs):
        C, n, m = carry
        qc, kc, vc, ic, fc = xs
        b = jnp.cumsum(fc, axis=-1)
        bL = b[..., -1]
        Dm = jnp.where(tril, b[..., :, None] - b[..., None, :] + ic[..., None, :], -jnp.inf)
        a = b + m[..., None]
        mq = jnp.maximum(a, Dm.max(axis=-1))
        inter = jnp.exp(a - mq)
        wqk = jnp.exp(Dm - mq[..., None]) * jnp.einsum('bhld,bhsd->bhls', qc, kc)
        num = inter[..., None] * jnp.einsum('bhld,bhde->bhle', qc, C) + jnp.einsum('bhls,bhse->bhle', wqk, vc)
        den = inter * jnp.einsum('bhld,bhd->bhl', qc, n) + wqk.sum(axis=-1)
        hc = num / jnp.maximum(jnp.abs(den), jnp.exp(-mq))[..., None]
        g = bL[..., None] - b + ic
        m_new = jnp.maximum(bL + m, g.max(axis=-1))
        decay = jnp.exp(bL + m - m_new)
        wk = jnp.exp(g - m_new[..., None])[..., None] * kc
        C_new = decay[..., None, None] * C + jnp.einsum('bhld,bhle->bhde', wk, vc)
        n_new = decay[..., None] * n + wk.sum(axis=-2)
        return (C_new, n_new, m_new), hc

    init = (jnp.zeros((B, H, Dh, Dh), f32), jnp.zeros((B, H, Dh), f32), jnp.zeros((B, H), f32))
    _, hs = lax.scan(step, init, (qs, ks, vs, logi, logf))
    hs = jnp.transpose(hs, (1, 0, 3, 2, 4)).reshape(B, -1, H, Dh)[:, pad:]
    return hs.astype(q.dtype)

def hybrid_mixer(u, w_in, w_conv, b_igate, b_fgate, mh_g, w_branch, w_out, cos, sin, topk):
    B, T, _ = u.shape
    offs = [int(o) for o in np.cumsum(SPLIT_SIZES)[:-1]]
    (cx, cb, cc, q, k, v, qi, ki, wi, mq, mk, mv, mo, mi, mf, gt) = jnp.split(u @ w_in, offs, axis=-1)
    y_a = cb * causal_dwconv(cc * cx, w_conv)
    q = rope(q.reshape(B, T, ATT_HEADS, ATT_HEAD_DIM), cos, sin)
    k = rope(k.reshape(B, T, ATT_KV_HEADS, ATT_HEAD_DIM), cos, sin)
    v = v.reshape(B, T, ATT_KV_HEADS, ATT_HEAD_DIM)
    qi = rope(qi.reshape(B, T, IDX_HEADS, IDX_HEAD_DIM), cos, sin)
    ki = rope(ki[:, :, None, :], cos, sin)[:, :, 0, :]
    y_b = indexed_sparse_attention(q, k, v, qi, ki, wi, topk)
    hm = mlstm_chunkwise(mq.reshape(B, T, MLSTM_HEADS, MLSTM_HEAD_DIM),
                         mk.reshape(B, T, MLSTM_HEADS, MLSTM_HEAD_DIM),
                         mv.reshape(B, T, MLSTM_HEADS, MLSTM_HEAD_DIM),
                         mi + b_igate, mf + b_fgate)
    y_c = headwise_rmsnorm(hm, mh_g) * jax.nn.sigmoid(mo)
    gates = jax.nn.sigmoid(gt.reshape(B, T, N_BRANCH, D_MODEL))
    merged = (gates[:, :, 0] * (y_a @ w_branch[0])
              + gates[:, :, 1] * (y_b @ w_branch[1])
              + gates[:, :, 2] * (y_c @ w_branch[2]))
    return merged @ w_out

def setup_inputs(seed: int = 0) -> dict:
    key = jax.random.key(seed)
    ks = jax.random.split(key, 12)
    f32 = jnp.float32

    def nrm(k, shape, scale):
        return jax.random.normal(k, shape, f32) * scale

    x = nrm(ks[0], (BATCH, SEQ, D_MODEL), 1.0)
    meta = nrm(ks[1], (N_META, D_MODEL), 1.0)
    norm_g = 1.0 + nrm(ks[2], (DEPTH, 6, D_MODEL), 0.02)
    w_ffn_gu = nrm(ks[3], (DEPTH, 2, D_MODEL, 2 * D_FF), D_MODEL ** -0.5)
    w_ffn_down = nrm(ks[4], (DEPTH, 2, D_FF, D_MODEL), D_FF ** -0.5)
    w_in = nrm(ks[5], (DEPTH, D_MODEL, IN_W), D_MODEL ** -0.5)
    w_conv = nrm(ks[6], (DEPTH, CONV_K, CONV_W), CONV_K ** -0.5)
    b_igate = nrm(ks[7], (DEPTH, MLSTM_HEADS), 0.1)
    b_fgate = jnp.linspace(3.0, 6.0, MLSTM_HEADS, dtype=f32)[None, :] + nrm(ks[8], (DEPTH, MLSTM_HEADS), 0.1)
    mh_norm_g = 1.0 + nrm(ks[9], (DEPTH, MLSTM_W), 0.02)
    w_branch = nrm(ks[10], (DEPTH, N_BRANCH, BRANCH_W, D_MODEL), BRANCH_W ** -0.5)
    w_out = nrm(ks[11], (DEPTH, D_MODEL, D_MODEL), D_MODEL ** -0.5)
    return {'x': x, 'meta': meta, 'norm_g': norm_g, 'w_ffn_gu': w_ffn_gu, 'w_ffn_down': w_ffn_down,
            'w_in': w_in, 'w_conv': w_conv, 'b_igate': b_igate, 'b_fgate': b_fgate,
            'mh_norm_g': mh_norm_g, 'w_branch': w_branch, 'w_out': w_out}

def reference(x, meta, norm_g, w_ffn_gu, w_ffn_down, w_in, w_conv, b_igate, b_fgate, mh_norm_g, w_branch, w_out):
    B, S, _ = x.shape
    h = jnp.concatenate([jnp.broadcast_to(meta.astype(x.dtype)[None], (B, N_META, D_MODEL)), x], axis=1)
    T = h.shape[1]
    cos, sin = rope_tables(T, ATT_HEAD_DIM)
    topk = min(IDX_TOPK_MAX, S // 4)
    for l in range(DEPTH):
        g = norm_g[l]
        h = h + 0.5 * rmsnorm(swiglu(rmsnorm(h, g[0]), w_ffn_gu[l, 0], w_ffn_down[l, 0]), g[1])
        y = hybrid_mixer(rmsnorm(h, g[2]), w_in[l], w_conv[l], b_igate[l], b_fgate[l], mh_norm_g[l],
                         w_branch[l], w_out[l], cos, sin, topk)
        h = h + rmsnorm(y, g[3])
        h = h + 0.5 * rmsnorm(swiglu(rmsnorm(h, g[4]), w_ffn_gu[l, 1], w_ffn_down[l, 1]), g[5])
    return h[:, N_META:]


_drawn_inputs = setup_inputs


def setup_inputs(seed=0):
    import zlib

    import numpy as np

    out = dict(_drawn_inputs(seed))
    spreads = {}
    factors = {'b_igate': 64.0, 'mh_norm_g': 4.609}
    for name, (base, spread) in spreads.items():
        noise = np.random.default_rng([zlib.crc32(name.encode()), seed]).standard_normal(out[name].shape)
        drawn = base * np.exp(spread * noise) if base else spread * noise
        out[name] = __import__('jax').numpy.asarray(drawn.astype(out[name].dtype))
    for name, factor in factors.items():
        out[name] = (out[name] * factor).astype(out[name].dtype)
    return out
```

```python
from contextlib import ExitStack

import concourse.bass as bass
from concourse import mybir

F32 = mybir.dt.float32
F32R = mybir.dt.float32r
ALU = mybir.AluOpType
ACT = mybir.ActivationFunctionType
AX = mybir.AxisListType

P = 128
HALF = 2
EPS = 1e-6
NEG = -1e30
TAKEN = -3e38
LN_EXP_SET = "natural_log_exp_and_others"
TANH_SET = "exp_and_others"


def trunk_program(nc, x, meta, norm_g, w_ffn_gu, w_ffn_down, w_in, w_conv, b_igate, b_fgate,
                  mh_norm_g, w_branch, w_out, rope_tab, mats, sel, out):
    DEPTH, _, D, F2 = w_ffn_gu.shape
    SEQ, META = x.shape[1], meta.shape[0]
    T = SEQ + META
    TH = T // HALF
    FF = F2 // 2
    KD = D // P
    KF = FF // P
    BW = w_branch.shape[2]
    KB = BW // P
    DH = 64
    NH = BW // DH
    NKV, NIDX = 2, 4
    NM = BW // P
    TOPK = min(256, SEQ // 4)
    NB = 5
    QB = (T - P) // (NB - 1)
    BL = [(0, P)] + [(P + i * QB, QB) for i in range(NB - 1)]
    KL = [t0 + n for t0, n in BL]
    MO = [sum(KL[:b]) for b in range(NB)]
    assert T == P + (NB - 1) * QB and TOPK == P and D == 2 * BW and KB == 4 and NM == 4
    C_CX, C_CB, C_CC = 0, BW, 2 * BW
    C_Q = 3 * BW
    C_K = C_Q + BW
    C_V = C_K + NKV * DH
    C_QI = C_V + NKV * DH
    C_KI = C_QI + NIDX * DH
    C_MQ = C_KI + DH + NIDX
    C_MK, C_MV, C_MO = C_MQ + BW, C_MQ + 2 * BW, C_MQ + 3 * BW
    C_MI = C_MQ + 4 * BW
    C_MF = C_MI + NM
    C_GT = C_MF + NM

    UP_UNITS = KF
    DOWN_K = [KD, KD, KF - 2 * KD]
    DOWN_UNITS = 3 * KD // 2
    FFN_UNITS = UP_UNITS + DOWN_UNITS
    MIX = [("qi", C_QI, C_QI + P), ("k", C_K, C_KI), ("q", C_Q, C_Q + P), ("q", C_Q + 2 * P, C_Q + 3 * P),
           ("v", C_V, C_V + P), ("if", C_MI, C_MF)]
    for kind, c in (("mq", C_MQ), ("mk", C_MK), ("mo", C_MO), ("mv", C_MV)):
        MIX += [(kind, c + 2 * j * P, c + (2 * j + 1) * P) for j in range(2)]
    for j in range(0, KB, 2):
        MIX += [("cxc", C_CX + j * P, C_CC + j * P), ("cxc", C_CX + (j + 1) * P, C_CC + (j + 1) * P),
                ("cb", C_CB + j * P, C_CB + (j + 1) * P)]
    N_MIX = len(MIX)
    FIRST_CONV = N_MIX - 6
    MERGE_UNITS = 3 * KD
    OUT_UNITS = KD // 2
    U_MIX = FFN_UNITS
    U_MERGE = U_MIX + N_MIX
    U_OUT = U_MERGE + MERGE_UNITS
    U_FFN = [0, U_OUT + OUT_UNITS]
    UNITS = U_FFN[1] + FFN_UNITS
    ACCS = {"v": 3, "mv": 3}
    N_MIXACC = [ACCS.get(kind, 2) for kind, _, _ in MIX]
    A_MIX = 2 * UP_UNITS + KD
    A_UNIT = [A_MIX + sum(N_MIXACC[:i]) for i in range(N_MIX)]
    A_MERGE = A_MIX + sum(N_MIXACC)
    A_OUT = A_MERGE + 6 * KD
    A_FFN = [0, A_OUT + KD]
    UNITS_AFTER = {1: (5, 6), 2: (7, 8), 3: (9, 10), 4: (11, 12, 13)}
    AUX = {}

    def aux_item(*key):
        AUX[key] = len(AUX)

    for q in range(3):
        aux_item("norm", q)
    for r in range(2 + KB):
        aux_item("rot", r)
    for r in range(3):
        aux_item("dup", r)
        aux_item("dup_rot", r)
    aux_item("wi")
    for b in range(1, NB):
        for i in range(NIDX):
            aux_item("index", b, i)
    NA = NB * NH
    O_LAG = 4
    for t in range(NA + O_LAG):
        if t < NA:
            aux_item("score", t)
        if t >= NH - 1 + O_LAG and (t - O_LAG) % NH == NH - 1:
            aux_item("turn", (t - O_LAG) // NH)
    aux_item("gate_cols")
    for m in range(NM):
        aux_item("stab", m)
        for c in range(NB):
            aux_item("qk", m, c)
    for m in range(NM):
        aux_item("hturn", m)
    for q in range(3, 6):
        aux_item("norm", q)

    ctx = ExitStack()
    with ctx:
        def sem(name):
            return ctx.enter_context(nc.semaphore(name))

        CH = 4 * T
        arena_bytes = 212800
        arena = ctx.enter_context(nc.sbuf_tensor("arena", [P, arena_bytes // 4], F32))
        del arena
        base = nc.sbuf_base - arena_bytes
        place = [0]

        def at(name, shape, dt, offset):
            return nc.alloc_sbuf_tensor_at(name, shape, dt, offset=base + offset)

        def sb(name, shape, dt=F32):
            size = 4
            for s in shape[1:]:
                size *= s
            t = at(name, shape, dt, place[0])
            place[0] += (size + 31) // 32 * 32
            assert place[0] <= arena_bytes, (name, place[0])
            return t

        h = sb("h", [P, KD, T])
        y = at("y", [P, KD, T], F32, place[0])
        x_hi = sb("x_hi", [P, KD, T], F32R)
        x_lo = sb("x_lo", [P, KD, T], F32R)
        w_raw = sb("w_raw", [P, 2, 2, KD, P])
        w_hi = sb("w_hi", [P, 2, 2, KD, P], F32R)
        w_lo = sb("w_lo", [P, 2, 2, KD, P], F32R)
        tmp = sb("tmp", [P, 6, T])
        region = place[0]
        place[0] += 46 * CH

        def at_chunk(name, shape, dt, chunk, extra=0):
            return at(name, shape, dt, region + chunk * CH + extra)

        a_hi = at_chunk("a_hi", [P, KF, T], F32R, 0)
        a_lo = at_chunk("a_lo", [P, KF, T], F32R, KF)
        q_t = at_chunk("q_t", [P, KB, T], F32, 0)
        qi_t = at_chunk("qi_t", [P, 2, T], F32, 4)
        ki_t = at_chunk("ki_t", [P, T], F32, 6)
        k_t = at_chunk("k_t", [P, NKV, T], F32, 7)
        cos_sin = at_chunk("cos_sin", [P, 2, T], F32, 9)
        mask = at_chunk("mask", [P, sum(KL)], F32, 11)
        rope_mats = at_chunk("rope_mats", [P, 5, P], F32, 15)
        prob = at_chunk("prob", [P, 2, T], F32, 15)
        prob_t = at_chunk("prob_t", [P, 2, 512], F32, 17)
        v_tok = at_chunk("v_tok", [P, NB, P], F32, 19)
        mq_t = at_chunk("mq_t", [P, NM, T], F32, 21)
        mk_t = at_chunk("mk_t", [P, NM, T], F32, 25)
        mo_t = at_chunk("mo_t", [P, NM, T], F32, 29)
        mv_tok = at_chunk("mv_tok", [P, NB, NM, P + 1], F32, 33)
        yb_hi = at_chunk("yb_hi", [P, KB, T], F32R, 38)
        yb_lo = at_chunk("yb_lo", [P, KB, T], F32R, 42)
        m_wt = at_chunk("m_wt", [P, NB, T], F32, 0)
        m_h = at_chunk("m_h", [P, NB, NM, P], F32, 5)
        sel_sb = at_chunk("sel_sb", [NM, NM, P], F32, 19)
        yc_hi = at_chunk("yc_hi", [P, KB, T], F32R, 11)
        yc_lo = at_chunk("yc_lo", [P, KB, T], F32R, 15)
        ya_hi = at_chunk("ya_hi", [P, KB, T], F32R, 21)
        ya_lo = at_chunk("ya_lo", [P, KB, T], F32R, 25)
        conv_u = at_chunk("conv_u", [P, 2, T + 4], F32, 29)
        mg_hi = at_chunk("mg_hi", [P, KD, T], F32R, 0)
        mg_lo = at_chunk("mg_lo", [P, KD, T], F32R, 29)
        ident = sb("ident", [P, P])
        ones = sb("ones", [P, P])
        causal_bias = sb("causal_bias", [P, P])
        causal_keep = sb("causal_keep", [P, P])
        params = sb("params", [P, P])
        cur = sb("cur", [P, 64])
        gate_bias = sb("gate_bias", [NM, 2, DEPTH])
        gate_bias_cur = sb("gate_bias_cur", [NM, 2])

        def small(first_chunk, offset, tiles):
            made = []
            for name, shape in tiles:
                made.append(at(name, [P, *shape], F32, region + first_chunk * CH + offset))
                size = 4
                for d in shape:
                    size *= d
                offset += (size + 31) // 32 * 32
            return made

        wi_tok, top8, row_max, neg_max, row_sum, row_inv = small(11, 4 * sum(KL), (
            ("wi_tok", (NB, NIDX)), ("top8", (8,)), ("row_max", (2,)), ("neg_max", (2,)), ("row_sum", (2, NH)),
            ("row_inv", (NH,))))
        c_tok, floor_tok, den, m_ss, m_var, m_r = small(10, 0, (
            ("c_tok", (NB, NM)), ("floor_tok", (NB, NM)), ("den", (2,)), ("m_ss", (NB * NM,)),
            ("m_var", (NB * NM,)), ("m_r", (NB * NM,))))
        yb, ya, yc = (yb_hi, yb_lo), (ya_hi, ya_lo), (yc_hi, yc_lo)
        ROT, DUP0, DUP1, DROT0, DROT1 = range(5)
        G_NORM, G_CONV, G_HEAD = 0, 6 * KD, 6 * KD + 3 * KB

        acc = ctx.enter_context(nc.psum_tensor("acc", [P, 4, 512], F32))
        aux = ctx.enter_context(nc.psum_tensor("aux", [P, 2, 1024], F32))

        def acc_halves(slot):
            return acc[:, 2 * slot:2 * slot + 2, 0:TH]

        def halves(t):
            return t.rearrange("p (a t) -> p a t", a=HALF)

        def aux_halves(slot):
            return aux[:, slot, :].rearrange("p (a t) -> p a t", a=HALF)[:, :, 0:TH]

        const_landed = sem("const_landed")
        arrived = sem("arrived")
        layer_go = sem("layer_go")
        loads_resumed = sem("loads_resumed")
        io_in = sem("io_in")
        io_turned = sem("io_turned")
        io_placed = sem("io_placed")
        io_first = sem("io_first")
        out_stored = [sem("out_stored0"), sem("out_stored1")]
        raw_landed = [sem("raw_landed0"), sem("raw_landed1")]
        whi_ready = sem("whi_ready")
        wlo_ready = sem("wlo_ready")
        acc_done = sem("acc_done")
        part_done = sem("part_done")
        acc_free = [sem("acc_free0"), sem("acc_free1")]
        aux_done = sem("aux_done")
        aux_free = [sem("aux_free0"), sem("aux_free1")]
        cur_ready = sem("cur_ready")
        h_ready = sem("h_ready")
        sq_ready = sem("sq_ready")
        sq_added = sem("sq_added")
        log_ready = sem("log_ready")
        seed_ready = sem("seed_ready")
        newton = sem("newton")
        rstd_ready = sem("rstd_ready")
        xf_ready = sem("xf_ready")
        xhi_ready = sem("xhi_ready")
        xlo_ready = sem("xlo_ready")
        silu_ready = sem("silu_ready")
        act_ready = sem("act_ready")
        ahi_ready = sem("ahi_ready")
        alo_ready = sem("alo_ready")
        ysum = sem("ysum")
        ysq_ready = sem("ysq_ready")
        res_ready = sem("res_ready")
        rope_landed = sem("rope_landed")
        rope_step = sem("rope_step")
        rope_done = sem("rope_done")
        wi_ready = sem("wi_ready")
        rel_ready = sem("rel_ready")
        index_step = sem("index_step")
        mask_ready = sem("mask_ready")
        topk_step = sem("topk_step")
        negmax_ready = sem("negmax_ready")
        p_ready = sem("p_ready")
        p_turned = sem("p_turned")
        pt_copied = sem("pt_copied")
        pv_done = sem("pv_done")
        inv_ready = sem("inv_ready")
        o_read = sem("o_read")
        ybhi_ready = sem("ybhi_ready")
        gate_step = sem("gate_step")
        gate_rows = sem("gate_rows")
        gates_ready = sem("gates_ready")
        sel_landed = sem("sel_landed")
        cols_ready = sem("cols_ready")
        stab_ready = sem("stab_ready")
        arg_ready = sem("arg_ready")
        decay_ready = sem("decay_ready")
        wt_step = sem("wt_step")
        wt_ready = sem("wt_ready")
        num_done = sem("num_done")
        den_abs = sem("den_abs")
        den_step = sem("den_step")
        num_read = sem("num_read")
        mh_squared = sem("mh_squared")
        mh_step = sem("mh_step")
        mh_act = sem("mh_act")
        mh_normed = sem("mh_normed")
        conv_step = sem("conv_step")
        brhi_ready = sem("brhi_ready")
        brlo_ready = sem("brlo_ready")
        merge_step = sem("merge_step")
        mf_ready = sem("mf_ready")
        mhi_ready = sem("mhi_ready")
        mlo_ready = sem("mlo_ready")
        PER_LAYER = [*raw_landed, whi_ready, wlo_ready, acc_done, part_done, *acc_free, aux_done, *aux_free,
                     cur_ready, h_ready, sq_ready, sq_added, silu_ready, act_ready, io_turned, io_placed, log_ready, seed_ready, newton,
                     rstd_ready, xf_ready, xhi_ready, xlo_ready, ahi_ready, alo_ready, ysum,
                     ysq_ready, res_ready, rope_landed, rope_step, rope_done, wi_ready, rel_ready,
                     index_step, mask_ready, topk_step, negmax_ready, p_ready, p_turned, pt_copied,
                     pv_done, inv_ready, o_read, ybhi_ready, gate_step, gate_rows, gates_ready, sel_landed,
                     cols_ready, stab_ready, arg_ready, decay_ready, wt_step, wt_ready, num_done, den_abs,
                     den_step, num_read, mh_squared, mh_step, mh_act, mh_normed, conv_step,
                     brhi_ready, brlo_ready, merge_step, mf_ready, mhi_ready, mlo_ready]
        ENGINES = 5

        class Steps:

            def __init__(self, eng, semaphore):
                self.eng, self.sem, self.n = eng, semaphore, 0

            def did(self, ins):
                ins.then_inc(self.sem, 1)
                self.n += 1

            def settle(self):
                self.eng.wait_ge(self.sem, self.n)

        def end_of_layer(eng, layer):
            eng.drain().then_inc(arrived, 1)
            eng.wait_ge(layer_go, layer + 1)

        def take_acc(eng, n):
            eng.wait_ge(acc_done, 1 + n + 1)

        def take_aux(eng, key):
            eng.wait_ge(aux_done, AUX[key] + 1)

        def aux_of(key):
            return AUX[key] % 2

        def free_aux(eng, key):
            eng.wait_ge(aux_free[aux_of(key)], AUX[key] // 2 + 2)

        gu_v = w_ffn_gu.rearrange("l f (k p) c -> l f p k c", p=P)
        down_v = w_ffn_down.rearrange("l f (k p) c -> l f p k c", p=P)
        in_v = w_in.rearrange("l (k p) c -> l p k c", p=P)
        branch_v = w_branch.rearrange("l b (k p) c -> l p (b k) c", p=P)
        out_v = w_out.rearrange("l (k p) c -> l p k c", p=P)

        block = ctx.enter_context(nc.Block())

        @block.sync
        def _(sp):
            for dst, src in ((ident, mats[0]), (ones, mats[1]), (causal_bias, mats[2]), (causal_keep, mats[3])):
                sp.dma_start(dst[:, :], src).then_inc(const_landed, 16)
            rows = 0
            for src in (norm_g.rearrange("l s (c p) -> (l s c) p", p=P),
                        w_conv.rearrange("l j (c p) -> (l j c) p", p=P),
                        mh_norm_g.rearrange("l (c p) -> (l c) p", p=P)):
                n = src.shape[0]
                sp.dma_start(tmp[rows:rows + n, 5, 0:P], src).then_inc(const_landed, 16)
                rows += n
            assert rows == P
            sp.dma_start(gate_bias[:, 0, :], b_igate.rearrange("l m -> m l"),
                         allow_slow_non_contiguous=True).then_inc(const_landed, 16)
            sp.dma_start(gate_bias[:, 1, :], b_fgate.rearrange("l m -> m l"),
                         allow_slow_non_contiguous=True).then_inc(const_landed, 16)
            rows_v = w_raw[:, :, :, :, :].rearrange("p s c k j -> p s (c k j)")
            sp.dma_start(tmp[0:META, 0:2, 0:512], meta.rearrange("t (a f) -> t a f", a=2)).then_inc(io_in, 16)
            for i in range(SEQ // P):
                if i >= 2:
                    sp.wait_ge(io_turned, 2 * (i - 1) + 2)
                sp.dma_start(rows_v[:, i % 2, 0:D], x[0, i * P:(i + 1) * P, :]).then_inc(raw_landed[i % 2], 16)
            sp.drain().then_inc(arrived, 1)
            sp.wait_ge(layer_go, 1)

            def load(u, parts, slot):
                sp.wait_ge(wlo_ready, u + 1)
                for dst, src in parts:
                    sp.dma_start(dst, src).then_inc(raw_landed[slot], 16)

            def chunk_pair(slot, srcs, kn):
                return [(w_raw[:, slot, c, 0:kn, :], s) for c, s in enumerate(srcs)]

            def load_ffn(f, layer):
                with sp.Fori(0, UP_UNITS // 2) as i:
                    for s in range(2):
                        col = sp.snap((2 * i + s) * P)
                        col2 = sp.snap((2 * i + s) * P + FF)
                        load(U_FFN[f] + 2 * i + s,
                             chunk_pair(s, [gu_v[layer, f, :, :, bass.ds(col, P)],
                                            gu_v[layer, f, :, :, bass.ds(col2, P)]], KD), s)
                with sp.Fori(0, KD // 4) as i:
                    for q in range(6):
                        kg = q % 3
                        rows = slice(kg * KD, kg * KD + DOWN_K[kg])
                        cols = [sp.snap((4 * i + 2 * (q // 3) + c) * P) for c in range(2)]
                        load(U_FFN[f] + UP_UNITS + 6 * i + q,
                             chunk_pair(q % 2, [down_v[layer, f, :, rows, bass.ds(c, P)] for c in cols],
                                        DOWN_K[kg]), q % 2)

            with sp.Fori(0, DEPTH) as layer:
                load_ffn(0, layer)
                for j, (kind, c0, c1) in enumerate(MIX):
                    u = U_MIX + j
                    load(u, chunk_pair(u % 2, [in_v[layer, :, :, c0:c0 + P], in_v[layer, :, :, c1:c1 + P]], KD), u % 2)
                    if j == 1:
                        sp.wait_ge(acc_done, 1 + A_MIX)
                        sp.dma_start(cos_sin[:, :, :], rope_tab.rearrange("a p t -> p a t")).then_inc(rope_landed, 16)
                        sp.dma_start(rope_mats[:, :, :], mats[4:9].rearrange("m p c -> p m c")).then_inc(rope_landed, 16)
                with sp.Fori(0, KD // 2) as i:
                    for s in range(2):
                        u = U_MERGE + 3 * s
                        cols = [sp.snap(C_GT + (2 * i + s) * P + b * D) for b in range(3)]
                        m = sp.snap((2 * i + s) * P)
                        load(u + 6 * i, chunk_pair(u % 2, [in_v[layer, :, :, bass.ds(c, P)] for c in cols[:2]], KD), u % 2)
                        load(u + 1 + 6 * i, chunk_pair((u + 1) % 2, [in_v[layer, :, :, bass.ds(cols[2], P)],
                                                                     branch_v[layer, :, 0:KD, bass.ds(m, P)]], KD), (u + 1) % 2)
                        load(u + 2 + 6 * i, [(w_raw[:, u % 2, 0, 2 * a:2 * a + 2, :],
                                              branch_v[layer, :, KD + 2 * a:KD + 2 * a + 2, bass.ds(m, P)]) for a in range(2)], u % 2)
                for j in range(OUT_UNITS):
                    u = U_OUT + j
                    load(u, chunk_pair(u % 2, [out_v[layer, :, :, (2 * j + c) * P:(2 * j + c + 1) * P] for c in range(2)], KD), u % 2)
                load_ffn(1, layer)
                end_of_layer(sp, layer + 1)
                sp.sem_inc(loads_resumed, 1)

            for i in range(SEQ // P):
                sp.wait_ge(io_placed, 2 * (i + 1))
                sp.dma_start(out[0, i * P:(i + 1) * P, :], rows_v[:, i % 2, 0:D]).then_inc(out_stored[i % 2], 16)
            for s in out_stored:
                sp.wait_ge(s, 16 * (SEQ // P // 2))

        def split_part(t, slot, kind):
            if kind == "full":
                return t[:, slot, :, :, :]
            if kind == "last_k":
                return t[:, slot, :, 0:DOWN_K[2], :]
            return t[:, slot, 0, 0:KB, :]

        @block.gpsimd
        def _(pool):
            def clear_counts():
                pool.wait_ge(arrived, ENGINES - 1)
                pool.drain()
                for s in PER_LAYER:
                    pool.sem_clear(s)
                pool.sem_clear(arrived)
                for s in (*acc_free, *aux_free, acc_done, alo_ready, mlo_ready):
                    pool.sem_inc(s, 1)
                pool.sem_inc(wlo_ready, 2)
                pool.sem_inc(layer_go, 1)

            def w_rest(u, slot, kind="full"):
                pool.wait_ge(whi_ready, u + 1)
                nc.gpsimd.tensor_tensor(split_part(w_lo, slot, kind), split_part(w_raw, slot, kind),
                                        split_part(w_hi, slot, kind).bitcast(F32), ALU.subtract).then_inc(wlo_ready, 1)

            def add_results(p):
                for k in range(KD):
                    pool.wait_ge(res_ready, KD * p + k + 1)
                    nc.gpsimd.tensor_tensor(h[:, k, :], h[:, k, :], tmp[:, 2 + k % 2, :], ALU.add).then_inc(h_ready, 1)

            def br_rest(g, dst):
                pool.wait_ge(brhi_ready, g + 1)
                nc.gpsimd.tensor_tensor(dst[1][:, g % KB, :], tmp[:, 4 + g % 2, :], dst[0][:, g % KB, :].bitcast(F32),
                                        ALU.subtract).then_inc(brlo_ready, 1)

            def ffn(f):
                u0 = U_FFN[f]
                with pool.Fori(0, UP_UNITS // 2) as i:
                    for s in range(2):
                        w_rest(u0 + 2 * i + s + 1, (s + 1) % 2)
                        n = f * KF + 2 * i + s
                        pool.wait_ge(ahi_ready, n + 1)
                        nc.gpsimd.tensor_tensor(a_lo[:, bass.ds(2 * i + s, 1), :], tmp[:, 2 + s:3 + s, :],
                                                a_hi[:, bass.ds(2 * i + s, 1), :].bitcast(F32), ALU.subtract)\
                            .then_inc(alo_ready, 1)
                last = f == 1
                for q in range(DOWN_UNITS - last):
                    w_rest(u0 + UP_UNITS + q + 1, (q + 1) % 2, "last_k" if q % 3 == 1 else "full")

            clear_counts()
            with pool.Fori(0, DEPTH) as layer:
                w_rest(0, 0)
                ffn(0)
                add_results(0)
                for j in range(FIRST_CONV):
                    w_rest(U_MIX + j + 1, (U_MIX + j + 1) % 2)
                for m in range(KB):
                    br_rest(m, yc)
                for j in range(FIRST_CONV, N_MIX):
                    w_rest(U_MIX + j + 1, (U_MIX + j + 1) % 2)
                    if MIX[j][0] == "cb":
                        for c in range(2):
                            br_rest(KB + 2 * ((j - FIRST_CONV) // 3) + c, ya)
                with pool.Fori(0, KD // 2) as i:
                    for s in range(2):
                        for r in range(3):
                            u = U_MERGE + 3 * s + r
                            w_rest(u + 1 + 6 * i, (u + 1) % 2, "branch2" if r == 1 else "full")
                        m = bass.ds(2 * i + s, 1)
                        pool.wait_ge(mhi_ready, 2 * i + s + 1)
                        nc.gpsimd.tensor_tensor(mg_lo[:, m, :], tmp[:, 3 * s:3 * s + 1, :],
                                                mg_hi[:, m, :].bitcast(F32), ALU.subtract).then_inc(mlo_ready, 1)
                for j in range(OUT_UNITS):
                    w_rest(U_OUT + j + 1, (U_OUT + j + 1) % 2)
                add_results(1)
                ffn(1)
                add_results(2)
                clear_counts()

        @block.scalar
        def _(act):
            A = nc.scalar.activation

            def w_round(u, slot, kind="full"):
                act.wait_ge(raw_landed[slot], 32 * (u // 2 + 1) if isinstance(u, int) else u)
                return A(split_part(w_hi, slot, kind), split_part(w_raw, slot, kind), ACT.Copy).then_inc(whi_ready, 1)

            def w_round_loop(u0, i, per, slot, kind="full"):
                act.wait_ge(raw_landed[slot], 32 * (u0 // 2 + 1) + 16 * per * i)
                A(split_part(w_hi, slot, kind), split_part(w_raw, slot, kind), ACT.Copy).then_inc(whi_ready, 1)

            def gain_of(p, k):
                return cur[:, G_NORM + 2 * p * KD + k:G_NORM + 2 * p * KD + k + 1]

            def square_h(p, with_x):
                if with_x:
                    act.wait_ge(cur_ready, 8)
                for k in range(KD):
                    if p > 0:
                        act.wait_ge(h_ready, KD * (p - 1) + k + 1)
                    if with_x:
                        A(x_hi[:, k, :], h[:, k, :], ACT.Copy, scale=gain_of(p, k)).then_inc(xhi_ready, 1)
                    if k >= 3:
                        act.wait_ge(sq_added, (KD - 1) * p + k - 2)
                    A(tmp[:, k % 2 if k else 4, :], h[:, k, :], ACT.Square).then_inc(sq_ready, 1)

            def rstd_seed(q):
                free_aux(act, ("norm", q))
                A(tmp[:, 3, :], tmp[:, 2, :], ACT.Ln).then_inc(log_ready, 1)
                act.wait_ge(log_ready, q + 1)
                A(tmp[:, 3, :], tmp[:, 3, :], ACT.Exp, scale=-0.5).then_inc(seed_ready, 1)

            def round_x(p):
                for k in range(KD):
                    act.wait_ge(xf_ready, k + 1)
                    A(x_hi[:, k, :], tmp[:, k % 2, :], ACT.Copy).then_inc(xhi_ready, 1)

            def ffn(f):
                u0, n0 = U_FFN[f], A_FFN[f]
                nc.scalar.preload_act_table(ACT.Silu)
                with act.Fori(0, UP_UNITS // 2) as i:
                    for s in range(2):
                        nn = n0 + 2 * s
                        act.wait_ge(acc_done, 1 + nn + 4 * i)
                        w_round_loop(u0 + s + 1, i, 2, (s + 1) % 2)
                        act.wait_ge(acc_free[nn % 2], nn // 2 + 2 * i + 2)
                        A(tmp[:, s, :], tmp[:, s, :], ACT.Silu).then_inc(silu_ready, 1)
                        act.wait_ge(act_ready, f * KF + 2 * i + s + 1)
                        A(a_hi[:, bass.ds(2 * i + s, 1), :], tmp[:, 2 + s:3 + s, :], ACT.Copy).then_inc(ahi_ready, 1)
                n1 = n0 + 2 * UP_UNITS

                def down_unit(i, q, skip=False):
                    if q == 0:
                        act.wait_ge(acc_done, 1 + n1 + 4 * i)
                    elif q == 3:
                        act.wait_ge(acc_done, 1 + n1 + 2 + 4 * i)
                    else:
                        act.wait_ge(part_done, f * KD + 4 * i + {1: 1, 2: 2, 4: 3, 5: 4}[q])
                    if not skip:
                        w_round_loop(u0 + UP_UNITS + q + 1, i, 6, (q + 1) % 2, "last_k" if q % 3 == 1 else "full")
                    if q % 3 == 2:
                        for c in range(2):
                            j = 2 * (q // 3) + c
                            slot = (n1 + j) % 2
                            act.wait_ge(acc_done, 1 + n1 + j + 4 * i + 1)
                            A(y[:, bass.ds(4 * i + j, 1), :].rearrange("p o (a t) -> p (o a) t", a=HALF),
                              acc_halves(slot), ACT.Copy).then_inc(acc_free[slot], 1)

                for i in range(KD // 4):
                    for q in range(6):
                        down_unit(i, q, skip=(f == 1 and i == KD // 4 - 1 and q == 5))
                nc.scalar.preload_act_table_set(LN_EXP_SET)
                rstd_seed(1 + 4 * f)

            def evac(n, dst, func=ACT.Copy, **kw):
                act.wait_ge(acc_done, 1 + n + 1)
                A(halves(dst), acc_halves(n % 2), func, **kw).then_inc(acc_free[n % 2], 1)

            def evac_tokens(n, pair, dst):
                act.wait_ge(acc_done, 1 + n + 1)
                for a, b in enumerate(pair):
                    rows = BL[b][1]
                    src, d = dst(b, acc[0:rows, 2 * (n % 2) + a, :])
                    ins = A(d, src, ACT.Copy)
                ins.then_inc(acc_free[n % 2], 1)

            def mixer_unit(j):
                kind, c0, _ = MIX[j]
                n = A_UNIT[j]
                act.wait_ge(acc_done, 1 + n)
                w_round(U_MIX + j + 1, (U_MIX + j + 1) % 2)
                if kind == "qi":
                    for c in range(2):
                        evac(n + c, qi_t[:, c, :])
                elif kind == "k":
                    evac(n, tmp[:, 4, :])
                    evac(n + 1, tmp[:, 5, :])
                elif kind == "q":
                    for c in range(2):
                        evac(n + c, q_t[:, (c0 - C_Q) // P + c, :])
                elif kind in ("v", "mv"):
                    for a, pair in enumerate(((0, 1), (2, 3), (4,))):
                        if kind == "v":
                            evac_tokens(n + a, pair, lambda b, s: (s[:, 0:P], v_tok[0:BL[b][1], b, :]))
                        else:
                            m0 = (c0 - C_MV) // P
                            evac_tokens(n + a, pair, lambda b, s: (
                                s[:, 0:2 * P].rearrange("p (m c) -> p m c", m=2),
                                mv_tok[0:BL[b][1], b, m0:m0 + 2, 0:P]))
                elif kind == "if":
                    for c in range(2):
                        act.wait_ge(acc_done, 1 + n + c + 1)
                        slot = (n + c) % 2
                        A(tmp[0:NM, 4 + c, :].rearrange("p (a t) -> p a t", a=HALF),
                          acc[0:NM, 2 * slot:2 * slot + 2, 0:TH], ACT.Identity,
                          bias=gate_bias_cur[:, c:c + 1]).then_inc(acc_free[slot], 1)
                elif kind == "mq":
                    for c in range(2):
                        evac(n + c, mq_t[:, (c0 - C_MQ) // P + c, :])
                elif kind == "mk":
                    for c in range(2):
                        evac(n + c, mk_t[:, (c0 - C_MK) // P + c, :], scale=float(P) ** -0.5)
                elif kind == "mo":
                    for c in range(2):
                        evac(n + c, mo_t[:, (c0 - C_MO) // P + c, :], ACT.Tanh, scale=0.5)

            def index_rel(b, i):
                g = NIDX * (b - 1) + i
                n = BL[b][1]
                key = ("index", b, i)
                act.wait_ge(aux_done, AUX[key] + 1)
                if g >= 2:
                    act.wait_ge(index_step, g - 1)
                A(tmp[0:n, g % 2, 0:KL[b]], aux[0:n, aux_of(key), 0:KL[b]], ACT.Relu, scale=float(DH) ** -0.5)\
                    .then_inc(aux_free[aux_of(key)], 1)

            def attention():
                for t in range(NA + O_LAG):
                    if t < NA:
                        b, hd = divmod(t, NH)
                        n = BL[b][1]
                        act.wait_ge(negmax_ready, t + 1)
                        A(prob[0:n, t % 2, 0:KL[b]], prob[0:n, t % 2, 0:KL[b]], ACT.Exp, bias=neg_max[0:n, t % 2:t % 2 + 1],
                          accum_out=row_sum[0:n, b % 2, hd:hd + 1]).then_inc(p_ready, 1)
                    if 1 <= t <= NA:
                        s = t - 1
                        b = s // NH
                        n = BL[b][1]
                        act.wait_ge(p_turned, s + 1)
                        if s >= 2:
                            act.wait_ge(pv_done, s - 1)
                        ins = A(prob_t[:, s % 2, 0:n], acc[:, s % 2, 0:n], ACT.Copy)
                        if b:
                            ins = A(prob_t[0:QB, s % 2, n:n * (b + 1)], acc[0:QB, s % 2, n:n * (b + 1)], ACT.Copy)
                        ins.then_inc(pt_copied, 1)
                    if t >= NH - 1 + O_LAG and (t - O_LAG) % NH == NH - 1:
                        b = (t - O_LAG) // NH
                        t0, n = BL[b]
                        take_aux(act, ("turn", b))
                        A(yb_hi[:, :, t0:t0 + n],
                          aux[:, aux_of(("turn", b)), 0:KB * n].rearrange("p (j t) -> p j t", j=KB),
                          ACT.Copy).then_inc(ybhi_ready, 1)

            def mlstm():
                g = Steps(act, gate_step)
                act.wait_ge(pv_done, NA)
                act.dma_start(sel_sb[:, :, :], sel).then_inc(sel_landed, 16)
                act.wait_ge(o_read, NB)
                act.wait_ge(acc_free[A_UNIT[6] % 2], A_UNIT[6] // 2 + 1)
                act.wait_ge(acc_free[(A_UNIT[6] + 1) % 2], (A_UNIT[6] + 1) // 2 + 1)
                g.did(A(tmp[0:NM, 0, :], tmp[0:NM, 5, :], ACT.Abs))
                g.settle()
                g.did(A(tmp[0:NM, 0, :], tmp[0:NM, 0, :], ACT.Exp, scale=-1.0))
                g.settle()
                g.did(A(tmp[0:NM, 0, :], tmp[0:NM, 0, :], ACT.Ln, bias=1.0))
                take_aux(act, ("gate_cols",))
                s = aux_of(("gate_cols",))
                for which, dst, func in ((0, c_tok, ACT.Copy), (1, floor_tok, ACT.Exp)):
                    v = aux[:, s, NB * NM * which:NB * NM * (which + 1)].rearrange("p (b m) -> p b m", m=NM)
                    A(dst[:, 0, :], v[:, 0, :], func)
                    ins = A(dst[0:QB, 1:NB, :], v[0:QB, 1:NB, :], func)
                ins.then_inc(aux_free[s], 1)
                for m in range(NM):
                    key = ("stab", m)
                    take_aux(act, key)
                    if m >= 2:
                        act.wait_ge(arg_ready, NB * (m - 1))
                    A(tmp[:, 1 + m % 2, :], aux[:, aux_of(key), 0:T], ACT.Copy).then_inc(aux_free[aux_of(key)], 1)
                    for c in range(NB):
                        k0, nk = BL[c]
                        i = NB * m + c
                        act.wait_ge(arg_ready, i + 1)
                        A(tmp[0:nk, 3 + i % 2, k0:T], tmp[0:nk, 3 + i % 2, k0:T], ACT.Exp).then_inc(decay_ready, 1)
                    for b in range(NB):
                        i = NB * m + b
                        n = BL[b][1]
                        act.wait_ge(num_done, i + 1)
                        if i >= 2:
                            act.wait_ge(num_read, i - 1)
                        A(den[0:n, i % 2:i % 2 + 1], acc[0:n, i % 4, P:P + 1], ACT.Abs).then_inc(den_abs, 1)
                        act.wait_ge(num_read, i + 1)
                        if i >= 1:
                            act.wait_ge(mh_squared, i)
                        A(tmp[0:n, 0, 0:P], m_h[0:n, b, m, :], ACT.Square,
                          accum_out=m_ss[0:n, NM * b + m:NM * b + m + 1]).then_inc(mh_squared, 1)
                act.wait_ge(mh_step, 2)
                A(m_r[:, :], m_var[:, :], ACT.Ln).then_inc(mh_act, 1)
                act.wait_ge(mh_act, 1)
                A(m_r[:, :], m_r[:, :], ACT.Exp, scale=-0.5).then_inc(mh_act, 1)
                for m in range(KB):
                    branch_round(m, yc)

            def branch_round(g, dst):
                if g < KB:
                    free_aux(act, ("hturn", g))
                else:
                    n = A_UNIT[FIRST_CONV + 3 * ((g - KB) // 2) + 2] + g % 2
                    act.wait_ge(acc_free[n % 2], n // 2 + 2)
                A(dst[0][:, g % KB, :], tmp[:, 4 + g % 2, :], ACT.Copy).then_inc(brhi_ready, 1)

            for i in range(SEQ // P):
                for j in range(2):
                    e = 2 * i + j
                    act.wait_ge(io_turned, 2 + e + 1)
                    A(h[:, 4 * j:4 * j + 4, META + i * P:META + (i + 1) * P],
                      acc[:, e % 4, :].rearrange("p (k t) -> p k t", k=4), ACT.Copy).then_inc(io_placed, 1)
            act.drain().then_inc(arrived, 1)
            act.wait_ge(layer_go, 1)

            with act.Fori(0, DEPTH) as layer:
                nc.scalar.preload_act_table_set(LN_EXP_SET)
                w_round(0, 0)
                square_h(0, True)
                rstd_seed(0)
                ffn(0)
                square_h(1, False)
                rstd_seed(2)
                round_x(1)
                for j in range(5):
                    mixer_unit(j)
                take_aux(act, ("wi",))
                s = aux_of(("wi",))
                A(wi_tok[0:QB, 1:NB, :], aux[0:QB, s, 0:(NB - 1) * P].rearrange("p (b c) -> p b c", b=NB - 1)[:, :, DH:DH + NIDX],
                  ACT.Copy, scale=float(NIDX) ** -0.5).then_inc(aux_free[s], 1)
                for b in range(1, NB):
                    for i in range(NIDX):
                        index_rel(b, i)
                    for j in UNITS_AFTER[b]:
                        mixer_unit(j)
                attention()
                mlstm()
                nc.scalar.preload_act_table_set(TANH_SET)
                for j in range(FIRST_CONV, N_MIX):
                    kind = MIX[j][0]
                    n = A_UNIT[j]
                    act.wait_ge(acc_done, 1 + n)
                    w_round(U_MIX + j + 1, (U_MIX + j + 1) % 2)
                    if kind == "cxc":
                        c = 2 * ((j - FIRST_CONV) // 3) + (j - FIRST_CONV) % 3
                        if c >= 2:
                            cc = A_UNIT[FIRST_CONV + c - 2] + 1
                            act.wait_ge(acc_free[cc % 2], cc // 2 + 2)
                        evac(n, tmp[:, c % 2, :])
                    else:
                        for c in range(2):
                            branch_round(KB + 2 * ((j - FIRST_CONV) // 3) + c, ya)
                with act.Fori(0, KD // 2) as i:
                    for s in range(2):
                        nn = A_MERGE + 6 * s
                        for r in range(3):
                            u = U_MERGE + 3 * s + r
                            act.wait_ge(acc_done, 1 + nn + (0, 2, 5)[r] + 12 * i)
                            w_round_loop(u + 1, i, 6, (u + 1) % 2, "branch2" if r == 1 else "full")
                            for c in ((0, 1), (0,), ())[r]:
                                g = 2 * r + c
                                act.wait_ge(acc_done, 1 + nn + g + 12 * i + 1)
                                act.wait_ge(mlo_ready, 1 + 2 * i + s)
                                A(halves(tmp[:, 3 * s + g, :]), acc_halves((nn + g) % 2), ACT.Tanh, scale=0.5)\
                                    .then_inc(acc_free[(nn + g) % 2], 1)
                        act.wait_ge(mf_ready, 2 * i + s + 1)
                        A(mg_hi[:, bass.ds(2 * i + s, 1), :], tmp[:, 3 * s:3 * s + 1, :], ACT.Copy).then_inc(mhi_ready, 1)
                for j in range(OUT_UNITS):
                    n = A_OUT + 2 * j
                    act.wait_ge(acc_done, 1 + n)
                    w_round(U_OUT + j + 1, (U_OUT + j + 1) % 2)
                    for c in range(2):
                        act.wait_ge(acc_done, 1 + n + c + 1)
                        A(halves(y[:, 2 * j + c, :]), acc_halves((n + c) % 2), ACT.Copy).then_inc(acc_free[(n + c) % 2], 1)
                nc.scalar.preload_act_table_set(LN_EXP_SET)
                rstd_seed(3)
                square_h(2, True)
                rstd_seed(4)
                ffn(1)
                end_of_layer(act, layer + 1)

        @block.vector
        def _(dve):
            V = nc.vector

            def variance(q, scale):
                take_aux(dve, ("norm", q))
                s = aux_of(("norm", q))
                V.tensor_scalar(halves(tmp[:, 2, :]), aux_halves(s), scale, EPS, ALU.mult, ALU.add).then_inc(aux_free[s], 1)

            def rstd(q):
                dve.wait_ge(seed_ready, q + 1)
                V.tensor_tensor(tmp[:, 2, :], tmp[:, 2, :], tmp[:, 3, :], ALU.mult).then_inc(newton, 1)
                dve.wait_ge(newton, 2 * q + 1)
                V.scalar_tensor_tensor(tmp[:, 2, :], tmp[:, 2, :], -0.5, tmp[:, 3, :], ALU.mult, ALU.mult).then_inc(newton, 1)
                dve.wait_ge(newton, 2 * q + 2)
                V.scalar_tensor_tensor(tmp[:, 5, :], tmp[:, 2, :], 1.5, tmp[:, 3, :], ALU.add, ALU.mult).then_inc(rstd_ready, 1)
                dve.wait_ge(rstd_ready, q + 1)

            def gain_of(s, k):
                return cur[:, G_NORM + s * KD + k:G_NORM + s * KD + k + 1]

            def result(p, k):
                if k >= 2:
                    dve.wait_ge(h_ready, KD * p + k - 1)
                V.scalar_tensor_tensor(tmp[:, 2 + k % 2, :], y[:, k, :], gain_of(2 * p + 1, k), tmp[:, 5, :],
                                       ALU.mult, ALU.mult).then_inc(res_ready, 1)

            def add_squares(p, k):
                dve.wait_ge(sq_ready, KD * p + k + 1)
                if k >= 2:
                    dve.wait_ge(sq_added, (KD - 1) * p + k - 1)
                V.tensor_tensor(tmp[:, 4, :], tmp[:, 4, :], tmp[:, k % 2, :], ALU.add).then_inc(sq_added, 1)

            def norm_out(p, scale, p_in):
                if p is not None:
                    variance(2 * p + 1, scale)
                    rstd(2 * p + 1)
                for k in range(KD + 2):
                    if p is not None and k < KD:
                        result(p, k)
                    if p_in is not None and 3 <= k:
                        add_squares(p_in, k - 2)

            def norm_in_late(p):
                variance(2 * p, 1.0 / D)
                for k in range(KD):
                    dve.wait_ge(xhi_ready, KD * p + k + 1)
                    V.scalar_tensor_tensor(x_lo[:, k, :], h[:, k, :], gain_of(2 * p, k), x_hi[:, k, :].bitcast(F32),
                                           ALU.mult, ALU.subtract).then_inc(xlo_ready, 1)
                rstd(2 * p)

            def norm_in(p):
                variance(2 * p, 1.0 / D)
                rstd(2 * p)
                for k in range(KD + 1):
                    if k < KD:
                        if k >= 2:
                            dve.wait_ge(xlo_ready, KD * p + k - 1)
                        V.scalar_tensor_tensor(tmp[:, k % 2, :], h[:, k, :], gain_of(2 * p, k), tmp[:, 5, :],
                                               ALU.mult, ALU.mult).then_inc(xf_ready, 1)
                    if k >= 1:
                        dve.wait_ge(xhi_ready, KD * p + k)
                        V.tensor_tensor(x_lo[:, k - 1, :], tmp[:, (k - 1) % 2, :], x_hi[:, k - 1, :].bitcast(F32),
                                        ALU.subtract).then_inc(xlo_ready, 1)

            def y_square(p, slot, free_count, m, count):
                dve.wait_ge(acc_free[slot], free_count)
                dve.wait_ge(ysum, (KD + 1) * p + 1 + count)
                V.tensor_tensor(tmp[:, 3:4, :], y[:, m, :], y[:, m, :], ALU.mult).then_inc(ysq_ready, 1)
                dve.wait_ge(ysq_ready, KD * p + 1 + count)
                V.tensor_tensor(tmp[:, 4:5, :], tmp[:, 4:5, :], tmp[:, 3:4, :], ALU.add).then_inc(ysum, 1)

            def ffn(f):
                n0 = A_FFN[f]
                with dve.Fori(0, UP_UNITS // 2) as i:
                    for s in range(2):
                        nn = n0 + 2 * s
                        g_slot, u_slot = nn % 2, (nn + 1) % 2
                        dve.wait_ge(acc_done, 1 + nn + 4 * i + 1)
                        V.tensor_tensor(halves(tmp[:, s, :]), acc_halves(g_slot), halves(tmp[:, 5, :]), ALU.mult)\
                            .then_inc(acc_free[g_slot], 1)
                        dve.wait_ge(acc_done, 1 + nn + 4 * i + 2)
                        dve.wait_ge(alo_ready, 1 + f * KF + 2 * i + s)
                        V.tensor_tensor(halves(tmp[:, 2 + s, :]), acc_halves(u_slot), halves(tmp[:, 5, :]), ALU.mult)\
                            .then_inc(acc_free[u_slot], 1)
                        dve.wait_ge(acc_free[u_slot], (nn + 1) // 2 + 2 * i + 2)
                        dve.wait_ge(silu_ready, f * KF + 2 * i + s + 1)
                        V.tensor_tensor(tmp[:, 2 + s, :], tmp[:, 2 + s, :], tmp[:, s, :], ALU.mult).then_inc(act_ready, 1)
                p = 2 * f
                V.memset(tmp[:, 4, :], 0.0).then_inc(ysum, 1)
                n1 = n0 + 2 * UP_UNITS
                with dve.Fori(0, KD // 4) as i:
                    for j in range(4):
                        slot = (n1 + j) % 2
                        y_square(p, slot, (n1 + j) // 2 + 2 * i + 2, bass.ds(4 * i + j, 1), j + 4 * i)
                norm_out(p, 1.0 / D, 1 if f == 0 else None)

            def rope_all():
                r = Steps(dve, rope_step)
                dve.wait_ge(rope_landed, 32)
                dve.wait_ge(xlo_ready, 2 * KD)
                cos, sin = cos_sin[:, 0, :], cos_sin[:, 1, :]
                for i in range(2 + KB):
                    dst = qi_t[:, i, :] if i < 2 else q_t[:, i - 2, :]
                    key = ("rot", i)
                    take_aux(dve, key)
                    V.tensor_tensor(tmp[:, i % 2, :], aux[:, aux_of(key), 0:T], sin, ALU.mult).then_inc(aux_free[aux_of(key)], 1)
                    r.did(V.tensor_tensor(dst, dst, cos, ALU.mult))
                    r.settle()
                    dve.wait_ge(aux_free[aux_of(key)], AUX[key] // 2 + 2)
                    r.did(V.tensor_tensor(dst, dst, tmp[:, i % 2, :], ALU.add))
                    r.settle()
                for i in range(3):
                    dst = ki_t[:, :] if i == 0 else k_t[:, i - 1, :]
                    key, key2 = ("dup", i), ("dup_rot", i)
                    take_aux(dve, key)
                    V.tensor_tensor(dst, aux[:, aux_of(key), 0:T], cos, ALU.mult).then_inc(aux_free[aux_of(key)], 1)
                    take_aux(dve, key2)
                    V.tensor_tensor(tmp[:, i % 2, :], aux[:, aux_of(key2), 0:T], sin, ALU.mult).then_inc(aux_free[aux_of(key2)], 1)
                    for kk in (key, key2):
                        dve.wait_ge(aux_free[aux_of(kk)], AUX[kk] // 2 + 2)
                    ins = V.tensor_tensor(dst, dst, tmp[:, i % 2, :], ALU.add)
                    if i < 2:
                        r.did(ins)
                        r.settle()
                ins.then_inc(rope_done, 1)
                dve.wait_ge(rope_done, 1)

            def select_keys(b, k):
                n, kl, t0 = BL[b][1], KL[b], BL[b][0]
                score, work = tmp[0:n, 2, 0:kl], tmp[0:n, 3, 0:kl]
                for i in range(NIDX):
                    g = NIDX * (b - 1) + i
                    key = ("index", b, i)
                    dve.wait_ge(aux_free[aux_of(key)], AUX[key] // 2 + 2)
                    if g == 0:
                        s = aux_of(("wi",))
                        dve.wait_ge(aux_free[s], AUX[("wi",)] // 2 + 2)
                    if i == 0:
                        V.tensor_scalar(score, tmp[0:n, g % 2, 0:kl], wi_tok[0:n, b, i:i + 1], None, ALU.mult).then_inc(index_step, 1)
                    else:
                        V.scalar_tensor_tensor(score, tmp[0:n, g % 2, 0:kl], wi_tok[0:n, b, i:i + 1], score,
                                               ALU.mult, ALU.add).then_inc(index_step, 1)
                    dve.wait_ge(index_step, g + 1)
                k.did(V.tensor_tensor(tmp[0:n, 2, t0:kl], tmp[0:n, 2, t0:kl], causal_bias[0:n, 0:n], ALU.add))
                k.settle()
                for i in range(TOPK // 8):
                    src = score if i == 0 else work
                    k.did(V.max(top8[0:n, :], src))
                    k.settle()
                    k.did(V.match_replace(work, top8[0:n, :], src, TAKEN))
                    k.settle()
                V.tensor_scalar(mask[0:n, MO[b]:MO[b] + kl], work, TAKEN / 2, NEG, ALU.is_gt, ALU.mult).then_inc(mask_ready, 1)

            def attention():
                def finish(b):
                    n = BL[b][1]
                    dve.wait_ge(pv_done, NH * (b + 1))
                    if b:
                        dve.wait_ge(o_read, b)
                    V.reciprocal(row_inv[0:n, :], row_sum[0:n, b % 2, :]).then_inc(inv_ready, 1)
                    dve.wait_ge(inv_ready, b + 1)
                    V.tensor_tensor(tmp[0:n, 2 + b % 2, 0:BW].rearrange("p (h d) -> p h d", h=NH),
                                    acc[0:n, 2 + b % 2, :].rearrange("p (h d) -> p h d", h=NH),
                                    row_inv[0:n, :].unsqueeze(2).to_broadcast([n, NH, DH]), ALU.mult).then_inc(o_read, 1)

                def turned(b):
                    t0, n = BL[b]
                    s = aux_of(("turn", b))
                    dve.wait_ge(ybhi_ready, b + 1)
                    V.tensor_tensor(yb_lo[:, :, t0:t0 + n], aux[:, s, 0:KB * n].rearrange("p (j t) -> p j t", j=KB),
                                    yb_hi[:, :, t0:t0 + n].bitcast(F32), ALU.subtract).then_inc(aux_free[s], 1)

                dve.wait_ge(mask_ready, NB)
                for t in range(NA + O_LAG):
                    if t < NA:
                        b = t // NH
                        n, kl = BL[b][1], KL[b]
                        key = ("score", t)
                        s = aux_of(key)
                        take_aux(dve, key)
                        if t >= 2:
                            dve.wait_ge(p_turned, t - 1)
                            dve.wait_ge(negmax_ready, t - 1)
                        V.tensor_tensor_reduce(prob[0:n, t % 2, 0:kl], aux[0:n, s, 0:kl], mask[0:n, MO[b]:MO[b] + kl],
                                               float(DH) ** -0.5, TAKEN, ALU.add, ALU.max, row_max[0:n, t % 2:t % 2 + 1])\
                            .then_inc(aux_free[s], 1)
                        dve.wait_ge(aux_free[s], AUX[key] // 2 + 2)
                        V.tensor_scalar(neg_max[0:n, t % 2:t % 2 + 1], row_max[0:n, t % 2:t % 2 + 1], -1.0, None, ALU.mult)\
                            .then_inc(negmax_ready, 1)
                    if t >= NH + 1 and (t - 2) % NH == NH - 1:
                        finish((t - 2) // NH)
                    if t >= NH - 1 + O_LAG and (t - O_LAG) % NH == NH - 1:
                        turned((t - O_LAG) // NH)

            def mlstm():
                g = Steps(dve, gate_rows)
                row = lambda i: tmp[0:NM, i, :]
                dve.wait_ge(gate_step, 3)
                g.did(V.tensor_scalar(row(1), row(5), 0.0, None, ALU.min))
                g.settle()
                g.did(V.tensor_tensor(row(1), row(1), row(0), ALU.subtract))
                g.settle()
                g.did(V.memset(row(0), 1.0))
                g.settle()
                g.did(V.tensor_tensor_scan(row(2), row(0), row(1), 0.0, ALU.mult, ALU.add))
                g.settle()
                g.did(V.tensor_tensor(row(3), row(4), row(2), ALU.subtract))
                g.settle()
                g.did(V.tensor_tensor_scan(row(5), row(3), row(3), 0.0, ALU.max, ALU.max))
                g.settle()
                g.did(V.tensor_scalar(row(5), row(5), -1.0, None, ALU.mult))
                g.settle()
                V.tensor_tensor(row(0), row(5), row(2), ALU.subtract).then_inc(gates_ready, 1)
                V.memset(mv_tok[:, :, :, P:P + 1], 1.0).then_inc(cols_ready, 1)
                V.memset(m_ss[:, :], 1.0).then_inc(cols_ready, 1)
                s0 = aux_of(("gate_cols",))
                dve.wait_ge(aux_free[s0], AUX[("gate_cols",)] // 2 + 2)
                w = Steps(dve, wt_step)

                def arg(m, c):
                    k0, nk = BL[c]
                    i = NB * m + c
                    if c == 0:
                        key = ("stab", m)
                        dve.wait_ge(aux_free[aux_of(key)], AUX[key] // 2 + 2)
                    V.tensor_scalar(tmp[0:nk, 3 + i % 2, k0:T], tmp[0:nk, 1 + m % 2, k0:T], c_tok[0:nk, c, m:m + 1], 0.0,
                                    ALU.add, ALU.min).then_inc(arg_ready, 1)

                for m in range(NM):
                    arg(m, 0)
                    for c in range(NB):
                        k0, nk = BL[c]
                        i = NB * m + c
                        key = ("qk", m, c)
                        s = aux_of(key)
                        if c + 1 < NB:
                            if i >= 1:
                                dve.wait_ge(wt_ready, i)
                            arg(m, c + 1)
                        take_aux(dve, key)
                        dve.wait_ge(decay_ready, i + 1)
                        if m and c == 0:
                            dve.wait_ge(num_done, NB * m)
                        V.tensor_tensor(m_wt[0:nk, c, 0:T - k0], aux[0:nk, s, 0:T - k0], tmp[0:nk, 3 + i % 2, k0:T], ALU.mult)\
                            .then_inc(aux_free[s], 1)
                        dve.wait_ge(aux_free[s], AUX[key] // 2 + 2)
                        V.tensor_tensor(m_wt[0:nk, c, 0:nk], m_wt[0:nk, c, 0:nk], causal_keep[0:nk, 0:nk], ALU.mult)\
                            .then_inc(wt_ready, 1)
                    for b in range(NB):
                        i = NB * m + b
                        n = BL[b][1]
                        d = den[0:n, i % 2:i % 2 + 1]
                        dve.wait_ge(den_abs, i + 1)
                        V.tensor_tensor(d, d, floor_tok[0:n, b, m:m + 1], ALU.max).then_inc(den_step, 1)
                        dve.wait_ge(den_step, 2 * i + 1)
                        V.reciprocal(d, d).then_inc(den_step, 1)
                        dve.wait_ge(den_step, 2 * i + 2)
                        V.tensor_scalar(m_h[0:n, b, m, :], acc[0:n, i % 4, 0:P], d, None, ALU.mult).then_inc(num_read, 1)
                    dve.wait_ge(wt_ready, NB * (m + 1))
                s = Steps(dve, mh_step)
                dve.wait_ge(mh_squared, NB * NM)
                s.did(V.tensor_scalar(m_var[:, :], m_ss[:, :], 1.0 / P, EPS, ALU.mult, ALU.add))
                s.settle()
                s.did(V.tensor_scalar(mo_t[:, :, :], mo_t[:, :, :], 1.0, None, ALU.add))
                dve.wait_ge(mh_act, 2)
                s.did(V.tensor_tensor(m_var[:, :], m_var[:, :], m_r[:, :], ALU.mult))
                s.settle()
                s.did(V.scalar_tensor_tensor(m_var[:, :], m_var[:, :], -0.5, m_r[:, :], ALU.mult, ALU.mult))
                s.settle()
                s.did(V.scalar_tensor_tensor(m_r[:, :], m_var[:, :], 1.5, m_r[:, :], ALU.add, ALU.mult))
                s.settle()
                for b in range(NB):
                    n = BL[b][1]
                    V.tensor_tensor(m_h[0:n, b, :, :], m_h[0:n, b, :, :],
                                    m_r[0:n, NM * b:NM * b + NM].unsqueeze(2).to_broadcast([n, NM, P]), ALU.mult)\
                        .then_inc(mh_normed, 1)
                for m in range(NM):
                    key = ("hturn", m)
                    sl = aux_of(key)
                    take_aux(dve, key)
                    if m >= 2:
                        dve.wait_ge(brlo_ready, m - 1)
                    gain = cur[:, G_HEAD + m:G_HEAD + m + 1]
                    V.scalar_tensor_tensor(tmp[:, 4 + m % 2, 0:P], aux[:, sl, 0:P], gain, mo_t[:, m, 0:P], ALU.mult, ALU.mult)
                    V.scalar_tensor_tensor(tmp[:, 4 + m % 2, P:T].rearrange("p (b t) -> p b t", t=QB),
                                           aux[:, sl, P:NB * P].rearrange("p (b t) -> p b t", t=P)[:, :, 0:QB], gain,
                                           mo_t[:, m, P:T].rearrange("p (b t) -> p b t", t=QB), ALU.mult, ALU.mult)\
                        .then_inc(aux_free[sl], 1)
                    free_aux(dve, key)

            def conv():
                s = Steps(dve, conv_step)
                z = Steps(dve, merge_step)
                z.did(V.memset(conv_u[:, :, 0:2], 0.0))
                z.settle()
                for j in range(FIRST_CONV, N_MIX):
                    kind, n = MIX[j][0], A_UNIT[j]
                    if kind == "cxc":
                        c = 2 * ((j - FIRST_CONV) // 3) + (j - FIRST_CONV) % 3
                        tap = lambda i: cur[:, G_CONV + KB * i + c:G_CONV + KB * i + c + 1]
                        u, t = conv_u[:, c % 2, :], tmp[:, 2 + c % 2, :]
                        dve.wait_ge(acc_free[n % 2], n // 2 + 2)
                        dve.wait_ge(acc_done, 1 + n + 2)
                        sl = (n + 1) % 2
                        V.tensor_tensor(halves(u[:, 2:T + 2]), acc_halves(sl), halves(tmp[:, c % 2, :]), ALU.mult)\
                            .then_inc(acc_free[sl], 1)
                        dve.wait_ge(acc_free[sl], (n + 1) // 2 + 2)
                        s.did(V.tensor_scalar(t, u[:, 0:T], tap(0), None, ALU.mult))
                        s.settle()
                        s.did(V.scalar_tensor_tensor(t, u[:, 1:T + 1], tap(1), t, ALU.mult, ALU.add))
                        s.settle()
                        s.did(V.scalar_tensor_tensor(t, u[:, 2:T + 2], tap(2), t, ALU.mult, ALU.add))
                        s.settle()
                    else:
                        for c in range(2):
                            g = KB + 2 * ((j - FIRST_CONV) // 3) + c
                            sl = (n + c) % 2
                            dve.wait_ge(acc_done, 1 + n + c + 1)
                            dve.wait_ge(brlo_ready, g - 1)
                            V.tensor_tensor(halves(tmp[:, 4 + g % 2, :]), acc_halves(sl), halves(tmp[:, 2 + g % 2, :]), ALU.mult)\
                                .then_inc(acc_free[sl], 1)
                            dve.wait_ge(acc_free[sl], (n + c) // 2 + 2)

            def merge():
                with dve.Fori(0, KD // 2) as i:
                    for s in range(2):
                        nn = A_MERGE + 6 * s
                        for b in range(3):
                            g = 3 + b
                            sl = (nn + g) % 2
                            gsl = (nn + b) % 2
                            dve.wait_ge(acc_free[gsl], (nn + b) // 2 + 6 * i + 2)
                            dve.wait_ge(acc_done, 1 + nn + g + 12 * i + 1)
                            t = tmp[:, 3 * s + b, :]
                            V.scalar_tensor_tensor(halves(t), halves(t), 1.0, acc_halves(sl), ALU.add, ALU.mult)\
                                .then_inc(acc_free[sl], 1)
                            dve.wait_ge(acc_free[sl], (nn + g) // 2 + 6 * i + 2)
                            if b == 1:
                                V.tensor_tensor(tmp[:, 3 * s, :], tmp[:, 3 * s, :], t, ALU.add).then_inc(merge_step, 1)
                                dve.wait_ge(merge_step, 2 * i + s + 2)
                        V.tensor_tensor(tmp[:, 3 * s, :], tmp[:, 3 * s, :], tmp[:, 3 * s + 2, :], ALU.add).then_inc(mf_ready, 1)

            dve.wait_ge(io_turned, 1)
            dve.wait_ge(const_landed, 16 * 9)
            V.tensor_copy(params[:, :], aux[:, 0, 0:P]).then_inc(io_first, 1)
            dve.wait_ge(io_turned, 2)
            V.tensor_copy(h[:, :, 0:META], aux[:, 1, 0:KD * META].rearrange("p (k t) -> p k t", k=KD)).then_inc(io_first, 1)
            dve.drain().then_inc(arrived, 1)
            dve.wait_ge(layer_go, 1)

            with dve.Fori(0, DEPTH) as layer:
                c = Steps(dve, cur_ready)
                c.did(V.tensor_copy(cur[:, G_NORM:G_CONV], params[:, bass.ds(layer * 6 * KD, 6 * KD)]))
                c.did(V.tensor_copy(cur[:, G_CONV:G_HEAD], params[:, bass.ds(layer * 3 * KB + DEPTH * 6 * KD, 3 * KB)]))
                c.did(V.tensor_copy(cur[:, G_HEAD:G_HEAD + NM],
                                    params[:, bass.ds(layer * NM + DEPTH * (6 * KD + 3 * KB), NM)]))
                c.did(V.tensor_copy(gate_bias_cur[:, :].unsqueeze(2), gate_bias[:, :, bass.ds(layer, 1)]))
                c.settle()
                for s in (1, 3, 5):
                    v = cur[:, G_NORM + s * KD:G_NORM + (s + 1) * KD]
                    c.did(V.tensor_scalar(v, v, 0.5, None, ALU.mult))
                v = cur[:, G_HEAD:G_HEAD + NM]
                c.did(V.tensor_scalar(v, v, 0.5, None, ALU.mult))
                c.settle()
                norm_out(None, None, 0)
                norm_in_late(0)
                ffn(0)
                norm_in(1)
                rope_all()
                V.tensor_copy(mask[:, 0:P], causal_bias[:, :]).then_inc(mask_ready, 1)
                k = Steps(dve, topk_step)
                for b in range(1, NB):
                    select_keys(b, k)
                attention()
                mlstm()
                conv()
                merge()
                dve.wait_ge(mf_ready, KD)
                dve.wait_ge(mlo_ready, 1 + KD)
                V.memset(tmp[:, 4, :], 0.0).then_inc(ysum, 1)
                for m in range(KD):
                    n = A_OUT + m
                    y_square(1, n % 2, n // 2 + 2, slice(m, m + 1), m)
                norm_out(1, 0.25 / D, 2)
                norm_in_late(2)
                ffn(1)
                end_of_layer(dve, layer + 1)

            for i in range(SEQ // P):
                for j in range(2):
                    e = 2 * i + j
                    dve.wait_ge(io_turned, e + 1)
                    if i >= 2:
                        dve.wait_ge(out_stored[i % 2], 16 * (i // 2))
                    V.tensor_copy(w_raw[:, i % 2, 0, 4 * j:4 * j + 4, :].rearrange("p k c -> p (k c)"), acc[:, e % 4, :])\
                        .then_inc(io_placed, 1)

        @block.tensor
        def _(pe):
            MM = nc.tensor.matmul

            def open_acc(n, slot, half_n):
                pe.wait_ge(acc_free[slot], half_n + 1)

            def open_aux(key):
                pe.wait_ge(aux_free[aux_of(key)], AUX[key] // 2 + 1)

            def chunk(slot, wslot, c, xs, k0, kn, wk0=0, first=True, last=True):
                for k in range(kn):
                    lh, ll = w_hi[:, wslot, c, wk0 + k, :], w_lo[:, wslot, c, wk0 + k, :]
                    for j, (w, xx) in enumerate(((lh, xs[0]), (lh, xs[1]), (ll, xs[0]))):
                        for a in range(HALF):
                            ins = MM(acc[:, 2 * slot + a, 0:TH], w, xx[:, k0 + k, a * TH:(a + 1) * TH],
                                     start=(first and k == 0 and j == 0), stop=(last and k == kn - 1 and j == 2))
                return ins

            def token_blocks(n, wslot, pair, cn):
                slot = n % 2
                open_acc(n, slot, n // 2)
                for a, b in enumerate(pair):
                    t0, rows = BL[b]
                    for k in range(KD):
                        for j in range(3):
                            xx, w = ((x_hi, w_hi), (x_lo, w_hi), (x_hi, w_lo))[j]
                            ins = MM(acc[0:rows, 2 * slot + a, 0:cn * P].rearrange("p (c n) -> p c n", c=cn),
                                     xx[:, k, t0:t0 + rows], w[:, wslot, 0:cn, k, :],
                                     start=(k == 0 and j == 0), stop=(k == KD - 1 and j == 2))
                ins.then_inc(acc_done, 1)

            def norm_sum(q, done, count):
                key = ("norm", q)
                open_aux(key)
                pe.wait_ge(done, count)
                for a in range(HALF):
                    ins = MM(aux_halves(aux_of(key))[:, a, :], ones[:, :], tmp[:, 4, a * TH:(a + 1) * TH], start=True, stop=True)
                ins.then_inc(aux_done, 1)

            def first_unit(n0, p, norm_between):
                for c in range(2):
                    open_acc(n0 + c, (n0 + c) % 2, (n0 + c) // 2)

                def passes(k, ws_xs, last):
                    for c in range(2):
                        slot = (n0 + c) % 2
                        for j, (w, xx) in enumerate(ws_xs):
                            for a in range(HALF):
                                ins = MM(acc[:, 2 * slot + a, 0:TH], w[:, 0, c, k, :], xx[:, k, a * TH:(a + 1) * TH],
                                         start=(k == 0 and j == 0 and xx is x_hi and w is w_hi), stop=(last and j == len(ws_xs) - 1))
                        if last:
                            ins.then_inc(acc_done, 1)

                if norm_between:
                    for k in range(KD):
                        pe.wait_ge(xhi_ready, KD * p + k + 1)
                        passes(k, ((w_hi, x_hi), (w_lo, x_hi)), False)
                    norm_sum(2 * p, sq_added, (KD - 1) * (p + 1))
                    for k in range(KD):
                        pe.wait_ge(xlo_ready, KD * p + k + 1)
                        passes(k, ((w_hi, x_lo),), k == KD - 1)
                else:
                    for k in range(KD):
                        pe.wait_ge(xlo_ready, KD * p + k + 1)
                        passes(k, ((w_hi, x_hi), (w_lo, x_hi), (w_hi, x_lo)), k == KD - 1)

            def ffn(f):
                u0, n0 = U_FFN[f], A_FFN[f]
                def up_unit(i, s):
                    pe.wait_ge(wlo_ready, u0 + s + 2 * i + 3)
                    for c in range(2):
                        n = n0 + 2 * s + c
                        open_acc(n, n % 2, n // 2 + 2 * i)
                        chunk(n % 2, s, c, (x_hi, x_lo), 0, KD).then_inc(acc_done, 1)

                pe.wait_ge(wlo_ready, u0 + 3)
                first_unit(n0, 2 * f, True)
                up_unit(0, 1)
                with pe.Fori(1, UP_UNITS // 2) as i:
                    for s in range(2):
                        up_unit(i, s)
                pe.wait_ge(alo_ready, 1 + KF * (f + 1))
                n1 = n0 + 2 * UP_UNITS
                with pe.Fori(0, KD // 4) as i:
                    for q in range(6):
                        kg = q % 3
                        pe.wait_ge(wlo_ready, u0 + UP_UNITS + q + 6 * i + 3)
                        for c in range(2):
                            n = n1 + 2 * (q // 3) + c
                            if kg == 0:
                                open_acc(n, n % 2, n // 2 + 2 * i)
                            ins = chunk(n % 2, q % 2, c, (a_hi, a_lo), kg * KD, DOWN_K[kg], 0, kg == 0, kg == 2)
                            if kg == 2:
                                ins.then_inc(acc_done, 1)
                        if kg < 2:
                            ins.then_inc(part_done, 1)
                norm_sum(4 * f + 1, ysum, (KD + 1) * (2 * f + 1))

            def mixer_unit(j):
                kind, n = MIX[j][0], A_UNIT[j]
                ws = (U_MIX + j) % 2
                pe.wait_ge(wlo_ready, U_MIX + j + 3)
                if kind in ("v", "mv"):
                    for a, pair in enumerate(((0, 1), (2, 3), (4,))):
                        token_blocks(n + a, ws, pair, 1 if kind == "v" else 2)
                else:
                    for c in range(2):
                        open_acc(n + c, (n + c) % 2, (n + c) // 2)
                        chunk((n + c) % 2, ws, c, (x_hi, x_lo), 0, KD).then_inc(acc_done, 1)

            def over_tokens(key, lhsT, rhs, n0, n1, rows=P):
                s = aux_of(key)
                open_aux(key)
                for a, z in ((0, 512), (512, 1024)):
                    if a < n1 - n0:
                        e = min(z, n1 - n0)
                        ins = MM(aux[0:rows, s, a:e], lhsT, rhs[:, n0 + a:n0 + e], start=True, stop=True)
                ins.then_inc(aux_done, 1)

            def rope_all():
                pe.wait_ge(rope_landed, 32)
                for c in range(4):
                    n = A_UNIT[0] + c
                    pe.wait_ge(acc_free[n % 2], n // 2 + 2)
                for i in range(2 + KB):
                    if i == 2:
                        for c in range(4):
                            n = A_UNIT[2] + c
                            pe.wait_ge(acc_free[n % 2], n // 2 + 2)
                    over_tokens(("rot", i), rope_mats[:, ROT, :], qi_t[:, i, :] if i < 2 else q_t[:, i - 2, :], 0, T)
                for i, (src, d, r) in enumerate(((5, DUP0, DROT0), (4, DUP0, DROT0), (4, DUP1, DROT1))):
                    over_tokens(("dup", i), rope_mats[:, d, :], tmp[:, src, :], 0, T)
                    over_tokens(("dup_rot", i), rope_mats[:, r, :], tmp[:, src, :], 0, T)
                key = ("wi",)
                open_aux(key)
                for b in range(1, NB):
                    t0, n = BL[b]
                    ins = nc.tensor.transpose(aux[0:n, aux_of(key), (b - 1) * P:b * P], tmp[:, 5, t0:t0 + n], ident[:, :])
                ins.then_inc(aux_done, 1)

            def attention():
                for c in range(2):
                    n = A_UNIT[FIRST_CONV] - 1 - c
                    pe.wait_ge(acc_free[n % 2], n // 2 + 2)
                for t in range(NA + O_LAG):
                    if t < NA:
                        b, hd = divmod(t, NH)
                        t0, n = BL[b]
                        po = DH * (hd % 2)
                        over_tokens(("score", t), q_t[po:po + DH, hd // 2, t0:t0 + n],
                                    k_t[po:po + DH, hd // (NH // NKV), :], 0, KL[b], n)
                    if 1 <= t <= NA:
                        s = t - 1
                        b = s // NH
                        n = BL[b][1]
                        pe.wait_ge(p_ready, s + 1)
                        if s >= 2:
                            pe.wait_ge(pt_copied, s - 1)
                        for c in range(b + 1):
                            k0, nk = BL[c]
                            ins = nc.tensor.transpose(acc[0:nk, s % 2, c * n:(c + 1) * n], prob[0:n, s % 2, k0:k0 + nk],
                                                      ident[0:n, 0:n])
                        ins.then_inc(p_turned, 1)
                    if 2 <= t <= NA + 1:
                        s = t - 2
                        b, hd = divmod(s, NH)
                        n = BL[b][1]
                        g = hd // (NH // NKV)
                        pe.wait_ge(pt_copied, s + 1)
                        if hd == 0 and b >= 2:
                            pe.wait_ge(o_read, b - 1)
                        for c in range(b + 1):
                            nk = BL[c][1]
                            ins = MM(acc[0:n, 2 + b % 2, hd * DH:(hd + 1) * DH], prob_t[0:nk, s % 2, c * n:(c + 1) * n],
                                     v_tok[0:nk, c, g * DH:(g + 1) * DH], start=(c == 0), stop=(c == b))
                        ins.then_inc(pv_done, 1)
                    if t >= NH - 1 + O_LAG and (t - O_LAG) % NH == NH - 1:
                        b = (t - O_LAG) // NH
                        n = BL[b][1]
                        key = ("turn", b)
                        open_aux(key)
                        pe.wait_ge(o_read, b + 1)
                        for j in range(KB):
                            ins = nc.tensor.transpose(aux[:, aux_of(key), j * n:(j + 1) * n],
                                                      tmp[0:n, 2 + b % 2, j * P:(j + 1) * P], ident[0:n, 0:n])
                        ins.then_inc(aux_done, 1)

            def mlstm():
                key = ("gate_cols",)
                open_aux(key)
                pe.wait_ge(gates_ready, 1)
                for which, r in ((0, 3), (1, 0)):
                    for b in range(NB):
                        t0, n = BL[b]
                        o = NM * (NB * which + b)
                        ins = nc.tensor.transpose(aux[0:n, aux_of(key), o:o + NM], tmp[0:NM, r, t0:t0 + n], ident[0:NM, 0:NM])
                ins.then_inc(aux_done, 1)
                pe.wait_ge(sel_landed, 16)
                pe.wait_ge(cols_ready, 2)

                def qk(m, c):
                    k0, nk = BL[c]
                    over_tokens(("qk", m, c), mk_t[:, m, k0:k0 + nk], mq_t[:, m, :], k0, T, nk)

                for m in range(NM):
                    over_tokens(("stab", m), sel_sb[:, m, :], tmp[0:NM, 5, :], 0, T)
                    for c in range(NB):
                        qk(m, c)
                    for b in range(NB):
                        i = NB * m + b
                        t0, n = BL[b]
                        pe.wait_ge(wt_ready, i + 1)
                        if i >= 4:
                            pe.wait_ge(num_read, i - 3)
                        for c in range(b + 1):
                            k0, nk = BL[c]
                            ins = MM(acc[0:n, i % 4, 0:P + 1], m_wt[0:nk, c, t0 - k0:t0 - k0 + n], mv_tok[0:nk, c, m, :],
                                     start=(c == 0), stop=(c == b))
                        ins.then_inc(num_done, 1)
                pe.wait_ge(mh_normed, NB)
                for m in range(NM):
                    key = ("hturn", m)
                    open_aux(key)
                    for b in range(NB):
                        n = BL[b][1]
                        ins = nc.tensor.transpose(aux[:, aux_of(key), b * P:b * P + n], m_h[0:n, b, m, :], ident[0:n, 0:n])
                    ins.then_inc(aux_done, 1)
                pe.wait_ge(num_read, NB * NM)

            pe.wait_ge(const_landed, 16 * 9)
            nc.tensor.transpose(aux[:, 0, 0:P], tmp[:, 5, 0:P], ident[:, :]).then_inc(io_turned, 1)
            pe.wait_ge(io_in, 16)
            for k in range(KD):
                ins = nc.tensor.transpose(aux[:, 1, k * META:(k + 1) * META], tmp[0:META, k // 4, (k % 4) * P:(k % 4 + 1) * P],
                                          ident[0:META, 0:META])
            ins.then_inc(io_turned, 1)
            for i in range(SEQ // P):
                pe.wait_ge(raw_landed[i % 2], 16 * (i // 2 + 1))
                for j in range(2):
                    e = 2 * i + j
                    if e >= 4:
                        pe.wait_ge(io_placed, e - 3)
                    for k in range(4):
                        ins = nc.tensor.transpose(acc[:, e % 4, k * P:(k + 1) * P], w_raw[:, i % 2, 0, 4 * j + k, :], ident[:, :])
                    ins.then_inc(io_turned, 1)
            pe.wait_ge(io_placed, 2 * (SEQ // P))
            pe.wait_ge(io_first, 2)
            pe.drain().then_inc(arrived, 1)
            pe.wait_ge(layer_go, 1)

            with pe.Fori(0, DEPTH) as layer:
                ffn(0)
                norm_sum(2, sq_added, (KD - 1) * 2)
                pe.wait_ge(wlo_ready, U_MIX + 3)
                first_unit(A_MIX, 1, False)
                for j in range(1, 5):
                    mixer_unit(j)
                rope_all()
                pe.wait_ge(rope_done, 1)
                for b in range(1, NB):
                    t0, n = BL[b]
                    for i in range(NIDX):
                        po = DH * (i % 2)
                        over_tokens(("index", b, i), qi_t[po:po + DH, i // 2, t0:t0 + n], ki_t[po:po + DH, :], 0, KL[b], n)
                    for j in UNITS_AFTER[b]:
                        mixer_unit(j)
                attention()
                mlstm()
                for j in range(FIRST_CONV, N_MIX):
                    mixer_unit(j)
                pe.wait_ge(brlo_ready, 2 * KB)
                with pe.Fori(0, KD // 2) as i:
                    for s in range(2):
                        nn = A_MERGE + 6 * s
                        u = U_MERGE + 3 * s
                        for r, parts in enumerate((((0, "x", 0), (1, "x", 0)), ((0, "x", 0), (1, ya, 0), (1, yb, KB)),
                                                   ((0, yc, 0),))):
                            pe.wait_ge(wlo_ready, u + r + 6 * i + 3)
                            for a, (c, xs, wk0) in enumerate(parts):
                                n = nn + 2 * r + a + (1 if r == 2 else 0)
                                open_acc(n, n % 2, n // 2 + 6 * i)
                                full = xs == "x"
                                chunk(n % 2, (u + r) % 2, c, (x_hi, x_lo) if full else xs, 0, KD if full else KB, wk0)\
                                    .then_inc(acc_done, 1)
                pe.wait_ge(mlo_ready, 1 + KD)
                for j in range(OUT_UNITS):
                    u = U_OUT + j
                    pe.wait_ge(wlo_ready, u + 3)
                    for c in range(2):
                        n = A_OUT + 2 * j + c
                        open_acc(n, n % 2, n // 2)
                        chunk(n % 2, u % 2, c, (mg_hi, mg_lo), 0, KD).then_inc(acc_done, 1)
                norm_sum(3, ysum, (KD + 1) * 2)
                ffn(1)
                end_of_layer(pe, layer + 1)

            for i in range(SEQ // P):
                for j in range(2):
                    e = 2 * i + j
                    if e >= 4:
                        pe.wait_ge(io_placed, e - 3)
                    for k in range(4):
                        ins = nc.tensor.transpose(acc[:, e % 4, k * P:(k + 1) * P],
                                                  h[:, 4 * j + k, META + i * P:META + (i + 1) * P], ident[:, :])
                    ins.then_inc(io_turned, 1)


def shape_constants(meta_rows, seq, head_dim):
    import numpy as np

    t = meta_rows + seq
    freq = (1.0 / (10000.0 ** (np.arange(0, head_dim, 2, dtype=np.float32) / head_dim))).astype(np.float32)
    angle = np.arange(t, dtype=np.float32)[None, :] * freq[np.arange(P) % (head_dim // 2)][:, None]
    tables = np.stack([np.cos(angle), np.sin(angle)]).astype(np.float32)
    half = head_dim // 2
    i = np.arange(P)
    rot = np.zeros((P, P), np.float32)
    rot[(i + half) % head_dim + i // head_dim * head_dim, i] = np.where(i % head_dim < half, -1.0, 1.0)
    dup = np.zeros((2, P, P), np.float32)
    for g in range(2):
        dup[g, g * head_dim + i % head_dim, i] = 1.0
    tri = i[None, :] <= i[:, None]
    mats = np.stack([np.eye(P), np.ones((P, P)), np.where(tri, 0.0, NEG), tri.T, rot, dup[0], dup[1],
                     dup[0] @ rot, dup[1] @ rot]).astype(np.float32)
    sel = np.zeros((4, 4, P), np.float32)
    sel[np.arange(4), np.arange(4)] = 1.0
    return {"rope_tab": tables, "mats": mats, "sel": sel}


_INS = ["x", "meta", "norm_g", "w_ffn_gu", "w_ffn_down", "w_in", "w_conv", "b_igate", "b_fgate",
        "mh_norm_g", "w_branch", "w_out"]


def kernel(**inputs):
    import numpy as np
    import concourse.bacc as bacc
    from concourse.bass_utils import run_bass_kernel_spmd

    nc = bacc.Bacc("TRN2", target_bir_lowering=False, num_devices=1)
    arrays, args = {}, []
    data = {name: np.ascontiguousarray(inputs[name]) for name in _INS}
    data.update(shape_constants(data["meta"].shape[0], data["x"].shape[1], 64))
    for name, a in data.items():
        arrays[f"in_{name}_dram"] = a
        args.append(nc.dram_tensor(f"in_{name}_dram", a.shape, mybir.dt.from_np(a.dtype), kind="ExternalInput").ap())
    out = nc.dram_tensor("out_dram", data["x"].shape, F32, kind="ExternalOutput").ap()
    trunk_program(nc, *args, out)
    r = run_bass_kernel_spmd(nc, [arrays], core_ids=[0])
    return r.results[0]["out_dram"]
```

```python
from contextlib import ExitStack

import concourse.bass as bass
from concourse import mybir

F32 = mybir.dt.float32
F32R = mybir.dt.float32r
ALU = mybir.AluOpType
ACT = mybir.ActivationFunctionType
AX = mybir.AxisListType

P = 128
HALF = 2
EPS = 1e-6
NEG = -1e30
TAKEN = -3e38
LN_EXP_SET = "natural_log_exp_and_others"
TANH_SET = "exp_and_others"


def trunk_program(nc, x, meta, norm_g, w_ffn_gu, w_ffn_down, w_in, w_conv, b_igate, b_fgate,
                  mh_norm_g, w_branch, w_out, rope_tab, mats, sel, out):
    DEPTH, _, D, F2 = w_ffn_gu.shape
    SEQ, META = x.shape[1], meta.shape[0]
    T = SEQ + META
    TH = T // HALF
    FF = F2 // 2
    KD = D // P
    KF = FF // P
    BW = w_branch.shape[2]
    KB = BW // P
    DH = 64
    NH = BW // DH
    NKV, NIDX = 2, 4
    NM = BW // P
    TOPK = min(256, SEQ // 4)
    NB = 5
    QB = (T - P) // (NB - 1)
    BL = [(0, P)] + [(P + i * QB, QB) for i in range(NB - 1)]
    KL = [t0 + n for t0, n in BL]
    MO = [sum(KL[:b]) for b in range(NB)]
    assert T == P + (NB - 1) * QB and TOPK == P and D == 2 * BW and KB == 4 and NM == 4
    C_CX, C_CB, C_CC = 0, BW, 2 * BW
    C_Q = 3 * BW
    C_K = C_Q + BW
    C_V = C_K + NKV * DH
    C_QI = C_V + NKV * DH
    C_KI = C_QI + NIDX * DH
    C_MQ = C_KI + DH + NIDX
    C_MK, C_MV, C_MO = C_MQ + BW, C_MQ + 2 * BW, C_MQ + 3 * BW
    C_MI = C_MQ + 4 * BW
    C_MF = C_MI + NM
    C_GT = C_MF + NM

    UP_UNITS = KF
    DOWN_K = [KD, KD, KF - 2 * KD]
    DOWN_UNITS = 3 * KD // 2
    FFN_UNITS = UP_UNITS + DOWN_UNITS
    MIX = [("qi", C_QI, C_QI + P), ("k", C_K, C_KI), ("q", C_Q, C_Q + P), ("q", C_Q + 2 * P, C_Q + 3 * P),
           ("v", C_V, C_V + P), ("if", C_MI, C_MF)]
    for kind, c in (("mq", C_MQ), ("mk", C_MK), ("mv", C_MV), ("mo", C_MO)):
        MIX += [(kind, c + 2 * j * P, c + (2 * j + 1) * P) for j in range(2)]
    for j in range(0, KB, 2):
        MIX += [("cxc", C_CX + j * P, C_CC + j * P), ("cxc", C_CX + (j + 1) * P, C_CC + (j + 1) * P),
                ("cb", C_CB + j * P, C_CB + (j + 1) * P)]
    N_MIX = len(MIX)
    FIRST_CONV = N_MIX - 6
    FIRST_FILL = FIRST_CONV - 2
    MERGE_UNITS = 3 * KD
    OUT_UNITS = KD // 2
    U_MIX = FFN_UNITS
    U_MERGE = U_MIX + N_MIX
    U_OUT = U_MERGE + MERGE_UNITS
    U_FFN = [0, U_OUT + OUT_UNITS]
    UNITS = U_FFN[1] + FFN_UNITS
    ACCS = {"v": 3, "mv": 3}
    N_MIXACC = [ACCS.get(kind, 2) for kind, _, _ in MIX]
    A_MIX = 2 * UP_UNITS + KD
    A_UNIT = [A_MIX + sum(N_MIXACC[:i]) for i in range(N_MIX)]
    A_MERGE = A_MIX + sum(N_MIXACC)
    A_OUT = A_MERGE + 6 * KD
    A_FFN = [0, A_OUT + KD]
    UNITS_AFTER = {1: (5,), 2: (6, 7), 3: (8, 9), 4: (10, 11)}
    assert UNITS_AFTER[NB - 1][-1] == FIRST_FILL - 1
    SLOT, USE = [], []
    for n in range(A_FFN[1] + 2 * UP_UNITS + KD):
        SLOT.append(0 if A_UNIT[FIRST_FILL] <= n < A_MERGE else n % 2)
        USE.append(SLOT[:-1].count(SLOT[-1]))
    FILLS = 2 * KD * (N_MIX - FIRST_FILL)
    ML_TAIL = KD
    ML_PLAN = NB * [1] + NM * NB * [2]
    ATT_FILLS = FILLS - ML_TAIL - sum(ML_PLAN)

    def att_fills(t):
        return range(ATT_FILLS * t // (NB * NH), ATT_FILLS * (t + 1) // (NB * NH))

    def ml_fills(step):
        f = ATT_FILLS + sum(ML_PLAN[:step])
        return range(f, f + ML_PLAN[step])

    AUX = {}

    def aux_item(*key):
        AUX[key] = len(AUX)

    for q in range(3):
        aux_item("norm", q)
    for r in range(2):
        aux_item("rot", r)
    for r in range(3):
        aux_item("dup", r)
        aux_item("dup_rot", r)
    for r in range(2, 2 + KB):
        aux_item("rot", r)
    aux_item("wi")
    N_EARLY = 4
    for b in range(1, NB):
        for i in range(NIDX):
            aux_item("index", b, i)
    NA = NB * NH
    GATE_STEP = 20
    O_LAG = 4
    for t in range(NA + O_LAG):
        if t < NA:
            aux_item("score", t)
        if t >= NH - 1 + O_LAG and (t - O_LAG) % NH == NH - 1:
            aux_item("turn", (t - O_LAG) // NH)
        if t == GATE_STEP:
            aux_item("gate_cols")
    for m in range(NM):
        aux_item("stab", m)
        for c in range(NB):
            aux_item("qk", m, c)
    for m in range(NM):
        aux_item("hturn", m)
    for q in range(3, 6):
        aux_item("norm", q)

    ctx = ExitStack()
    with ctx:
        def sem(name):
            return ctx.enter_context(nc.semaphore(name))

        CH = 4 * T
        arena_bytes = 212800
        arena = ctx.enter_context(nc.sbuf_tensor("arena", [P, arena_bytes // 4], F32))
        del arena
        base = nc.sbuf_base - arena_bytes
        place = [0]

        def at(name, shape, dt, offset):
            return nc.alloc_sbuf_tensor_at(name, shape, dt, offset=base + offset)

        def sb(name, shape, dt=F32):
            size = 4
            for s in shape[1:]:
                size *= s
            t = at(name, shape, dt, place[0])
            place[0] += (size + 31) // 32 * 32
            assert place[0] <= arena_bytes, (name, place[0])
            return t

        h = sb("h", [P, KD, T])
        y = at("y", [P, KD, T], F32, place[0])
        x_hi = sb("x_hi", [P, KD, T], F32R)
        x_lo = sb("x_lo", [P, KD, T], F32R)
        w_raw = sb("w_raw", [P, 2, 2, KD, P])
        w_hi = sb("w_hi", [P, 2, 2, KD, P], F32R)
        w_lo = sb("w_lo", [P, 2, 2, KD, P], F32R)
        tmp = sb("tmp", [P, 6, T])
        region = place[0]
        place[0] += 46 * CH

        def at_chunk(name, shape, dt, chunk, extra=0):
            return at(name, shape, dt, region + chunk * CH + extra)

        a_hi = at_chunk("a_hi", [P, KF, T], F32R, 0)
        a_lo = at_chunk("a_lo", [P, KF, T], F32R, KF)
        xu_hi = at_chunk("xu_hi", [P, KD, T], F32R, 21)
        xu_lo = at_chunk("xu_lo", [P, KD, T], F32R, 29)
        q_t = at_chunk("q_t", [P, KB, T], F32, 0)
        qi_t = at_chunk("qi_t", [P, 2, T], F32, 4)
        ki_t = at_chunk("ki_t", [P, T], F32, 6)
        k_t = at_chunk("k_t", [P, NKV, T], F32, 7)
        cos_sin = at_chunk("cos_sin", [P, 2, T], F32, 9)
        mask = at_chunk("mask", [P, sum(KL)], F32, 11)
        rope_mats = at_chunk("rope_mats", [P, 5, P], F32, 15)
        prob = at_chunk("prob", [P, 2, T], F32, 15)
        prob_t = at_chunk("prob_t", [P, 2, 512], F32, 17)
        v_tok = at_chunk("v_tok", [P, NB, P], F32, 19)
        mq_t = at_chunk("mq_t", [P, NM, T], F32, 21)
        mk_t = at_chunk("mk_t", [P, NM, T], F32, 25)
        mo_t = at_chunk("mo_t", [P, NM, T], F32, 29)
        mv_tok = at_chunk("mv_tok", [P, NB, NM, P + 1], F32, 33)
        yb_hi = at_chunk("yb_hi", [P, KB, T], F32R, 38)
        yb_lo = at_chunk("yb_lo", [P, KB, T], F32R, 42)
        WT = [sum(T - BL[i][0] for i in range(c)) for c in range(NB + 1)]
        m_wt = [at_chunk("m_wt0", [P, WT[NB]], F32, 0), at_chunk("m_wt1", [P, WT[NB]], F32, 16)]
        assert WT[NB] <= 3 * T
        m_h = at_chunk("m_h", [P, NB, NM, P], F32, 11)
        cx_t = at_chunk("cx_t", [P, T], F32, 6)
        ya_f = [at_chunk(f"ya_f{c}", [P, T], F32, (4, 5, 7, 8)[c]) for c in range(KB)]
        conv_u = at_chunk("conv_u", [P, T + 2], F32, 9)
        sel_sb = at_chunk("sel_sb", [NM, NM, P], F32, 10, 64)
        yc_hi = at_chunk("yc_hi", [P, KB, T], F32R, 21)
        yc_lo = at_chunk("yc_lo", [P, KB, T], F32R, 25)
        ya_hi = at_chunk("ya_hi", [P, KB, T], F32R, 11)
        ya_lo = at_chunk("ya_lo", [P, KB, T], F32R, 15)
        mg_hi = at_chunk("mg_hi", [P, KD, T], F32R, 0)
        mg_lo = at_chunk("mg_lo", [P, KD, T], F32R, 29)
        ident = sb("ident", [P, P])
        ones = sb("ones", [P, P])
        causal_bias = sb("causal_bias", [P, P])
        causal_keep = sb("causal_keep", [P, P])
        params = sb("params", [P, P])
        cur = sb("cur", [P, 64])
        gate_bias = sb("gate_bias", [NM, 2, DEPTH])
        gate_bias_cur = sb("gate_bias_cur", [NM, 2])

        def small(first_chunk, offset, tiles):
            made = []
            for name, shape in tiles:
                made.append(at(name, [P, *shape], F32, region + first_chunk * CH + offset))
                size = 4
                for d in shape:
                    size *= d
                offset += (size + 31) // 32 * 32
            return made

        wi_tok, top8, row_max, neg_max, row_sum, row_inv = small(11, 4 * sum(KL), (
            ("wi_tok", (NB, NIDX)), ("top8", (8,)), ("row_max", (2,)), ("neg_max", (2,)), ("row_sum", (2, NH)),
            ("row_inv", (NH,))))
        c_tok, floor_tok, den, m_ss, m_var, m_r = small(19, 4 * NB * P, (
            ("c_tok", (NB, NM)), ("floor_tok", (NB, NM)), ("den", (2,)), ("m_ss", (NB * NM,)),
            ("m_var", (NB * NM,)), ("m_r", (NB * NM,))))
        yb, ya, yc = (yb_hi, yb_lo), (ya_hi, ya_lo), (yc_hi, yc_lo)
        ROT, DUP0, DUP1, DROT0, DROT1 = range(5)
        G_NORM, G_CONV, G_HEAD = 0, 6 * KD, 6 * KD + 3 * KB

        acc = ctx.enter_context(nc.psum_tensor("acc", [P, 4, 512], F32))
        aux = ctx.enter_context(nc.psum_tensor("aux", [P, 2, 1024], F32))

        def acc_halves(slot):
            return acc[:, 2 * slot:2 * slot + 2, 0:TH]

        def halves(t):
            return t.rearrange("p (a t) -> p a t", a=HALF)

        def aux_halves(slot):
            return aux[:, slot, :].rearrange("p (a t) -> p a t", a=HALF)[:, :, 0:TH]

        const_landed = sem("const_landed")
        arrived = sem("arrived")
        layer_go = sem("layer_go")
        loads_resumed = sem("loads_resumed")
        io_in = sem("io_in")
        io_turned = sem("io_turned")
        io_placed = sem("io_placed")
        io_first = sem("io_first")
        out_stored = [sem("out_stored0"), sem("out_stored1")]
        raw_landed = [sem("raw_landed0"), sem("raw_landed1")]
        whi_ready = sem("whi_ready")
        wlo_ready = sem("wlo_ready")
        acc_done = sem("acc_done")
        part_done = sem("part_done")
        acc_free = [sem("acc_free0"), sem("acc_free1")]
        aux_done = sem("aux_done")
        aux_free = [sem("aux_free0"), sem("aux_free1")]
        cur_ready = sem("cur_ready")
        h_ready = sem("h_ready")
        sq_ready = sem("sq_ready")
        sq_added = sem("sq_added")
        log_ready = sem("log_ready")
        seed_ready = sem("seed_ready")
        newton = sem("newton")
        rstd_ready = sem("rstd_ready")
        xf_ready = sem("xf_ready")
        xhi_ready = sem("xhi_ready")
        xlo_ready = sem("xlo_ready")
        silu_ready = sem("silu_ready")
        act_ready = sem("act_ready")
        xnhi_ready = sem("xnhi_ready")
        xnlo_ready = sem("xnlo_ready")
        wi_scaled = sem("wi_scaled")
        ahi_ready = sem("ahi_ready")
        alo_ready = sem("alo_ready")
        ysum = sem("ysum")
        ysq_ready = sem("ysq_ready")
        res_ready = sem("res_ready")
        rope_landed = sem("rope_landed")
        rope_step = sem("rope_step")
        rope_done = sem("rope_done")
        wi_ready = sem("wi_ready")
        rel_ready = sem("rel_ready")
        index_step = sem("index_step")
        mask_ready = sem("mask_ready")
        topk_step = sem("topk_step")
        negmax_ready = sem("negmax_ready")
        p_ready = sem("p_ready")
        p_turned = sem("p_turned")
        pt_copied = sem("pt_copied")
        pv_done = sem("pv_done")
        inv_ready = sem("inv_ready")
        o_read = sem("o_read")
        ybhi_ready = sem("ybhi_ready")
        gate_step = sem("gate_step")
        gate_rows = sem("gate_rows")
        gates_ready = sem("gates_ready")
        sel_landed = sem("sel_landed")
        cols_ready = sem("cols_ready")
        stab_ready = sem("stab_ready")
        arg_ready = sem("arg_ready")
        decay_ready = sem("decay_ready")
        wt_step = sem("wt_step")
        wt_ready = sem("wt_ready")
        num_done = sem("num_done")
        den_abs = sem("den_abs")
        den_step = sem("den_step")
        num_read = sem("num_read")
        mh_squared = sem("mh_squared")
        mh_step = sem("mh_step")
        mh_act = sem("mh_act")
        mh_normed = sem("mh_normed")
        conv_step = sem("conv_step")
        brhi_ready = sem("brhi_ready")
        brlo_ready = sem("brlo_ready")
        merge_step = sem("merge_step")
        mf_ready = sem("mf_ready")
        mhi_ready = sem("mhi_ready")
        mlo_ready = sem("mlo_ready")
        PER_LAYER = [*raw_landed, whi_ready, wlo_ready, acc_done, part_done, *acc_free, aux_done, *aux_free,
                     cur_ready, h_ready, sq_ready, sq_added, silu_ready, act_ready, io_turned, io_placed, log_ready, seed_ready, newton,
                     rstd_ready, xf_ready, xhi_ready, xlo_ready, xnhi_ready, xnlo_ready, wi_scaled, ahi_ready, alo_ready, ysum,
                     ysq_ready, res_ready, rope_landed, rope_step, rope_done, wi_ready, rel_ready,
                     index_step, mask_ready, topk_step, negmax_ready, p_ready, p_turned, pt_copied,
                     pv_done, inv_ready, o_read, ybhi_ready, gate_step, gate_rows, gates_ready, sel_landed,
                     cols_ready, stab_ready, arg_ready, decay_ready, wt_step, wt_ready, num_done, den_abs,
                     den_step, num_read, mh_squared, mh_step, mh_act, mh_normed, conv_step,
                     brhi_ready, brlo_ready, merge_step, mf_ready, mhi_ready, mlo_ready]
        ENGINES = 5

        class Steps:

            def __init__(self, eng, semaphore):
                self.eng, self.sem, self.n = eng, semaphore, 0

            def did(self, ins):
                ins.then_inc(self.sem, 1)
                self.n += 1

            def settle(self):
                self.eng.wait_ge(self.sem, self.n)

        def end_of_layer(eng, layer):
            eng.drain().then_inc(arrived, 1)
            eng.wait_ge(layer_go, layer + 1)

        def take_acc(eng, n):
            eng.wait_ge(acc_done, 1 + n + 1)

        def take_aux(eng, key):
            eng.wait_ge(aux_done, AUX[key] + 1)

        def aux_of(key):
            return AUX[key] % 2

        def free_aux(eng, key):
            eng.wait_ge(aux_free[aux_of(key)], AUX[key] // 2 + 2)

        gu_v = w_ffn_gu.rearrange("l f (k p) c -> l f p k c", p=P)
        down_v = w_ffn_down.rearrange("l f (k p) c -> l f p k c", p=P)
        in_v = w_in.rearrange("l (k p) c -> l p k c", p=P)
        branch_v = w_branch.rearrange("l b (k p) c -> l p (b k) c", p=P)
        out_v = w_out.rearrange("l (k p) c -> l p k c", p=P)

        block = ctx.enter_context(nc.Block())

        @block.sync
        def _(sp):
            for dst, src in ((ident, mats[0]), (ones, mats[1]), (causal_bias, mats[2]), (causal_keep, mats[3])):
                sp.dma_start(dst[:, :], src).then_inc(const_landed, 16)
            rows = 0
            for src in (norm_g.rearrange("l s (c p) -> (l s c) p", p=P),
                        w_conv.rearrange("l j (c p) -> (l j c) p", p=P),
                        mh_norm_g.rearrange("l (c p) -> (l c) p", p=P)):
                n = src.shape[0]
                sp.dma_start(tmp[rows:rows + n, 5, 0:P], src).then_inc(const_landed, 16)
                rows += n
            assert rows == P
            sp.dma_start(gate_bias[:, 0, :], b_igate.rearrange("l m -> m l"),
                         allow_slow_non_contiguous=True).then_inc(const_landed, 16)
            sp.dma_start(gate_bias[:, 1, :], b_fgate.rearrange("l m -> m l"),
                         allow_slow_non_contiguous=True).then_inc(const_landed, 16)
            rows_v = w_raw[:, :, :, :, :].rearrange("p s c k j -> p s (c k j)")
            sp.dma_start(tmp[0:META, 0:2, 0:512], meta.rearrange("t (a f) -> t a f", a=2)).then_inc(io_in, 16)
            for i in range(SEQ // P):
                if i >= 2:
                    sp.wait_ge(io_turned, 2 * (i - 1) + 2)
                sp.dma_start(rows_v[:, i % 2, 0:D], x[0, i * P:(i + 1) * P, :]).then_inc(raw_landed[i % 2], 16)
            sp.drain().then_inc(arrived, 1)
            sp.wait_ge(layer_go, 1)

            def load(u, parts, slot):
                sp.wait_ge(wlo_ready, 2 * u + 2)
                for dst, src in parts:
                    sp.dma_start(dst, src).then_inc(raw_landed[slot], 16)

            def chunk_pair(slot, srcs, kn):
                return [(w_raw[:, slot, c, 0:kn, :], s) for c, s in enumerate(srcs)]

            def load_ffn(f, layer):
                with sp.Fori(0, UP_UNITS // 2) as i:
                    for s in range(2):
                        col = sp.snap((2 * i + s) * P)
                        col2 = sp.snap((2 * i + s) * P + FF)
                        load(U_FFN[f] + 2 * i + s,
                             chunk_pair(s, [gu_v[layer, f, :, :, bass.ds(col, P)],
                                            gu_v[layer, f, :, :, bass.ds(col2, P)]], KD), s)
                with sp.Fori(0, KD // 4) as i:
                    for q in range(6):
                        kg = q % 3
                        rows = slice(kg * KD, kg * KD + DOWN_K[kg])
                        cols = [sp.snap((4 * i + 2 * (q // 3) + c) * P) for c in range(2)]
                        load(U_FFN[f] + UP_UNITS + 6 * i + q,
                             chunk_pair(q % 2, [down_v[layer, f, :, rows, bass.ds(c, P)] for c in cols],
                                        DOWN_K[kg]), q % 2)

            with sp.Fori(0, DEPTH) as layer:
                load_ffn(0, layer)
                for j, (kind, c0, c1) in enumerate(MIX):
                    u = U_MIX + j
                    load(u, chunk_pair(u % 2, [in_v[layer, :, :, c0:c0 + P], in_v[layer, :, :, c1:c1 + P]], KD), u % 2)
                    if j == 1:
                        sp.wait_ge(acc_done, 1 + A_MIX)
                        sp.dma_start(cos_sin[:, :, :], rope_tab.rearrange("a p t -> p a t")).then_inc(rope_landed, 16)
                        sp.dma_start(rope_mats[:, :, :], mats[4:9].rearrange("m p c -> p m c")).then_inc(rope_landed, 16)
                with sp.Fori(0, KD // 2) as i:
                    for s in range(2):
                        u = U_MERGE + 3 * s
                        cols = [sp.snap(C_GT + (2 * i + s) * P + b * D) for b in range(3)]
                        m = sp.snap((2 * i + s) * P)
                        load(u + 6 * i, chunk_pair(u % 2, [in_v[layer, :, :, bass.ds(c, P)] for c in cols[:2]], KD), u % 2)
                        load(u + 1 + 6 * i, chunk_pair((u + 1) % 2, [in_v[layer, :, :, bass.ds(cols[2], P)],
                                                                     branch_v[layer, :, 0:KD, bass.ds(m, P)]], KD), (u + 1) % 2)
                        load(u + 2 + 6 * i, [(w_raw[:, u % 2, 0, 2 * a:2 * a + 2, :],
                                              branch_v[layer, :, KD + 2 * a:KD + 2 * a + 2, bass.ds(m, P)]) for a in range(2)], u % 2)
                for j in range(OUT_UNITS):
                    u = U_OUT + j
                    load(u, chunk_pair(u % 2, [out_v[layer, :, :, (2 * j + c) * P:(2 * j + c + 1) * P] for c in range(2)], KD), u % 2)
                load_ffn(1, layer)
                end_of_layer(sp, layer + 1)
                sp.sem_inc(loads_resumed, 1)

            for i in range(SEQ // P):
                sp.wait_ge(io_placed, 2 * (i + 1))
                sp.dma_start(out[0, i * P:(i + 1) * P, :], rows_v[:, i % 2, 0:D]).then_inc(out_stored[i % 2], 16)
            for s in out_stored:
                sp.wait_ge(s, 16 * (SEQ // P // 2))

        def split_part(t, slot, kind, part):
            if kind == "full":
                return t[:, slot, part, :, :]
            if kind == "last_k":
                return t[:, slot, part, 0:DOWN_K[2], :]
            return t[:, slot, 0, 2 * part:2 * part + 2, :]

        def split_wait(u, part=1):
            return 2 * u + part + 5

        @block.gpsimd
        def _(pool):
            def clear_counts():
                pool.wait_ge(arrived, ENGINES - 1)
                pool.drain()
                for s in PER_LAYER:
                    pool.sem_clear(s)
                pool.sem_clear(arrived)
                for s in (*acc_free, *aux_free, acc_done, alo_ready, mlo_ready):
                    pool.sem_inc(s, 1)
                pool.sem_inc(wlo_ready, 4)
                pool.sem_inc(layer_go, 1)

            def w_rest(u, slot, kind="full"):
                for part in range(2):
                    pool.wait_ge(whi_ready, 2 * u + part + 1)
                    nc.gpsimd.tensor_tensor(split_part(w_lo, slot, kind, part), split_part(w_raw, slot, kind, part),
                                            split_part(w_hi, slot, kind, part).bitcast(F32), ALU.subtract)\
                        .then_inc(wlo_ready, 1)

            def add_results(p):
                for k in range(KD):
                    pool.wait_ge(res_ready, KD * p + k + 1)
                    nc.gpsimd.tensor_tensor(h[:, k, :], h[:, k, :], tmp[:, 2 + k % 2, :], ALU.add).then_inc(h_ready, 1)

            def br_rest(g, dst):
                pool.wait_ge(brhi_ready, g + 1)
                src = tmp[:, 4 + g % 2, :] if g < KB else ya_f[g - KB][:, :]
                nc.gpsimd.tensor_tensor(dst[1][:, g % KB, :], src, dst[0][:, g % KB, :].bitcast(F32),
                                        ALU.subtract).then_inc(brlo_ready, 1)

            def ffn(f):
                u0 = U_FFN[f]
                with pool.Fori(0, UP_UNITS // 2) as i:
                    for s in range(2):
                        w_rest(u0 + 2 * i + s + 1, (s + 1) % 2)
                        n = f * KF + 2 * i + s
                        pool.wait_ge(ahi_ready, n + 1)
                        nc.gpsimd.tensor_tensor(a_lo[:, bass.ds(2 * i + s, 1), :], tmp[:, 2 + s:3 + s, :],
                                                a_hi[:, bass.ds(2 * i + s, 1), :].bitcast(F32), ALU.subtract)\
                            .then_inc(alo_ready, 1)
                last = f == 1
                for q in range(DOWN_UNITS - last):
                    w_rest(u0 + UP_UNITS + q + 1, (q + 1) % 2, "last_k" if q % 3 == 1 else "full")

            clear_counts()
            with pool.Fori(0, DEPTH) as layer:
                w_rest(0, 0)
                ffn(0)
                add_results(0)
                for j in range(N_MIX):
                    w_rest(U_MIX + j + 1, (U_MIX + j + 1) % 2)
                for g in range(2 * KB):
                    br_rest(g, yc if g < KB else ya)
                with pool.Fori(0, KD // 2) as i:
                    for s in range(2):
                        for r in range(3):
                            u = U_MERGE + 3 * s + r
                            w_rest(u + 1 + 6 * i, (u + 1) % 2, "branch2" if r == 1 else "full")
                        m = bass.ds(2 * i + s, 1)
                        pool.wait_ge(mhi_ready, 2 * i + s + 1)
                        nc.gpsimd.tensor_tensor(mg_lo[:, m, :], tmp[:, 3 * s:3 * s + 1, :],
                                                mg_hi[:, m, :].bitcast(F32), ALU.subtract).then_inc(mlo_ready, 1)
                for j in range(OUT_UNITS):
                    w_rest(U_OUT + j + 1, (U_OUT + j + 1) % 2)
                add_results(1)
                ffn(1)
                add_results(2)
                clear_counts()

        @block.scalar
        def _(act):
            A = nc.scalar.activation

            def w_round(u, slot, kind="full"):
                act.wait_ge(raw_landed[slot], 32 * (u // 2 + 1) if isinstance(u, int) else u)
                for part in range(2):
                    A(split_part(w_hi, slot, kind, part), split_part(w_raw, slot, kind, part), ACT.Copy).then_inc(whi_ready, 1)

            def w_round_loop(u0, i, per, slot, kind="full", parts=(0, 1)):
                act.wait_ge(raw_landed[slot], 32 * (u0 // 2 + 1) + 16 * per * i)
                for part in parts:
                    A(split_part(w_hi, slot, kind, part), split_part(w_raw, slot, kind, part), ACT.Copy).then_inc(whi_ready, 1)

            def gain_of(p, k):
                return cur[:, G_NORM + 2 * p * KD + k:G_NORM + 2 * p * KD + k + 1]

            def square_h(p, hi):
                act.wait_ge(cur_ready, 8)
                for k in range(KD):
                    if p > 0:
                        act.wait_ge(h_ready, KD * (p - 1) + k + 1)
                    A(hi[:, k, :], h[:, k, :], ACT.Copy, scale=gain_of(p, k)).then_inc(xhi_ready, 1)
                    if k >= 3:
                        act.wait_ge(sq_added, (KD - 1) * p + k - 2)
                    A(tmp[:, k % 2 if k else 4, :], h[:, k, :], ACT.Square).then_inc(sq_ready, 1)

            def rstd_seed(q):
                free_aux(act, ("norm", q))
                A(tmp[:, 3, :], tmp[:, 2, :], ACT.Ln).then_inc(log_ready, 1)
                act.wait_ge(log_ready, q + 1)
                A(tmp[:, 3, :], tmp[:, 3, :], ACT.Exp, scale=-0.5).then_inc(seed_ready, 1)

            def round_x():
                for k in range(KD):
                    act.wait_ge(xf_ready, k + 1)
                    A(x_hi[:, k, :], tmp[:, k % 2, :], ACT.Copy).then_inc(xnhi_ready, 1)

            def ffn(f):
                u0, n0 = U_FFN[f], A_FFN[f]
                nc.scalar.preload_act_table(ACT.Silu)
                with act.Fori(0, UP_UNITS // 2) as i:
                    for s in range(2):
                        nn = n0 + 2 * s
                        act.wait_ge(acc_free[SLOT[nn]], USE[nn] + 2 * i + 2)
                        A(tmp[:, s, :], tmp[:, s, :], ACT.Silu).then_inc(silu_ready, 1)
                        act.wait_ge(acc_done, 1 + nn + 4 * i + 2)
                        w_round_loop(u0 + s + 2, i, 2, s)
                        act.wait_ge(act_ready, f * KF + 2 * i + s + 1)
                        A(a_hi[:, bass.ds(2 * i + s, 1), :], tmp[:, 2 + s:3 + s, :], ACT.Copy).then_inc(ahi_ready, 1)
                n1 = n0 + 2 * UP_UNITS

                def down_unit(i, q, skip=False):
                    if q == 0:
                        act.wait_ge(acc_done, 1 + n1 + 4 * i)
                        skip = skip or i == 0
                    elif q == 3:
                        act.wait_ge(acc_done, 1 + n1 + 2 + 4 * i)
                    else:
                        act.wait_ge(part_done, f * KD + 4 * i + {1: 1, 2: 2, 4: 3, 5: 4}[q])
                    if not skip:
                        w_round_loop(u0 + UP_UNITS + q + 1, i, 6, (q + 1) % 2, "last_k" if q % 3 == 1 else "full")
                    if q % 3 == 2:
                        for c in range(2):
                            j = 2 * (q // 3) + c
                            slot = SLOT[n1 + j]
                            act.wait_ge(acc_done, 1 + n1 + j + 4 * i + 1)
                            A(y[:, bass.ds(4 * i + j, 1), :].rearrange("p o (a t) -> p (o a) t", a=HALF),
                              acc_halves(slot), ACT.Copy).then_inc(acc_free[slot], 1)

                for i in range(KD // 4):
                    for q in range(6):
                        down_unit(i, q, skip=(f == 1 and i == KD // 4 - 1 and q == 5))
                nc.scalar.preload_act_table_set(LN_EXP_SET)
                rstd_seed(1 + 4 * f)
                if f == 0:
                    mixer_weights(0)

            def evac(n, dst, func=ACT.Copy, **kw):
                act.wait_ge(acc_done, 1 + n + 1)
                A(halves(dst), acc_halves(SLOT[n]), func, **kw).then_inc(acc_free[SLOT[n]], 1)

            def evac_tokens(n, pair, dst):
                act.wait_ge(acc_done, 1 + n + 1)
                for a, b in enumerate(pair):
                    rows = BL[b][1]
                    src, d = dst(b, acc[0:rows, 2 * SLOT[n] + a, :])
                    ins = A(d, src, ACT.Copy)
                ins.then_inc(acc_free[SLOT[n]], 1)

            def mixer_weights(j):
                act.wait_ge(acc_done, 1 + A_UNIT[j])
                w_round(U_MIX + j + 1, (U_MIX + j + 1) % 2)

            def mixer_unit(j):
                mixer_weights(j)
                mixer_out(j)

            def mixer_out(j):
                kind, c0, _ = MIX[j]
                n = A_UNIT[j]
                if kind == "qi":
                    for c in range(2):
                        evac(n + c, qi_t[:, c, :])
                elif kind == "k":
                    evac(n, tmp[:, 4, :])
                    act.wait_ge(rstd_ready, 3)
                    evac(n + 1, tmp[:, 3, :])
                elif kind == "q":
                    for c in range(2):
                        evac(n + c, q_t[:, (c0 - C_Q) // P + c, :])
                elif kind in ("v", "mv"):
                    for a, pair in enumerate(((0, 1), (2, 3), (4,))):
                        if kind == "v":
                            evac_tokens(n + a, pair, lambda b, s: (s[:, 0:P], v_tok[0:BL[b][1], b, :]))
                        else:
                            m0 = (c0 - C_MV) // P
                            evac_tokens(n + a, pair, lambda b, s: (
                                s[:, 0:2 * P].rearrange("p (m c) -> p m c", m=2),
                                mv_tok[0:BL[b][1], b, m0:m0 + 2, 0:P]))
                elif kind == "if":
                    for c in range(2):
                        act.wait_ge(acc_done, 1 + n + c + 1)
                        slot = SLOT[n + c]
                        A(tmp[0:NM, 4 + c, :].rearrange("p (a t) -> p a t", a=HALF),
                          acc[0:NM, 2 * slot:2 * slot + 2, 0:TH], ACT.Identity,
                          bias=gate_bias_cur[:, c:c + 1]).then_inc(acc_free[slot], 1)
                elif kind == "mq":
                    for c in range(2):
                        evac(n + c, mq_t[:, (c0 - C_MQ) // P + c, :])
                elif kind == "mk":
                    for c in range(2):
                        evac(n + c, mk_t[:, (c0 - C_MK) // P + c, :], scale=float(P) ** -0.5)

            def filled(g):
                j, c, k = FIRST_FILL + g // (2 * KD), g // KD % 2, g % KD
                kind, c0, _ = MIX[j]
                n = A_UNIT[j] + c
                if c == 0 and k == 0:
                    act.wait_ge(acc_done, 1 + n)
                    w_round(U_MIX + j + 1, (U_MIX + j + 1) % 2)
                if k == KD - 1 and kind == "mo":
                    evac(n, mo_t[:, (c0 - C_MO) // P + c, :], ACT.Tanh, scale=0.5)
                elif k == KD - 1 and kind == "cxc" and c == 0:
                    if j > FIRST_CONV:
                        act.wait_ge(acc_free[0], USE[n])
                    evac(n, cx_t[:, :])

            def index_rel(b, i):
                g = NIDX * (b - 1) + i
                n = BL[b][1]
                key = ("index", b, i)
                act.wait_ge(aux_done, AUX[key] + 1)
                if g == 0:
                    act.wait_ge(rope_done, 2)
                if g >= 2:
                    act.wait_ge(index_step, g - 1)
                A(tmp[0:n, g % 2, 0:KL[b]], aux[0:n, aux_of(key), 0:KL[b]], ACT.Relu, scale=float(DH) ** -0.5)\
                    .then_inc(aux_free[aux_of(key)], 1)

            def attention():
                g = Steps(act, gate_step)
                act.wait_ge(index_step, NIDX * (NB - 1))
                n = A_UNIT[5]
                for c in range(2):
                    act.wait_ge(acc_free[SLOT[n + c]], USE[n + c] + 2)
                g.did(A(tmp[0:NM, 0, :], tmp[0:NM, 5, :], ACT.Abs))
                g.settle()
                g.did(A(tmp[0:NM, 0, :], tmp[0:NM, 0, :], ACT.Exp, scale=-1.0))
                g.settle()
                g.did(A(tmp[0:NM, 0, :], tmp[0:NM, 0, :], ACT.Ln, bias=1.0))
                act.dma_start(sel_sb[:, :, :], sel).then_inc(sel_landed, 16)
                nc.scalar.preload_act_table_set(TANH_SET)
                for t in range(NA + O_LAG):
                    if 1 <= t <= NA:
                        for f in att_fills(t - 1):
                            filled(f)
                    if t < NA:
                        b, hd = divmod(t, NH)
                        n = BL[b][1]
                        act.wait_ge(negmax_ready, t + 1)
                        A(prob[0:n, t % 2, 0:KL[b]], prob[0:n, t % 2, 0:KL[b]], ACT.Exp, bias=neg_max[0:n, t % 2:t % 2 + 1],
                          accum_out=row_sum[0:n, b % 2, hd:hd + 1]).then_inc(p_ready, 1)
                    if 1 <= t <= NA:
                        s = t - 1
                        b = s // NH
                        n = BL[b][1]
                        act.wait_ge(p_turned, s + 1)
                        if s >= 2:
                            act.wait_ge(pv_done, s - 1)
                        ins = A(prob_t[:, s % 2, 0:n], acc[:, 2, 0:n], ACT.Copy)
                        if b:
                            ins = A(prob_t[0:QB, s % 2, n:n * (b + 1)], acc[0:QB, 2, n:n * (b + 1)], ACT.Copy)
                        ins.then_inc(pt_copied, 1)
                    if t >= NH - 1 + O_LAG and (t - O_LAG) % NH == NH - 1:
                        b = (t - O_LAG) // NH
                        t0, n = BL[b]
                        take_aux(act, ("turn", b))
                        A(yb_hi[:, :, t0:t0 + n],
                          aux[:, aux_of(("turn", b)), 0:KB * n].rearrange("p (j t) -> p j t", j=KB),
                          ACT.Copy).then_inc(ybhi_ready, 1)
                    if t == GATE_STEP:
                        take_aux(act, ("gate_cols",))
                        s = aux_of(("gate_cols",))
                        for which, dst, func in ((0, c_tok, ACT.Copy), (1, floor_tok, ACT.Exp)):
                            v = aux[:, s, NB * NM * which:NB * NM * (which + 1)].rearrange("p (b m) -> p b m", m=NM)
                            A(dst[:, 0, :], v[:, 0, :], func)
                            ins = A(dst[0:QB, 1:NB, :], v[0:QB, 1:NB, :], func)
                        ins.then_inc(aux_free[s], 1)

            def mlstm():
                def square(m, b):
                    i = NB * m + b
                    n = BL[b][1]
                    act.wait_ge(num_read, i + 1)
                    if i >= 1:
                        act.wait_ge(mh_squared, i)
                    A(tmp[0:n, 0, 0:P], m_h[0:n, b, m, :], ACT.Square,
                      accum_out=m_ss[0:n, NM * b + m:NM * b + m + 1]).then_inc(mh_squared, 1)

                for step in range(NB * (NM + 1)):
                    m, c = divmod(step, NB)
                    if m < NM:
                        key = ("stab", m)
                        if c == 0:
                            take_aux(act, key)
                            if m >= 2:
                                act.wait_ge(arg_ready, NB * (m - 1))
                            A(tmp[:, 1 + m % 2, :], aux[:, aux_of(key), 0:T], ACT.Copy).then_inc(aux_free[aux_of(key)], 1)
                        k0, nk = BL[c]
                        act.wait_ge(arg_ready, step + 1)
                        A(tmp[0:nk, 3 + step % 2, k0:T], tmp[0:nk, 3 + step % 2, k0:T], ACT.Exp).then_inc(decay_ready, 1)
                    i = step - NB
                    if i >= 0:
                        n = BL[c][1]
                        act.wait_ge(num_done, i + 1)
                        if i >= 2:
                            act.wait_ge(num_read, i - 1)
                        A(den[0:n, i % 2:i % 2 + 1], acc[0:n, 2 + i % 2, P:P + 1], ACT.Abs).then_inc(den_abs, 1)
                    for f in ml_fills(step):
                        filled(f)
                    if i >= 1:
                        square(*divmod(i - 1, NB))
                square(NM - 1, NB - 1)
                nc.scalar.preload_act_table_set(LN_EXP_SET)
                act.wait_ge(mh_step, 1)
                A(m_r[:, :], m_var[:, :], ACT.Ln).then_inc(mh_act, 1)
                act.wait_ge(mh_act, 1)
                A(m_r[:, :], m_r[:, :], ACT.Exp, scale=-0.5).then_inc(mh_act, 1)
                nc.scalar.preload_act_table_set(TANH_SET)
                for m in range(KB):
                    free_aux(act, ("hturn", m))
                    A(yc_hi[:, m, :], tmp[:, 4 + m % 2, :], ACT.Copy).then_inc(brhi_ready, 1)
                act.wait_ge(acc_free[0], USE[A_MERGE - 1] + 2)
                for c in range(KB):
                    A(ya_hi[:, c, :], ya_f[c][:, :], ACT.Copy).then_inc(brhi_ready, 1)

            for i in range(SEQ // P):
                for j in range(2):
                    e = 2 * i + j
                    act.wait_ge(io_turned, 2 + e + 1)
                    A(h[:, 4 * j:4 * j + 4, META + i * P:META + (i + 1) * P],
                      acc[:, e % 4, :].rearrange("p (k t) -> p k t", k=4), ACT.Copy).then_inc(io_placed, 1)
            act.drain().then_inc(arrived, 1)
            act.wait_ge(layer_go, 1)

            with act.Fori(0, DEPTH) as layer:
                nc.scalar.preload_act_table_set(LN_EXP_SET)
                w_round(0, 0)
                w_round(1, 1)
                square_h(0, x_hi)
                rstd_seed(0)
                ffn(0)
                square_h(1, xu_hi)
                rstd_seed(2)
                mixer_out(0)
                mixer_weights(1)
                round_x()
                mixer_out(1)
                for j in range(2, 5):
                    mixer_unit(j)
                take_aux(act, ("wi",))
                s = aux_of(("wi",))
                A(wi_tok[0:QB, 1:NB, :], aux[0:QB, s, 0:(NB - 1) * P].rearrange("p (b c) -> p b c", b=NB - 1)[:, :, DH:DH + NIDX],
                  ACT.Copy, scale=float(NIDX) ** -0.5).then_inc(aux_free[s], 1)
                for b in range(1, NB):
                    for i in range(NIDX):
                        index_rel(b, i)
                    for j in UNITS_AFTER[b]:
                        mixer_unit(j)
                attention()
                mlstm()
                with act.Fori(0, KD // 2) as i:
                    for s in range(2):
                        nn = A_MERGE + 6 * s
                        for r in range(3):
                            u = U_MERGE + 3 * s + r
                            act.wait_ge(acc_done, 1 + nn + (0, 2, 5)[r] + 12 * i)
                            w_round_loop(u + 1, i, 6, (u + 1) % 2, "branch2" if r == 1 else "full",
                                         (1,) if r == 2 else (0, 1))
                            for c in ((0, 1), (0,), ())[r]:
                                g = 2 * r + c
                                act.wait_ge(acc_done, 1 + nn + g + 12 * i + 1)
                                act.wait_ge(mlo_ready, 1 + 2 * i + s)
                                A(halves(tmp[:, 3 * s + g, :]), acc_halves(SLOT[nn + g]), ACT.Tanh, scale=0.5)\
                                    .then_inc(acc_free[SLOT[nn + g]], 1)
                            if r == 1:
                                w_round_loop(u + 2, i, 6, u % 2, parts=(0,))
                        act.wait_ge(mf_ready, 2 * i + s + 1)
                        A(mg_hi[:, bass.ds(2 * i + s, 1), :], tmp[:, 3 * s:3 * s + 1, :], ACT.Copy).then_inc(mhi_ready, 1)
                for j in range(OUT_UNITS):
                    n = A_OUT + 2 * j
                    act.wait_ge(acc_done, 1 + n)
                    w_round(U_OUT + j + 1, (U_OUT + j + 1) % 2)
                    for c in range(2):
                        act.wait_ge(acc_done, 1 + n + c + 1)
                        A(halves(y[:, 2 * j + c, :]), acc_halves(SLOT[n + c]), ACT.Copy).then_inc(acc_free[SLOT[n + c]], 1)
                nc.scalar.preload_act_table_set(LN_EXP_SET)
                rstd_seed(3)
                act.wait_ge(acc_done, 1 + A_FFN[1])
                w_round(U_FFN[1] + 1, 1)
                square_h(2, x_hi)
                rstd_seed(4)
                ffn(1)
                end_of_layer(act, layer + 1)

        @block.vector
        def _(dve):
            V = nc.vector

            def variance(q, scale):
                take_aux(dve, ("norm", q))
                s = aux_of(("norm", q))
                V.tensor_scalar(halves(tmp[:, 2, :]), aux_halves(s), scale, EPS, ALU.mult, ALU.add).then_inc(aux_free[s], 1)

            def rstd(q):
                dve.wait_ge(seed_ready, q + 1)
                V.tensor_tensor(tmp[:, 2, :], tmp[:, 2, :], tmp[:, 3, :], ALU.mult).then_inc(newton, 1)
                dve.wait_ge(newton, 2 * q + 1)
                V.scalar_tensor_tensor(tmp[:, 2, :], tmp[:, 2, :], -0.5, tmp[:, 3, :], ALU.mult, ALU.mult).then_inc(newton, 1)
                dve.wait_ge(newton, 2 * q + 2)
                V.scalar_tensor_tensor(tmp[:, 5, :], tmp[:, 2, :], 1.5, tmp[:, 3, :], ALU.add, ALU.mult).then_inc(rstd_ready, 1)
                dve.wait_ge(rstd_ready, q + 1)

            def gain_of(s, k):
                return cur[:, G_NORM + s * KD + k:G_NORM + s * KD + k + 1]

            def result(p, k):
                if k >= 2:
                    dve.wait_ge(h_ready, KD * p + k - 1)
                V.scalar_tensor_tensor(tmp[:, 2 + k % 2, :], y[:, k, :], gain_of(2 * p + 1, k), tmp[:, 5, :],
                                       ALU.mult, ALU.mult).then_inc(res_ready, 1)

            def add_squares(p, k):
                dve.wait_ge(sq_ready, KD * p + k + 1)
                if k >= 2:
                    dve.wait_ge(sq_added, (KD - 1) * p + k - 1)
                V.tensor_tensor(tmp[:, 4, :], tmp[:, 4, :], tmp[:, k % 2, :], ALU.add).then_inc(sq_added, 1)

            def norm_out(p, scale, p_in):
                if p is not None:
                    variance(2 * p + 1, scale)
                    rstd(2 * p + 1)
                for k in range(KD + 2):
                    if p is not None and k < KD:
                        result(p, k)
                    if p_in is not None and 3 <= k:
                        add_squares(p_in, k - 2)

            def norm_in_late(p, hi, lo):
                variance(2 * p, 1.0 / D)
                for k in range(KD):
                    dve.wait_ge(xhi_ready, KD * p + k + 1)
                    V.scalar_tensor_tensor(lo[:, k, :], h[:, k, :], gain_of(2 * p, k), hi[:, k, :].bitcast(F32),
                                           ALU.mult, ALU.subtract).then_inc(xlo_ready, 1)
                rstd(2 * p)

            def norm_in(p):
                for k in range(KD + 1):
                    if k < KD:
                        if k >= 2:
                            dve.wait_ge(xnlo_ready, k - 1)
                        V.scalar_tensor_tensor(tmp[:, k % 2, :], h[:, k, :], gain_of(2 * p, k), tmp[:, 5, :],
                                               ALU.mult, ALU.mult).then_inc(xf_ready, 1)
                    if k >= 1:
                        dve.wait_ge(xnhi_ready, k)
                        V.tensor_tensor(x_lo[:, k - 1, :], tmp[:, (k - 1) % 2, :], x_hi[:, k - 1, :].bitcast(F32),
                                        ALU.subtract).then_inc(xnlo_ready, 1)

            def y_square(p, slot, free_count, m, count):
                dve.wait_ge(acc_free[slot], free_count)
                dve.wait_ge(ysum, (KD + 1) * p + 1 + count)
                V.tensor_tensor(tmp[:, 3:4, :], y[:, m, :], y[:, m, :], ALU.mult).then_inc(ysq_ready, 1)
                dve.wait_ge(ysq_ready, KD * p + 1 + count)
                V.tensor_tensor(tmp[:, 4:5, :], tmp[:, 4:5, :], tmp[:, 3:4, :], ALU.add).then_inc(ysum, 1)

            def ffn(f):
                n0 = A_FFN[f]
                with dve.Fori(0, UP_UNITS // 2) as i:
                    for s in range(2):
                        nn = n0 + 2 * s
                        g_slot, u_slot = SLOT[nn], SLOT[nn + 1]
                        dve.wait_ge(acc_done, 1 + nn + 4 * i + 1)
                        V.tensor_tensor(halves(tmp[:, s, :]), acc_halves(g_slot), halves(tmp[:, 5, :]), ALU.mult)\
                            .then_inc(acc_free[g_slot], 1)
                        dve.wait_ge(acc_done, 1 + nn + 4 * i + 2)
                        dve.wait_ge(alo_ready, 1 + f * KF + 2 * i + s)
                        V.tensor_tensor(halves(tmp[:, 2 + s, :]), acc_halves(u_slot), halves(tmp[:, 5, :]), ALU.mult)\
                            .then_inc(acc_free[u_slot], 1)
                        dve.wait_ge(acc_free[u_slot], USE[nn + 1] + 2 * i + 2)
                        dve.wait_ge(silu_ready, f * KF + 2 * i + s + 1)
                        V.tensor_tensor(tmp[:, 2 + s, :], tmp[:, 2 + s, :], tmp[:, s, :], ALU.mult).then_inc(act_ready, 1)
                p = 2 * f
                V.memset(tmp[:, 4, :], 0.0).then_inc(ysum, 1)
                n1 = n0 + 2 * UP_UNITS
                with dve.Fori(0, KD // 4) as i:
                    for j in range(4):
                        slot = SLOT[n1 + j]
                        y_square(p, slot, USE[n1 + j] + 2 * i + 2, bass.ds(4 * i + j, 1), j + 4 * i)
                norm_out(p, 1.0 / D, 1 if f == 0 else None)

            def rope_all():
                r = Steps(dve, rope_step)
                dve.wait_ge(rope_landed, 32)
                dve.wait_ge(xnlo_ready, KD)
                cos, sin = cos_sin[:, 0, :], cos_sin[:, 1, :]
                for table in (cos, sin):
                    r.did(V.tensor_tensor(table, table, tmp[:, 5, :], ALU.mult))
                r.settle()

                def rotated(i):
                    dst = qi_t[:, i, :] if i < 2 else q_t[:, i - 2, :]
                    key = ("rot", i)
                    take_aux(dve, key)
                    V.tensor_tensor(tmp[:, i % 2, :], aux[:, aux_of(key), 0:T], sin, ALU.mult).then_inc(aux_free[aux_of(key)], 1)
                    r.did(V.tensor_tensor(dst, dst, cos, ALU.mult))
                    r.settle()
                    dve.wait_ge(aux_free[aux_of(key)], AUX[key] // 2 + 2)
                    ins = V.tensor_tensor(dst, dst, tmp[:, i % 2, :], ALU.add)
                    if i == 1 + KB:
                        ins.then_inc(rope_done, 1)
                    else:
                        r.did(ins)
                        r.settle()

                rotated(0)
                rotated(1)
                for i in range(3):
                    dst = ki_t[:, :] if i == 0 else k_t[:, i - 1, :]
                    key, key2 = ("dup", i), ("dup_rot", i)
                    take_aux(dve, key)
                    V.tensor_tensor(dst, aux[:, aux_of(key), 0:T], cos, ALU.mult).then_inc(aux_free[aux_of(key)], 1)
                    take_aux(dve, key2)
                    V.tensor_tensor(tmp[:, i % 2, :], aux[:, aux_of(key2), 0:T], sin, ALU.mult).then_inc(aux_free[aux_of(key2)], 1)
                    for kk in (key, key2):
                        dve.wait_ge(aux_free[aux_of(kk)], AUX[kk] // 2 + 2)
                    if i == 0:
                        V.tensor_tensor(tmp[:, 3, :], tmp[:, 3, :], tmp[:, 5, :], ALU.mult).then_inc(wi_scaled, 1)
                    ins = V.tensor_tensor(dst, dst, tmp[:, i % 2, :], ALU.add)
                    if i < 2:
                        r.did(ins)
                        r.settle()
                ins.then_inc(rope_done, 1)
                dve.wait_ge(rope_done, 1)
                for i in range(2, 2 + KB):
                    rotated(i)
                dve.wait_ge(rope_done, 2)
                V.tensor_copy(mask[:, 0:P], causal_bias[:, :]).then_inc(mask_ready, 1)

            def select_keys(b, k):
                n, kl, t0 = BL[b][1], KL[b], BL[b][0]
                score, work = tmp[0:n, 2, 0:kl], tmp[0:n, 3, 0:kl]
                for i in range(NIDX):
                    g = NIDX * (b - 1) + i
                    key = ("index", b, i)
                    dve.wait_ge(aux_free[aux_of(key)], AUX[key] // 2 + 2)
                    if g == 0:
                        s = aux_of(("wi",))
                        dve.wait_ge(aux_free[s], AUX[("wi",)] // 2 + 2)
                    if i == 0:
                        V.tensor_scalar(score, tmp[0:n, g % 2, 0:kl], wi_tok[0:n, b, i:i + 1], None, ALU.mult).then_inc(index_step, 1)
                    else:
                        V.scalar_tensor_tensor(score, tmp[0:n, g % 2, 0:kl], wi_tok[0:n, b, i:i + 1], score,
                                               ALU.mult, ALU.add).then_inc(index_step, 1)
                    dve.wait_ge(index_step, g + 1)
                k.did(V.tensor_tensor(tmp[0:n, 2, t0:kl], tmp[0:n, 2, t0:kl], causal_bias[0:n, 0:n], ALU.add))
                k.settle()
                for i in range(TOPK // 8):
                    src = score if i == 0 else work
                    k.did(V.max(top8[0:n, :], src))
                    k.settle()
                    k.did(V.match_replace(work, top8[0:n, :], src, TAKEN))
                    k.settle()
                V.tensor_scalar(mask[0:n, MO[b]:MO[b] + kl], work, TAKEN / 2, NEG, ALU.is_gt, ALU.mult).then_inc(mask_ready, 1)

            GATE_OPS = 8

            def gate_op(g, i):
                row = lambda r: tmp[0:NM, r, :]
                if i == 0:
                    dve.wait_ge(gate_step, 3)
                    g.did(V.tensor_scalar(row(1), row(5), 0.0, None, ALU.min))
                elif i == 1:
                    g.did(V.tensor_tensor(row(1), row(1), row(0), ALU.subtract))
                elif i == 2:
                    g.did(V.memset(row(0), 1.0))
                elif i == 3:
                    g.did(V.tensor_tensor_scan(row(5), row(0), row(1), 0.0, ALU.mult, ALU.add))
                elif i == 4:
                    g.did(V.tensor_tensor(row(4), row(4), row(5), ALU.subtract))
                elif i == 5:
                    g.did(V.tensor_tensor_scan(row(1), row(4), row(4), 0.0, ALU.max, ALU.max))
                elif i == 6:
                    g.did(V.scalar_tensor_tensor(row(0), row(1), -1.0, row(5), ALU.mult, ALU.subtract))
                else:
                    V.tensor_scalar(row(5), row(1), -1.0, None, ALU.mult).then_inc(gates_ready, 1)
                if i < GATE_OPS - 1:
                    g.settle()

            def filled(g):
                j, c, k = FIRST_FILL + g // (2 * KD), g // KD % 2, g % KD
                if k < KD - 1 or j < FIRST_CONV:
                    return
                n = A_UNIT[j] + c
                pair, of_pair = divmod(j - FIRST_CONV, 3)
                if of_pair < 2 and c == 1:
                    y_c = 2 * pair + of_pair
                    tap = lambda i: cur[:, G_CONV + KB * i + y_c:G_CONV + KB * i + y_c + 1]
                    t = ya_f[y_c][:, :]
                    dve.wait_ge(acc_free[0], USE[n - 1] + 2)
                    dve.wait_ge(acc_done, 1 + n + 1)
                    V.tensor_tensor(halves(conv_u[:, 2:T + 2]), acc_halves(0), halves(cx_t[:, :]), ALU.mult)\
                        .then_inc(acc_free[0], 1)
                    dve.wait_ge(acc_free[0], USE[n] + 2)
                    taps.did(V.tensor_scalar(t, conv_u[:, 0:T], tap(0), None, ALU.mult))
                    taps.settle()
                    taps.did(V.scalar_tensor_tensor(t, conv_u[:, 1:T + 1], tap(1), t, ALU.mult, ALU.add))
                    taps.settle()
                    taps.did(V.scalar_tensor_tensor(t, conv_u[:, 2:T + 2], tap(2), t, ALU.mult, ALU.add))
                    taps.settle()
                elif of_pair == 2:
                    t = ya_f[2 * pair + c][:, :]
                    dve.wait_ge(acc_done, 1 + n + 1)
                    V.tensor_tensor(halves(t), acc_halves(0), halves(t), ALU.mult).then_inc(acc_free[0], 1)

            def attention():
                def finish(b):
                    n = BL[b][1]
                    dve.wait_ge(pv_done, NH * (b + 1))
                    if b:
                        dve.wait_ge(o_read, b)
                    V.reciprocal(row_inv[0:n, :], row_sum[0:n, b % 2, :]).then_inc(inv_ready, 1)
                    dve.wait_ge(inv_ready, b + 1)
                    V.tensor_tensor(tmp[0:n, 2 + b % 2, 0:BW].rearrange("p (h d) -> p h d", h=NH),
                                    acc[0:n, 3, :].rearrange("p (h d) -> p h d", h=NH),
                                    row_inv[0:n, :].unsqueeze(2).to_broadcast([n, NH, DH]), ALU.mult).then_inc(o_read, 1)

                def turned(b):
                    t0, n = BL[b]
                    s = aux_of(("turn", b))
                    dve.wait_ge(ybhi_ready, b + 1)
                    V.tensor_tensor(yb_lo[:, :, t0:t0 + n], aux[:, s, 0:KB * n].rearrange("p (j t) -> p j t", j=KB),
                                    yb_hi[:, :, t0:t0 + n].bitcast(F32), ALU.subtract).then_inc(aux_free[s], 1)

                dve.wait_ge(mask_ready, NB)
                V.memset(conv_u[:, 0:2], 0.0).then_inc(merge_step, 1)
                dve.wait_ge(merge_step, 1)
                g = Steps(dve, gate_rows)
                for t in range(NA + O_LAG):
                    if 1 <= t <= NA:
                        for f in att_fills(t - 1):
                            filled(f)
                    if 1 <= t <= GATE_OPS:
                        gate_op(g, t - 1)
                    if t < NA:
                        b = t // NH
                        n, kl = BL[b][1], KL[b]
                        key = ("score", t)
                        s = aux_of(key)
                        take_aux(dve, key)
                        if t >= 2:
                            dve.wait_ge(p_turned, t - 1)
                            dve.wait_ge(negmax_ready, t - 1)
                        V.tensor_tensor_reduce(prob[0:n, t % 2, 0:kl], aux[0:n, s, 0:kl], mask[0:n, MO[b]:MO[b] + kl],
                                               float(DH) ** -0.5, TAKEN, ALU.add, ALU.max, row_max[0:n, t % 2:t % 2 + 1])\
                            .then_inc(aux_free[s], 1)
                        dve.wait_ge(aux_free[s], AUX[key] // 2 + 2)
                        V.tensor_scalar(neg_max[0:n, t % 2:t % 2 + 1], row_max[0:n, t % 2:t % 2 + 1], -1.0, None, ALU.mult)\
                            .then_inc(negmax_ready, 1)
                    if t >= NH + 1 and (t - 2) % NH == NH - 1:
                        finish((t - 2) // NH)
                    if t >= NH - 1 + O_LAG and (t - O_LAG) % NH == NH - 1:
                        turned((t - O_LAG) // NH)

            def mlstm():
                V.memset(mv_tok[:, :, :, P:P + 1], 1.0).then_inc(cols_ready, 1)
                V.memset(m_ss[:, :], 1.0).then_inc(cols_ready, 1)
                s0 = aux_of(("gate_cols",))
                dve.wait_ge(aux_free[s0], AUX[("gate_cols",)] // 2 + 2)
                w = Steps(dve, wt_step)

                def arg(m, c):
                    k0, nk = BL[c]
                    i = NB * m + c
                    if c == 0:
                        key = ("stab", m)
                        dve.wait_ge(aux_free[aux_of(key)], AUX[key] // 2 + 2)
                    V.tensor_scalar(tmp[0:nk, 3 + i % 2, k0:T], tmp[0:nk, 1 + m % 2, k0:T], c_tok[0:nk, c, m:m + 1], 0.0,
                                    ALU.add, ALU.min).then_inc(arg_ready, 1)

                def weights(m, c):
                    k0, nk = BL[c]
                    i = NB * m + c
                    key = ("qk", m, c)
                    sl = aux_of(key)
                    take_aux(dve, key)
                    dve.wait_ge(decay_ready, i + 1)
                    if m >= 2 and c == 0:
                        dve.wait_ge(num_done, NB * (m - 1))
                    wt = m_wt[m % 2]
                    V.tensor_tensor(wt[0:nk, WT[c]:WT[c + 1]], aux[0:nk, sl, 0:T - k0], tmp[0:nk, 3 + i % 2, k0:T], ALU.mult)\
                        .then_inc(aux_free[sl], 1)
                    dve.wait_ge(aux_free[sl], AUX[key] // 2 + 2)
                    diagonal = wt[0:nk, WT[c]:WT[c] + nk]
                    V.tensor_tensor(diagonal, diagonal, causal_keep[0:nk, 0:nk], ALU.mult).then_inc(wt_ready, 1)

                def values(m, b):
                    i = NB * m + b
                    n = BL[b][1]
                    d = den[0:n, i % 2:i % 2 + 1]
                    dve.wait_ge(den_abs, i + 1)
                    V.tensor_tensor(d, d, floor_tok[0:n, b, m:m + 1], ALU.max).then_inc(den_step, 1)
                    dve.wait_ge(den_step, 2 * i + 1)
                    V.reciprocal(d, d).then_inc(den_step, 1)
                    dve.wait_ge(den_step, 2 * i + 2)
                    V.tensor_scalar(m_h[0:n, b, m, :], acc[0:n, 2 + i % 2, 0:P], d, None, ALU.mult).then_inc(num_read, 1)

                for step in range(NB * (NM + 1)):
                    m, c = divmod(step, NB)
                    if m < NM:
                        if c == 0:
                            if m:
                                dve.wait_ge(wt_ready, step)
                            arg(m, 0)
                        if c + 1 < NB:
                            if step >= 1:
                                dve.wait_ge(wt_ready, step)
                            arg(m, c + 1)
                    if step:
                        for f in ml_fills(step - 1):
                            filled(f)
                    if m < NM:
                        weights(m, c)
                    if m >= 1:
                        values(m - 1, c)
                for f in ml_fills(NB * (NM + 1) - 1):
                    filled(f)
                dve.wait_ge(wt_ready, NB * NM)
                s = Steps(dve, mh_step)
                dve.wait_ge(mh_squared, NB * NM)
                s.did(V.tensor_scalar(m_var[:, :], m_ss[:, :], 1.0 / P, EPS, ALU.mult, ALU.add))
                s.settle()
                n = A_UNIT[FIRST_FILL] + 3
                dve.wait_ge(acc_free[0], USE[n] + 2)
                s.did(V.tensor_scalar(mo_t[:, :, :], mo_t[:, :, :], 1.0, None, ALU.add))
                dve.wait_ge(mh_act, 2)
                s.did(V.tensor_tensor(m_var[:, :], m_var[:, :], m_r[:, :], ALU.mult))
                s.settle()
                s.did(V.scalar_tensor_tensor(m_var[:, :], m_var[:, :], -0.5, m_r[:, :], ALU.mult, ALU.mult))
                s.settle()
                s.did(V.scalar_tensor_tensor(m_r[:, :], m_var[:, :], 1.5, m_r[:, :], ALU.add, ALU.mult))
                s.settle()
                for b in range(NB):
                    n = BL[b][1]
                    V.tensor_tensor(m_h[0:n, b, :, :], m_h[0:n, b, :, :],
                                    m_r[0:n, NM * b:NM * b + NM].unsqueeze(2).to_broadcast([n, NM, P]), ALU.mult)\
                        .then_inc(mh_normed, 1)
                for f in range(FILLS - ML_TAIL, FILLS):
                    filled(f)
                for m in range(NM):
                    key = ("hturn", m)
                    sl = aux_of(key)
                    take_aux(dve, key)
                    if m >= 2:
                        dve.wait_ge(brlo_ready, m - 1)
                    gain = cur[:, G_HEAD + m:G_HEAD + m + 1]
                    V.scalar_tensor_tensor(tmp[:, 4 + m % 2, 0:P], aux[:, sl, 0:P], gain, mo_t[:, m, 0:P], ALU.mult, ALU.mult)
                    V.scalar_tensor_tensor(tmp[:, 4 + m % 2, P:T].rearrange("p (b t) -> p b t", t=QB),
                                           aux[:, sl, P:NB * P].rearrange("p (b t) -> p b t", t=P)[:, :, 0:QB], gain,
                                           mo_t[:, m, P:T].rearrange("p (b t) -> p b t", t=QB), ALU.mult, ALU.mult)\
                        .then_inc(aux_free[sl], 1)
                    free_aux(dve, key)

            def merge():
                with dve.Fori(0, KD // 2) as i:
                    for s in range(2):
                        nn = A_MERGE + 6 * s
                        for b in range(3):
                            g = 3 + b
                            sl = SLOT[nn + g]
                            gsl = SLOT[nn + b]
                            dve.wait_ge(acc_free[gsl], USE[nn + b] + 6 * i + 2)
                            dve.wait_ge(acc_done, 1 + nn + g + 12 * i + 1)
                            t = tmp[:, 3 * s + b, :]
                            V.scalar_tensor_tensor(halves(t), halves(t), 1.0, acc_halves(sl), ALU.add, ALU.mult)\
                                .then_inc(acc_free[sl], 1)
                            dve.wait_ge(acc_free[sl], USE[nn + g] + 6 * i + 2)
                            if b == 1:
                                V.tensor_tensor(tmp[:, 3 * s, :], tmp[:, 3 * s, :], t, ALU.add).then_inc(merge_step, 1)
                                dve.wait_ge(merge_step, 2 * i + s + 2)
                        V.tensor_tensor(tmp[:, 3 * s, :], tmp[:, 3 * s, :], tmp[:, 3 * s + 2, :], ALU.add).then_inc(mf_ready, 1)

            dve.wait_ge(io_turned, 1)
            dve.wait_ge(const_landed, 16 * 9)
            V.tensor_copy(params[:, :], aux[:, 0, 0:P]).then_inc(io_first, 1)
            dve.wait_ge(io_turned, 2)
            V.tensor_copy(h[:, :, 0:META], aux[:, 1, 0:KD * META].rearrange("p (k t) -> p k t", k=KD)).then_inc(io_first, 1)
            dve.drain().then_inc(arrived, 1)
            dve.wait_ge(layer_go, 1)

            with dve.Fori(0, DEPTH) as layer:
                c = Steps(dve, cur_ready)
                c.did(V.tensor_copy(cur[:, G_NORM:G_CONV], params[:, bass.ds(layer * 6 * KD, 6 * KD)]))
                c.did(V.tensor_copy(cur[:, G_CONV:G_HEAD], params[:, bass.ds(layer * 3 * KB + DEPTH * 6 * KD, 3 * KB)]))
                c.did(V.tensor_copy(cur[:, G_HEAD:G_HEAD + NM],
                                    params[:, bass.ds(layer * NM + DEPTH * (6 * KD + 3 * KB), NM)]))
                c.did(V.tensor_copy(gate_bias_cur[:, :].unsqueeze(2), gate_bias[:, :, bass.ds(layer, 1)]))
                c.settle()
                for s in (1, 3, 5):
                    v = cur[:, G_NORM + s * KD:G_NORM + (s + 1) * KD]
                    c.did(V.tensor_scalar(v, v, 0.5, None, ALU.mult))
                v = cur[:, G_HEAD:G_HEAD + NM]
                c.did(V.tensor_scalar(v, v, 0.5, None, ALU.mult))
                c.settle()
                norm_out(None, None, 0)
                norm_in_late(0, x_hi, x_lo)
                ffn(0)
                norm_in_late(1, xu_hi, xu_lo)
                norm_in(1)
                rope_all()
                k = Steps(dve, topk_step)
                taps = Steps(dve, conv_step)
                for b in range(1, NB):
                    select_keys(b, k)
                attention()
                mlstm()
                merge()
                dve.wait_ge(mf_ready, KD)
                dve.wait_ge(mlo_ready, 1 + KD)
                V.memset(tmp[:, 4, :], 0.0).then_inc(ysum, 1)
                for m in range(KD):
                    n = A_OUT + m
                    y_square(1, SLOT[n], USE[n] + 2, slice(m, m + 1), m)
                norm_out(1, 0.25 / D, 2)
                norm_in_late(2, x_hi, x_lo)
                ffn(1)
                end_of_layer(dve, layer + 1)

            for i in range(SEQ // P):
                for j in range(2):
                    e = 2 * i + j
                    dve.wait_ge(io_turned, e + 1)
                    if i >= 2:
                        dve.wait_ge(out_stored[i % 2], 16 * (i // 2))
                    V.tensor_copy(w_raw[:, i % 2, 0, 4 * j:4 * j + 4, :].rearrange("p k c -> p (k c)"), acc[:, e % 4, :])\
                        .then_inc(io_placed, 1)

        @block.tensor
        def _(pe):
            MM = nc.tensor.matmul

            def open_acc(n, later=0):
                pe.wait_ge(acc_free[SLOT[n]], USE[n] + later + 1)

            def open_aux(key):
                pe.wait_ge(aux_free[aux_of(key)], AUX[key] // 2 + 1)

            def chunk(slot, wslot, c, xs, k0, kn, wk0=0, first=True, last=True):
                for k in range(kn):
                    lh, ll = w_hi[:, wslot, c, wk0 + k, :], w_lo[:, wslot, c, wk0 + k, :]
                    for j, (w, xx) in enumerate(((lh, xs[0]), (lh, xs[1]), (ll, xs[0]))):
                        for a in range(HALF):
                            ins = MM(acc[:, 2 * slot + a, 0:TH], w, xx[:, k0 + k, a * TH:(a + 1) * TH],
                                     start=(first and k == 0 and j == 0), stop=(last and k == kn - 1 and j == 2))
                return ins

            def token_blocks(n, wslot, pair, cn):
                slot = SLOT[n]
                open_acc(n)
                for a, b in enumerate(pair):
                    t0, rows = BL[b]
                    for k in range(KD):
                        for j in range(3):
                            xx, w = ((x_hi, w_hi), (x_lo, w_hi), (x_hi, w_lo))[j]
                            ins = MM(acc[0:rows, 2 * slot + a, 0:cn * P].rearrange("p (c n) -> p c n", c=cn),
                                     xx[:, k, t0:t0 + rows], w[:, wslot, 0:cn, k, :],
                                     start=(k == 0 and j == 0), stop=(k == KD - 1 and j == 2))
                ins.then_inc(acc_done, 1)

            def norm_sum(q, done, count):
                key = ("norm", q)
                open_aux(key)
                pe.wait_ge(done, count)
                for a in range(HALF):
                    ins = MM(aux_halves(aux_of(key))[:, a, :], ones[:, :], tmp[:, 4, a * TH:(a + 1) * TH], start=True, stop=True)
                ins.then_inc(aux_done, 1)

            def first_unit(n0, p, hi, lo):
                for c in range(2):
                    open_acc(n0 + c)

                def passes(k, ws_xs, last):
                    for c in range(2):
                        slot = SLOT[n0 + c]
                        for j, (w, xx) in enumerate(ws_xs):
                            for a in range(HALF):
                                ins = MM(acc[:, 2 * slot + a, 0:TH], w[:, 0, c, k, :], xx[:, k, a * TH:(a + 1) * TH],
                                         start=(k == 0 and j == 0 and xx is hi), stop=(last and j == len(ws_xs) - 1))
                        if last:
                            ins.then_inc(acc_done, 1)

                for k in range(KD):
                    pe.wait_ge(xhi_ready, KD * p + k + 1)
                    passes(k, ((w_hi, hi), (w_lo, hi)), False)
                norm_sum(2 * p, sq_added, (KD - 1) * (p + 1))
                for k in range(KD):
                    pe.wait_ge(xlo_ready, KD * p + k + 1)
                    passes(k, ((w_hi, lo),), k == KD - 1)

            def ffn(f):
                u0, n0 = U_FFN[f], A_FFN[f]
                def up_unit(i, s):
                    for c in range(2):
                        pe.wait_ge(wlo_ready, split_wait(u0 + s + 2 * i, c))
                        n = n0 + 2 * s + c
                        open_acc(n, 2 * i)
                        chunk(SLOT[n], s, c, (x_hi, x_lo), 0, KD).then_inc(acc_done, 1)

                pe.wait_ge(wlo_ready, split_wait(u0))
                first_unit(n0, 2 * f, x_hi, x_lo)
                up_unit(0, 1)
                with pe.Fori(1, UP_UNITS // 2) as i:
                    for s in range(2):
                        up_unit(i, s)
                pe.wait_ge(alo_ready, 1 + KF * (f + 1))
                n1 = n0 + 2 * UP_UNITS
                with pe.Fori(0, KD // 4) as i:
                    for q in range(6):
                        kg = q % 3
                        for c in range(2):
                            pe.wait_ge(wlo_ready, split_wait(u0 + UP_UNITS + q + 6 * i, c))
                            n = n1 + 2 * (q // 3) + c
                            if kg == 0:
                                open_acc(n, 2 * i)
                            ins = chunk(SLOT[n], q % 2, c, (a_hi, a_lo), kg * KD, DOWN_K[kg], 0, kg == 0, kg == 2)
                            if kg == 2:
                                ins.then_inc(acc_done, 1)
                        if kg < 2:
                            ins.then_inc(part_done, 1)
                norm_sum(4 * f + 1, ysum, (KD + 1) * (2 * f + 1))

            def mixer_acc(j, c):
                kind, n, ws = MIX[j][0], A_UNIT[j] + c, (U_MIX + j) % 2
                if kind in ("v", "mv"):
                    pe.wait_ge(wlo_ready, split_wait(U_MIX + j))
                    token_blocks(n, ws, ((0, 1), (2, 3), (4,))[c], 1 if kind == "v" else 2)
                else:
                    pe.wait_ge(wlo_ready, split_wait(U_MIX + j, c))
                    open_acc(n)
                    chunk(SLOT[n], ws, c, (xu_hi, xu_lo) if j < N_EARLY else (x_hi, x_lo), 0, KD).then_inc(acc_done, 1)

            def mixer_unit(j):
                for c in range(N_MIXACC[j]):
                    mixer_acc(j, c)

            def over_tokens(key, lhsT, rhs, n0, n1, rows=P):
                s = aux_of(key)
                open_aux(key)
                for a, z in ((0, 512), (512, 1024)):
                    if a < n1 - n0:
                        e = min(z, n1 - n0)
                        ins = MM(aux[0:rows, s, a:e], lhsT, rhs[:, n0 + a:n0 + e], start=True, stop=True)
                ins.then_inc(aux_done, 1)

            def in_sbuf(j):
                for n in (A_UNIT[j], A_UNIT[j] + 1):
                    pe.wait_ge(acc_free[SLOT[n]], USE[n] + 2)

            def rotate(i):
                over_tokens(("rot", i), rope_mats[:, ROT, :], qi_t[:, i, :] if i < 2 else q_t[:, i - 2, :], 0, T)

            def duplicate(i):
                src, d, r = ((3, DUP0, DROT0), (4, DUP0, DROT0), (4, DUP1, DROT1))[i]
                over_tokens(("dup", i), rope_mats[:, d, :], tmp[:, src, :], 0, T)
                over_tokens(("dup_rot", i), rope_mats[:, r, :], tmp[:, src, :], 0, T)

            def early_units():
                mixer_unit(1)
                mixer_acc(2, 0)
                pe.wait_ge(rope_landed, 32)
                in_sbuf(0)
                rotate(0)
                rotate(1)
                mixer_acc(2, 1)
                in_sbuf(1)
                duplicate(0)
                mixer_acc(3, 0)
                duplicate(1)
                mixer_acc(3, 1)
                duplicate(2)
                pe.wait_ge(xnlo_ready, KD)
                mixer_acc(4, 0)
                in_sbuf(2)
                rotate(2)
                rotate(3)
                mixer_acc(4, 1)
                in_sbuf(3)
                rotate(4)
                rotate(5)
                mixer_acc(4, 2)
                pe.wait_ge(wi_scaled, 1)
                key = ("wi",)
                open_aux(key)
                for b in range(1, NB):
                    t0, n = BL[b]
                    ins = nc.tensor.transpose(aux[0:n, aux_of(key), (b - 1) * P:b * P], tmp[:, 3, t0:t0 + n], ident[:, :])
                ins.then_inc(aux_done, 1)

            def fill(g):
                j, c, k = FIRST_FILL + g // (2 * KD), g // KD % 2, g % KD
                n = A_UNIT[j] + c
                if k == 0:
                    pe.wait_ge(wlo_ready, split_wait(U_MIX + j, c))
                    open_acc(n)
                ins = chunk(0, (U_MIX + j) % 2, c, (x_hi, x_lo), k, 1, k, k == 0, k == KD - 1)
                if k == KD - 1:
                    ins.then_inc(acc_done, 1)

            def attention():
                pe.wait_ge(rope_done, 2)
                for c in range(2):
                    n = A_UNIT[FIRST_FILL] - 1 - c
                    pe.wait_ge(acc_free[SLOT[n]], USE[n] + 2)
                for t in range(NA + O_LAG):
                    if t < NA:
                        b, hd = divmod(t, NH)
                        t0, n = BL[b]
                        po = DH * (hd % 2)
                        over_tokens(("score", t), q_t[po:po + DH, hd // 2, t0:t0 + n],
                                    k_t[po:po + DH, hd // (NH // NKV), :], 0, KL[b], n)
                        for f in att_fills(t)[:1]:
                            fill(f)
                    if 1 <= t <= NA:
                        s = t - 1
                        b = s // NH
                        n = BL[b][1]
                        pe.wait_ge(p_ready, s + 1)
                        if s >= 1:
                            pe.wait_ge(pt_copied, s)
                        for c in range(b + 1):
                            k0, nk = BL[c]
                            ins = nc.tensor.transpose(acc[0:nk, 2, c * n:(c + 1) * n], prob[0:n, s % 2, k0:k0 + nk],
                                                      ident[0:n, 0:n])
                        ins.then_inc(p_turned, 1)
                    if 2 <= t <= NA + 1:
                        s = t - 2
                        b, hd = divmod(s, NH)
                        n = BL[b][1]
                        g = hd // (NH // NKV)
                        pe.wait_ge(pt_copied, s + 1)
                        if hd == 0 and b >= 1:
                            pe.wait_ge(o_read, b)
                        for c in range(b + 1):
                            nk = BL[c][1]
                            ins = MM(acc[0:n, 3, hd * DH:(hd + 1) * DH], prob_t[0:nk, s % 2, c * n:(c + 1) * n],
                                     v_tok[0:nk, c, g * DH:(g + 1) * DH], start=(c == 0), stop=(c == b))
                        ins.then_inc(pv_done, 1)
                    if t >= NH - 1 + O_LAG and (t - O_LAG) % NH == NH - 1:
                        b = (t - O_LAG) // NH
                        n = BL[b][1]
                        key = ("turn", b)
                        open_aux(key)
                        pe.wait_ge(o_read, b + 1)
                        for j in range(KB):
                            ins = nc.tensor.transpose(aux[:, aux_of(key), j * n:(j + 1) * n],
                                                      tmp[0:n, 2 + b % 2, j * P:(j + 1) * P], ident[0:n, 0:n])
                        ins.then_inc(aux_done, 1)

                    if t == GATE_STEP:
                        key = ("gate_cols",)
                        open_aux(key)
                        pe.wait_ge(gates_ready, 1)
                        for which, r in ((0, 4), (1, 0)):
                            for b in range(NB):
                                t0, n = BL[b]
                                o = NM * (NB * which + b)
                                ins = nc.tensor.transpose(aux[0:n, aux_of(key), o:o + NM], tmp[0:NM, r, t0:t0 + n],
                                                          ident[0:NM, 0:NM])
                        ins.then_inc(aux_done, 1)
                    if t < NA:
                        for f in att_fills(t)[1:]:
                            fill(f)

            def mlstm():
                pe.wait_ge(sel_landed, 16)
                pe.wait_ge(cols_ready, 2)

                def qk(m, c):
                    k0, nk = BL[c]
                    over_tokens(("qk", m, c), mk_t[:, m, k0:k0 + nk], mq_t[:, m, :], k0, T, nk)

                def stab(m):
                    over_tokens(("stab", m), sel_sb[:, m, :], tmp[0:NM, 5, :], 0, T)

                stab(0)
                for step in range(NB * (NM + 1)):
                    m, b = divmod(step, NB)
                    if m < NM:
                        qk(m, b)
                    i = step - NB
                    if i >= 0:
                        t0, n = BL[b]
                        pe.wait_ge(wt_ready, i + 1)
                        if i >= 2:
                            pe.wait_ge(num_read, i - 1)
                        for c in range(b + 1):
                            k0, nk = BL[c]
                            o = WT[c] + t0 - k0
                            ins = MM(acc[0:n, 2 + i % 2, 0:P + 1], m_wt[(m - 1) % 2][0:nk, o:o + n], mv_tok[0:nk, c, m - 1, :],
                                     start=(c == 0), stop=(c == b))
                        ins.then_inc(num_done, 1)
                    if b == NB - 1 and m + 1 < NM:
                        stab(m + 1)
                    for f in ml_fills(step):
                        fill(f)
                for f in range(FILLS - ML_TAIL, FILLS):
                    fill(f)
                pe.wait_ge(mh_normed, NB)
                for m in range(NM):
                    key = ("hturn", m)
                    open_aux(key)
                    for b in range(NB):
                        n = BL[b][1]
                        ins = nc.tensor.transpose(aux[:, aux_of(key), b * P:b * P + n], m_h[0:n, b, m, :], ident[0:n, 0:n])
                    ins.then_inc(aux_done, 1)
                pe.wait_ge(num_read, NB * NM)

            pe.wait_ge(const_landed, 16 * 9)
            nc.tensor.transpose(aux[:, 0, 0:P], tmp[:, 5, 0:P], ident[:, :]).then_inc(io_turned, 1)
            pe.wait_ge(io_in, 16)
            for k in range(KD):
                ins = nc.tensor.transpose(aux[:, 1, k * META:(k + 1) * META], tmp[0:META, k // 4, (k % 4) * P:(k % 4 + 1) * P],
                                          ident[0:META, 0:META])
            ins.then_inc(io_turned, 1)
            for i in range(SEQ // P):
                pe.wait_ge(raw_landed[i % 2], 16 * (i // 2 + 1))
                for j in range(2):
                    e = 2 * i + j
                    if e >= 4:
                        pe.wait_ge(io_placed, e - 3)
                    for k in range(4):
                        ins = nc.tensor.transpose(acc[:, e % 4, k * P:(k + 1) * P], w_raw[:, i % 2, 0, 4 * j + k, :], ident[:, :])
                    ins.then_inc(io_turned, 1)
            pe.wait_ge(io_placed, 2 * (SEQ // P))
            pe.wait_ge(io_first, 2)
            pe.drain().then_inc(arrived, 1)
            pe.wait_ge(layer_go, 1)

            with pe.Fori(0, DEPTH) as layer:
                ffn(0)
                pe.wait_ge(wlo_ready, split_wait(U_MIX))
                first_unit(A_MIX, 1, xu_hi, xu_lo)
                early_units()
                pe.wait_ge(rope_done, 1)
                for b in range(1, NB):
                    t0, n = BL[b]
                    for i in range(NIDX):
                        po = DH * (i % 2)
                        over_tokens(("index", b, i), qi_t[po:po + DH, i // 2, t0:t0 + n], ki_t[po:po + DH, :], 0, KL[b], n)
                    for j in UNITS_AFTER[b]:
                        mixer_unit(j)
                attention()
                mlstm()
                with pe.Fori(0, KD // 2) as i:
                    for s in range(2):
                        nn = A_MERGE + 6 * s
                        u = U_MERGE + 3 * s
                        for r, parts in enumerate((((0, "x", 0), (1, "x", 0)), ((0, "x", 0), (1, ya, 0), (1, yb, KB)),
                                                   ((0, yc, 0),))):
                            for a, (c, xs, wk0) in enumerate(parts):
                                pe.wait_ge(wlo_ready, split_wait(u + r + 6 * i, 1 if r == 2 else c))
                                n = nn + 2 * r + a + (1 if r == 2 else 0)
                                if xs == ya:
                                    pe.wait_ge(brlo_ready, 2 * KB)
                                open_acc(n, 6 * i)
                                full = xs == "x"
                                chunk(SLOT[n], (u + r) % 2, c, (x_hi, x_lo) if full else xs, 0, KD if full else KB, wk0)\
                                    .then_inc(acc_done, 1)
                pe.wait_ge(mlo_ready, 1 + KD)
                for j in range(OUT_UNITS):
                    u = U_OUT + j
                    for c in range(2):
                        pe.wait_ge(wlo_ready, split_wait(u, c))
                        n = A_OUT + 2 * j + c
                        open_acc(n)
                        chunk(SLOT[n], u % 2, c, (mg_hi, mg_lo), 0, KD).then_inc(acc_done, 1)
                norm_sum(3, ysum, (KD + 1) * 2)
                ffn(1)
                end_of_layer(pe, layer + 1)

            for i in range(SEQ // P):
                for j in range(2):
                    e = 2 * i + j
                    if e >= 4:
                        pe.wait_ge(io_placed, e - 3)
                    for k in range(4):
                        ins = nc.tensor.transpose(acc[:, e % 4, k * P:(k + 1) * P],
                                                  h[:, 4 * j + k, META + i * P:META + (i + 1) * P], ident[:, :])
                    ins.then_inc(io_turned, 1)


def shape_constants(meta_rows, seq, head_dim):
    import numpy as np

    t = meta_rows + seq
    freq = (1.0 / (10000.0 ** (np.arange(0, head_dim, 2, dtype=np.float32) / head_dim))).astype(np.float32)
    angle = np.arange(t, dtype=np.float32)[None, :] * freq[np.arange(P) % (head_dim // 2)][:, None]
    tables = np.stack([np.cos(angle), np.sin(angle)]).astype(np.float32)
    half = head_dim // 2
    i = np.arange(P)
    rot = np.zeros((P, P), np.float32)
    rot[(i + half) % head_dim + i // head_dim * head_dim, i] = np.where(i % head_dim < half, -1.0, 1.0)
    dup = np.zeros((2, P, P), np.float32)
    for g in range(2):
        dup[g, g * head_dim + i % head_dim, i] = 1.0
    tri = i[None, :] <= i[:, None]
    mats = np.stack([np.eye(P), np.ones((P, P)), np.where(tri, 0.0, NEG), tri.T, rot, dup[0], dup[1],
                     dup[0] @ rot, dup[1] @ rot]).astype(np.float32)
    sel = np.zeros((4, 4, P), np.float32)
    sel[np.arange(4), np.arange(4)] = 1.0
    return {"rope_tab": tables, "mats": mats, "sel": sel}


_INS = ["x", "meta", "norm_g", "w_ffn_gu", "w_ffn_down", "w_in", "w_conv", "b_igate", "b_fgate",
        "mh_norm_g", "w_branch", "w_out"]


def kernel(**inputs):
    import numpy as np
    import concourse.bacc as bacc
    from concourse.bass_utils import run_bass_kernel_spmd

    nc = bacc.Bacc("TRN2", target_bir_lowering=False, num_devices=1)
    arrays, args = {}, []
    data = {name: np.ascontiguousarray(inputs[name]) for name in _INS}
    data.update(shape_constants(data["meta"].shape[0], data["x"].shape[1], 64))
    for name, a in data.items():
        arrays[f"in_{name}_dram"] = a
        args.append(nc.dram_tensor(f"in_{name}_dram", a.shape, mybir.dt.from_np(a.dtype), kind="ExternalInput").ap())
    out = nc.dram_tensor("out_dram", data["x"].shape, F32, kind="ExternalOutput").ap()
    trunk_program(nc, *args, out)
    r = run_bass_kernel_spmd(nc, [arrays], core_ids=[0])
    return r.results[0]["out_dram"]
```

```python
from contextlib import ExitStack

import concourse.bass as bass
from concourse import mybir

F32 = mybir.dt.float32
F32R = mybir.dt.float32r
ALU = mybir.AluOpType
ACT = mybir.ActivationFunctionType
AX = mybir.AxisListType

P = 128
HALF = 2
EPS = 1e-6
NEG = -1e30
TAKEN = -3e38
LN_EXP_SET = "natural_log_exp_and_others"
TANH_SET = "exp_and_others"


def trunk_program(nc, x, meta, norm_g, w_ffn_gu, w_ffn_down, w_in, w_conv, b_igate, b_fgate,
                  mh_norm_g, w_branch, w_out, rope_tab, mats, sel, out):
    DEPTH, _, D, F2 = w_ffn_gu.shape
    SEQ, META = x.shape[1], meta.shape[0]
    T = SEQ + META
    TH = T // HALF
    FF = F2 // 2
    KD = D // P
    KF = FF // P
    BW = w_branch.shape[2]
    KB = BW // P
    DH = 64
    NH = BW // DH
    NKV, NIDX = 2, 4
    NM = BW // P
    TOPK = min(256, SEQ // 4)
    NB = 5
    QB = (T - P) // (NB - 1)
    BL = [(0, P)] + [(P + i * QB, QB) for i in range(NB - 1)]
    KL = [t0 + n for t0, n in BL]
    MO = [sum(KL[:b]) for b in range(NB)]
    assert T == P + (NB - 1) * QB and TOPK == P and D == 2 * BW and KB == 4 and NM == 4
    C_CX, C_CB, C_CC = 0, BW, 2 * BW
    C_Q = 3 * BW
    C_K = C_Q + BW
    C_V = C_K + NKV * DH
    C_QI = C_V + NKV * DH
    C_KI = C_QI + NIDX * DH
    C_MQ = C_KI + DH + NIDX
    C_MK, C_MV, C_MO = C_MQ + BW, C_MQ + 2 * BW, C_MQ + 3 * BW
    C_MI = C_MQ + 4 * BW
    C_MF = C_MI + NM
    C_GT = C_MF + NM

    UP_UNITS = KF
    DOWN_K = [KD, KD, KF - 2 * KD]
    DOWN_UNITS = 3 * KD // 2
    FFN_UNITS = UP_UNITS + DOWN_UNITS
    MIX = [("qi", C_QI, C_QI + P), ("k", C_K, C_KI), ("q", C_Q, C_Q + P), ("q", C_Q + 2 * P, C_Q + 3 * P),
           ("v", C_V, C_V + P), ("if", C_MI, C_MF)]
    for kind, c in (("mq", C_MQ), ("mk", C_MK), ("mv", C_MV), ("mo", C_MO)):
        MIX += [(kind, c + 2 * j * P, c + (2 * j + 1) * P) for j in range(2)]
    for j in range(0, KB, 2):
        MIX += [("cxc", C_CX + j * P, C_CC + j * P), ("cxc", C_CX + (j + 1) * P, C_CC + (j + 1) * P),
                ("cb", C_CB + j * P, C_CB + (j + 1) * P)]
    N_MIX = len(MIX)
    FIRST_CONV = N_MIX - 6
    FIRST_FILL = FIRST_CONV - 2
    MERGE_UNITS = 3 * KD
    OUT_UNITS = KD // 2
    U_MIX = FFN_UNITS
    U_MERGE = U_MIX + N_MIX
    U_OUT = U_MERGE + MERGE_UNITS
    U_FFN = [0, U_OUT + OUT_UNITS]
    UNITS = U_FFN[1] + FFN_UNITS
    assert DEPTH == 2 and UNITS % 2 == 0
    ACCS = {"v": 3, "mv": 3}
    N_MIXACC = [ACCS.get(kind, 2) for kind, _, _ in MIX]
    A_MIX = 2 * UP_UNITS + KD
    A_UNIT = [A_MIX + sum(N_MIXACC[:i]) for i in range(N_MIX)]
    A_MERGE = A_MIX + sum(N_MIXACC)
    A_OUT = A_MERGE + 6 * KD
    A_FFN = [0, A_OUT + KD]
    UNITS_AFTER = {1: (5,), 2: (6, 7), 3: (8, 9), 4: (10, 11)}
    assert UNITS_AFTER[NB - 1][-1] == FIRST_FILL - 1
    SLOT, USE = [], []
    for n in range(A_FFN[1] + 2 * UP_UNITS + KD):
        SLOT.append(0 if A_UNIT[FIRST_FILL] <= n < A_MERGE else n % 2)
        USE.append(SLOT[:-1].count(SLOT[-1]))
    FILLS = 2 * KD * (N_MIX - FIRST_FILL)
    ML_TAIL = KD
    ML_PLAN = [2, 1, 1, 1, 1] + NM * NB * [2]
    ATT_FILLS = FILLS - ML_TAIL - sum(ML_PLAN)
    ATT_TAIL = 10

    def att_fills(t):
        steps, spread = NB * NH, ATT_FILLS - ATT_TAIL
        if t == steps + 2:
            return range(spread, ATT_FILLS)
        return range(spread * min(t, steps) // steps, spread * min(t + 1, steps) // steps)

    def ml_fills(step):
        f = ATT_FILLS + sum(ML_PLAN[:step])
        return range(f, f + ML_PLAN[step])

    AUX = {}

    def aux_item(*key):
        AUX[key] = len(AUX)

    for q in range(3):
        aux_item("norm", q)
    for r in range(2):
        aux_item("rot", r)
    for r in range(3):
        aux_item("dup", r)
        aux_item("dup_rot", r)
    for r in range(2, 2 + KB):
        aux_item("rot", r)
    aux_item("wi")
    N_EARLY = 4
    for b in range(1, NB):
        for i in range(NIDX):
            aux_item("index", b, i)
    NA = NB * NH
    GATE_STEP = 20
    O_LAG = 4
    for t in range(NA + O_LAG):
        if t < NA:
            aux_item("score", t)
        if t >= NH - 1 + O_LAG and (t - O_LAG) % NH == NH - 1:
            aux_item("turn", (t - O_LAG) // NH)
        if t == GATE_STEP:
            aux_item("gate_cols")
    for m in range(NM):
        aux_item("stab", m)
        for c in range(NB):
            aux_item("qk", m, c)
    for m in range(NM):
        aux_item("hturn", m)
    for q in range(3, 6):
        aux_item("norm", q)

    ctx = ExitStack()
    with ctx:
        def sem(name):
            return ctx.enter_context(nc.semaphore(name))

        CH = 4 * T
        arena_bytes = 212800
        arena = ctx.enter_context(nc.sbuf_tensor("arena", [P, arena_bytes // 4], F32))
        del arena
        base = nc.sbuf_base - arena_bytes
        place = [0]

        def at(name, shape, dt, offset):
            return nc.alloc_sbuf_tensor_at(name, shape, dt, offset=base + offset)

        def sb(name, shape, dt=F32):
            size = 4
            for s in shape[1:]:
                size *= s
            t = at(name, shape, dt, place[0])
            place[0] += (size + 31) // 32 * 32
            assert place[0] <= arena_bytes, (name, place[0])
            return t

        h = sb("h", [P, KD, T])
        y = at("y", [P, KD, T], F32, place[0])
        x_hi = sb("x_hi", [P, KD, T], F32R)
        x_lo = sb("x_lo", [P, KD, T], F32R)
        w_raw = sb("w_raw", [P, 2, 2, KD, P])
        w_hi = sb("w_hi", [P, 2, 2, KD, P], F32R)
        w_lo = sb("w_lo", [P, 2, 2, KD, P], F32R)
        tmp = sb("tmp", [P, 6, T])
        region = place[0]
        place[0] += 46 * CH

        def at_chunk(name, shape, dt, chunk, extra=0):
            return at(name, shape, dt, region + chunk * CH + extra)

        a_hi = at_chunk("a_hi", [P, KF, T], F32R, 0)
        a_lo = at_chunk("a_lo", [P, KF, T], F32R, KF)
        x_rows = at_chunk("x_rows", [P, SEQ // P, D], F32, 0)
        xu_hi = at_chunk("xu_hi", [P, KD, T], F32R, 21)
        xu_lo = at_chunk("xu_lo", [P, KD, T], F32R, 29)
        q_t = at_chunk("q_t", [P, KB, T], F32, 0)
        qi_t = at_chunk("qi_t", [P, 2, T], F32, 4)
        ki_t = at_chunk("ki_t", [P, T], F32, 6)
        k_t = at_chunk("k_t", [P, NKV, T], F32, 7)
        cos_sin = at_chunk("cos_sin", [P, 2, T], F32, 9)
        mask = at_chunk("mask", [P, sum(KL)], F32, 11)
        rope_mats = at_chunk("rope_mats", [P, 5, P], F32, 15)
        prob = at_chunk("prob", [P, 2, T], F32, 15)
        prob_t = at_chunk("prob_t", [P, 2, 512], F32, 17)
        v_tok = at_chunk("v_tok", [P, NB, P], F32, 19)
        mq_t = at_chunk("mq_t", [P, NM, T], F32, 21)
        mk_t = at_chunk("mk_t", [P, NM, T], F32, 25)
        mo_t = at_chunk("mo_t", [P, NM, T], F32, 29)
        mv_tok = at_chunk("mv_tok", [P, NB, NM, P + 1], F32, 33)
        yb_hi = at_chunk("yb_hi", [P, KB, T], F32R, 38)
        yb_lo = at_chunk("yb_lo", [P, KB, T], F32R, 42)
        WT = [sum(T - BL[i][0] for i in range(c)) for c in range(NB + 1)]
        m_wt = [at_chunk("m_wt0", [P, WT[NB]], F32, 0), at_chunk("m_wt1", [P, WT[NB]], F32, 16)]
        assert WT[NB] <= 3 * T
        m_h = at_chunk("m_h", [P, NB, NM, P], F32, 11)
        cx_t = at_chunk("cx_t", [P, T], F32, 6)
        ya_f = [at_chunk(f"ya_f{c}", [P, T], F32, (4, 5, 7, 8)[c]) for c in range(KB)]
        conv_u = at_chunk("conv_u", [P, T + 2], F32, 9)
        sel_sb = at_chunk("sel_sb", [NM, NM, P], F32, 10, 64)
        yc_hi = at_chunk("yc_hi", [P, KB, T], F32R, 21)
        yc_lo = at_chunk("yc_lo", [P, KB, T], F32R, 25)
        ya_hi = at_chunk("ya_hi", [P, KB, T], F32R, 11)
        ya_lo = at_chunk("ya_lo", [P, KB, T], F32R, 15)
        mg_hi = at_chunk("mg_hi", [P, KD, T], F32R, 0)
        mg_lo = at_chunk("mg_lo", [P, KD, T], F32R, 29)
        ident = sb("ident", [P, P])
        ones = sb("ones", [P, P])
        causal_bias = sb("causal_bias", [P, P])
        causal_keep = sb("causal_keep", [P, P])
        params = sb("params", [P, P])
        cur = sb("cur", [P, 64])
        next_gain = sb("next_gain", [P, KD])
        eps_col = sb("eps_col", [P, 1])
        gate_bias = sb("gate_bias", [NM, 2, DEPTH])
        gate_bias_cur = sb("gate_bias_cur", [NM, 2])

        def small(first_chunk, offset, tiles):
            made = []
            for name, shape in tiles:
                made.append(at(name, [P, *shape], F32, region + first_chunk * CH + offset))
                size = 4
                for d in shape:
                    size *= d
                offset += (size + 31) // 32 * 32
            return made

        wi_tok, top8, row_max, neg_max, row_sum, row_inv = small(11, 4 * sum(KL), (
            ("wi_tok", (NB, NIDX)), ("top8", (8,)), ("row_max", (2,)), ("neg_max", (2,)), ("row_sum", (2, NH)),
            ("row_inv", (NH,))))
        c_tok, floor_tok, den, m_ss, m_var, m_r = small(19, 4 * NB * P, (
            ("c_tok", (NB, NM)), ("floor_tok", (NB, NM)), ("den", (2,)), ("m_ss", (NB * NM,)),
            ("m_var", (NB * NM,)), ("m_r", (NB * NM,))))
        yb, ya, yc = (yb_hi, yb_lo), (ya_hi, ya_lo), (yc_hi, yc_lo)
        ROT, DUP0, DUP1, DROT0, DROT1 = range(5)
        G_NORM, G_CONV, G_HEAD = 0, 6 * KD, 6 * KD + 3 * KB

        acc = ctx.enter_context(nc.psum_tensor("acc", [P, 4, 512], F32))
        aux = ctx.enter_context(nc.psum_tensor("aux", [P, 2, 1024], F32))

        def out_tile(i):
            return acc[:, 2 * i:2 * i + 2, :].rearrange("p a c -> p (a c)") if i < 2 else aux[:, i - 2, :]

        def acc_halves(slot):
            return acc[:, 2 * slot:2 * slot + 2, 0:TH]

        def halves(t):
            return t.rearrange("p (a t) -> p a t", a=HALF)

        def aux_halves(slot):
            return aux[:, slot, :].rearrange("p (a t) -> p a t", a=HALF)[:, :, 0:TH]

        const_landed = sem("const_landed")
        later_landed = sem("later_landed")
        arrived = sem("arrived")
        layer_go = sem("layer_go")
        out_turned = sem("out_turned")
        out_copied = [sem("out_copied0"), sem("out_copied1")]
        io_in = sem("io_in")
        x_landed = [sem(f"x_landed{i}") for i in range(SEQ // P)]
        io_turned = sem("io_turned")
        io_placed = sem("io_placed")
        io_first = sem("io_first")
        out_stored = [sem("out_stored0"), sem("out_stored1")]
        raw_landed = [sem("raw_landed0"), sem("raw_landed1")]
        whi_ready = sem("whi_ready")
        wlo_ready = sem("wlo_ready")
        acc_done = sem("acc_done")
        part_done = sem("part_done")
        acc_free = [sem("acc_free0"), sem("acc_free1")]
        aux_done = sem("aux_done")
        aux_free = [sem("aux_free0"), sem("aux_free1")]
        cur_ready = sem("cur_ready")
        h_ready = sem("h_ready")
        sq_ready = sem("sq_ready")
        sq_added = sem("sq_added")
        log_ready = sem("log_ready")
        seed_ready = sem("seed_ready")
        newton = sem("newton")
        rstd_ready = sem("rstd_ready")
        xf_ready = sem("xf_ready")
        xhi_ready = sem("xhi_ready")
        xlo_ready = sem("xlo_ready")
        first_scaled = sem("first_scaled")
        silu_ready = sem("silu_ready")
        act_ready = sem("act_ready")
        xnhi_ready = sem("xnhi_ready")
        xnlo_ready = sem("xnlo_ready")
        wi_scaled = sem("wi_scaled")
        ahi_ready = sem("ahi_ready")
        alo_ready = sem("alo_ready")
        ysum = sem("ysum")
        ysq_ready = sem("ysq_ready")
        res_ready = sem("res_ready")
        rope_landed = sem("rope_landed")
        rope_step = sem("rope_step")
        rope_done = sem("rope_done")
        index_step = sem("index_step")
        mask_ready = sem("mask_ready")
        topk_step = sem("topk_step")
        negmax_ready = sem("negmax_ready")
        p_ready = sem("p_ready")
        p_turned = sem("p_turned")
        pt_copied = sem("pt_copied")
        pv_done = sem("pv_done")
        inv_ready = sem("inv_ready")
        o_read = sem("o_read")
        ybhi_ready = sem("ybhi_ready")
        gate_step = sem("gate_step")
        gate_rows = sem("gate_rows")
        gates_ready = sem("gates_ready")
        sel_landed = sem("sel_landed")
        cols_ready = sem("cols_ready")
        arg_ready = sem("arg_ready")
        decay_ready = sem("decay_ready")
        wt_ready = sem("wt_ready")
        num_done = sem("num_done")
        den_abs = sem("den_abs")
        den_step = sem("den_step")
        num_read = sem("num_read")
        mh_squared = sem("mh_squared")
        mh_step = sem("mh_step")
        mh_act = sem("mh_act")
        mh_normed = sem("mh_normed")
        conv_step = sem("conv_step")
        brhi_ready = sem("brhi_ready")
        brlo_ready = sem("brlo_ready")
        merge_step = sem("merge_step")
        mf_ready = sem("mf_ready")
        mhi_ready = sem("mhi_ready")
        mlo_ready = sem("mlo_ready")
        OF_STREAM = [res_ready, h_ready, sq_ready, sq_added, xhi_ready]
        OF_MIXER = [rope_landed, rope_step, rope_done, xf_ready, xnhi_ready, xnlo_ready, wi_scaled, index_step, mask_ready,
                    topk_step, negmax_ready, p_ready, p_turned, pt_copied, pv_done, inv_ready, o_read, ybhi_ready,
                    gate_step, gate_rows, gates_ready, sel_landed, cols_ready, arg_ready, decay_ready, wt_ready,
                    num_done, den_abs, den_step, num_read, mh_squared, mh_step, mh_act, mh_normed, conv_step,
                    brhi_ready, brlo_ready, merge_step, mf_ready, mhi_ready, mlo_ready]
        PER_LAYER = [*raw_landed, whi_ready, wlo_ready, acc_done, part_done, *acc_free, aux_done, *aux_free,
                     cur_ready, first_scaled, silu_ready, act_ready, log_ready, seed_ready, newton, rstd_ready, xlo_ready, ahi_ready,
                     alo_ready, ysum, ysq_ready]
        ENGINES = 5
        OUT_TURN, IN_TURN = (2, 0, 1), (1, 2, 0)
        N_CUR = 9

        class Steps:

            def __init__(self, eng, semaphore):
                self.eng, self.sem, self.n = eng, semaphore, 0

            def did(self, ins):
                ins.then_inc(self.sem, 1)
                self.n += 1

            def settle(self):
                self.eng.wait_ge(self.sem, self.n)

        def layer_used(eng):
            eng.drain().then_inc(arrived, 1)

        def next_layer(eng, layer):
            eng.wait_ge(layer_go, layer + 2)

        def take_aux(eng, key):
            eng.wait_ge(aux_done, AUX[key] + 1)

        def aux_of(key):
            return AUX[key] % 2

        def free_aux(eng, key):
            eng.wait_ge(aux_free[aux_of(key)], AUX[key] // 2 + 2)

        gu_v = w_ffn_gu.rearrange("l f (k p) c -> l f p k c", p=P)
        down_v = w_ffn_down.rearrange("l f (k p) c -> l f p k c", p=P)
        in_v = w_in.rearrange("l (k p) c -> l p k c", p=P)
        branch_v = w_branch.rearrange("l b (k p) c -> l p (b k) c", p=P)
        out_v = w_out.rearrange("l (k p) c -> l p k c", p=P)

        block = ctx.enter_context(nc.Block())

        @block.sync
        def _(sp):
            sp.dma_start(ident[:, :], mats[0]).then_inc(const_landed, 16)
            rows = 0
            for src in (norm_g.rearrange("l s (c p) -> (l s c) p", p=P),
                        w_conv.rearrange("l j (c p) -> (l j c) p", p=P),
                        mh_norm_g.rearrange("l (c p) -> (l c) p", p=P)):
                n = src.shape[0]
                sp.dma_start(tmp[rows:rows + n, 5, 0:P], src).then_inc(const_landed, 16)
                rows += n
            assert rows == P
            sp.dma_start(tmp[0:META, 0:2, 0:512], meta.rearrange("t (a f) -> t a f", a=2)).then_inc(io_in, 16)
            def first_weights(u):
                for c in range(2):
                    sp.dma_start(w_raw[:, u, c, :, :], gu_v[0, 0, :, :, c * FF + u * P:c * FF + (u + 1) * P])\
                        .then_inc(raw_landed[u], 16)

            first_weights(0)
            for i in range(SEQ // P):
                sp.dma_start(x_rows[:, i, :], x[0, i * P:(i + 1) * P, :]).then_inc(x_landed[i], 16)
            first_weights(1)
            for dst, src in ((ones, mats[1]), (causal_bias, mats[2]), (causal_keep, mats[3])):
                sp.dma_start(dst[:, :], src).then_inc(later_landed, 16)
            sp.dma_start(gate_bias[:, 0, :], b_igate.rearrange("l m -> m l"),
                         allow_slow_non_contiguous=True).then_inc(later_landed, 16)
            sp.dma_start(gate_bias[:, 1, :], b_fgate.rearrange("l m -> m l"),
                         allow_slow_non_contiguous=True).then_inc(later_landed, 16)
            rows_v = w_raw[:, :, :, :, :].rearrange("p s c k j -> p (s c k j)")

            def load(u, parts, slot):
                sp.wait_ge(wlo_ready, 2 * u + 2)
                for dst, src in parts:
                    sp.dma_start(dst, src).then_inc(raw_landed[slot], 16)

            def chunk_pair(slot, srcs, kn):
                return [(w_raw[:, slot, c, 0:kn, :], s) for c, s in enumerate(srcs)]

            def load_ffn(f, layer):
                with sp.Fori(1 if f == 0 else 0, UP_UNITS // 2) as i:
                    for s in range(2):
                        col = sp.snap((2 * i + s) * P)
                        col2 = sp.snap((2 * i + s) * P + FF)
                        load(U_FFN[f] + 2 * i + s,
                             chunk_pair(s, [gu_v[layer, f, :, :, bass.ds(col, P)],
                                            gu_v[layer, f, :, :, bass.ds(col2, P)]], KD), s)
                with sp.Fori(0, KD // 4) as i:
                    for q in range(6):
                        kg = q % 3
                        rows = slice(kg * KD, kg * KD + DOWN_K[kg])
                        cols = [sp.snap((4 * i + 2 * (q // 3) + c) * P) for c in range(2)]
                        load(U_FFN[f] + UP_UNITS + 6 * i + q,
                             chunk_pair(q % 2, [down_v[layer, f, :, rows, bass.ds(c, P)] for c in cols],
                                        DOWN_K[kg]), q % 2)

            with sp.Fori(0, DEPTH) as layer:
                load_ffn(0, layer)
                for j, (kind, c0, c1) in enumerate(MIX):
                    u = U_MIX + j
                    load(u, chunk_pair(u % 2, [in_v[layer, :, :, c0:c0 + P], in_v[layer, :, :, c1:c1 + P]], KD), u % 2)
                    if j == 1:
                        sp.wait_ge(acc_done, 1 + A_MIX)
                        sp.dma_start(cos_sin[:, :, :], rope_tab.rearrange("a p t -> p a t")).then_inc(rope_landed, 16)
                        sp.dma_start(rope_mats[:, :, :], mats[4:9].rearrange("m p c -> p m c")).then_inc(rope_landed, 16)
                with sp.Fori(0, KD // 2) as i:
                    for s in range(2):
                        u = U_MERGE + 3 * s
                        cols = [sp.snap(C_GT + (2 * i + s) * P + b * D) for b in range(3)]
                        m = sp.snap((2 * i + s) * P)
                        load(u + 6 * i, chunk_pair(u % 2, [in_v[layer, :, :, bass.ds(c, P)] for c in cols[:2]], KD), u % 2)
                        load(u + 1 + 6 * i, chunk_pair((u + 1) % 2, [in_v[layer, :, :, bass.ds(cols[2], P)],
                                                                     branch_v[layer, :, 0:KD, bass.ds(m, P)]], KD), (u + 1) % 2)
                        load(u + 2 + 6 * i, [(w_raw[:, u % 2, 0, 2 * a:2 * a + 2, :],
                                              branch_v[layer, :, KD + 2 * a:KD + 2 * a + 2, bass.ds(m, P)]) for a in range(2)], u % 2)
                for j in range(OUT_UNITS):
                    u = U_OUT + j
                    load(u, chunk_pair(u % 2, [out_v[layer, :, :, (2 * j + c) * P:(2 * j + c + 1) * P] for c in range(2)], KD), u % 2)
                load_ffn(1, layer)
                other = sp.snap((DEPTH - 1) - layer)
                for u in range(2):
                    load(UNITS + u, chunk_pair(u, [gu_v[bass.ds(other, 1), 0, :, :, c * FF + u * P:c * FF + (u + 1) * P]
                                                   .rearrange("o p k c -> p (o k) c") for c in range(2)], KD), u)
                for s in raw_landed:
                    sp.wait_ge(s, 32 * (UNITS // 2 + 1))
                sp.wait_ge(arrived, ENGINES - 1)
                for s in (*PER_LAYER, arrived):
                    sp.sem_clear(s)
                for s in (*acc_free, *aux_free, acc_done, alo_ready):
                    sp.sem_inc(s, 1)
                for s in raw_landed:
                    sp.sem_inc(s, 32)
                sp.sem_inc(whi_ready, 2)
                sp.sem_inc(wlo_ready, 4 + 2)
                sp.sem_inc(layer_go, 1)

            for i in range(SEQ // P):
                sp.wait_ge(out_copied[i % 2], i // 2 + 1)
                sp.dma_start(out[0, i * P:(i + 1) * P, :], rows_v[:, i * D:(i + 1) * D]).then_inc(out_stored[i % 2], 16)
            for s in out_stored:
                sp.wait_ge(s, 16 * (SEQ // P // 2))

        def split_part(t, slot, kind, part):
            if kind == "full":
                return t[:, slot, part, :, :]
            if kind == "last_k":
                return t[:, slot, part, 0:DOWN_K[2], :]
            return t[:, slot, 0, 2 * part:2 * part + 2, :]

        def split_wait(u, part=1):
            return 2 * u + part + 5

        @block.gpsimd
        def _(pool):
            def clear_mixer():
                for s in OF_MIXER:
                    pool.sem_clear(s)
                pool.sem_inc(mlo_ready, 1)

            def clear_stream():
                for s in OF_STREAM:
                    pool.sem_clear(s)

            def w_rest(u, slot, kind="full"):
                for part in range(2):
                    pool.wait_ge(whi_ready, 2 * u + part + 1)
                    nc.gpsimd.tensor_tensor(split_part(w_lo, slot, kind, part), split_part(w_raw, slot, kind, part),
                                            split_part(w_hi, slot, kind, part).bitcast(F32), ALU.subtract)\
                        .then_inc(wlo_ready, 1)

            def add_results(p):
                for k in range(KD):
                    pool.wait_ge(res_ready, KD * OUT_TURN[p] + k + 1)
                    nc.gpsimd.tensor_tensor(h[:, k, :], h[:, k, :], tmp[:, 2 + k % 2, :], ALU.add).then_inc(h_ready, 1)

            def br_rest(g, dst):
                pool.wait_ge(brhi_ready, g + 1)
                src = tmp[:, 4 + g % 2, :] if g < KB else ya_f[g - KB][:, :]
                nc.gpsimd.tensor_tensor(dst[1][:, g % KB, :], src, dst[0][:, g % KB, :].bitcast(F32),
                                        ALU.subtract).then_inc(brlo_ready, 1)

            def ffn(f):
                u0 = U_FFN[f]
                with pool.Fori(0, UP_UNITS // 2) as i:
                    for s in range(2):
                        w_rest(u0 + 2 * i + s + 1, (s + 1) % 2)
                        n = f * KF + 2 * i + s
                        pool.wait_ge(ahi_ready, n + 1)
                        nc.gpsimd.tensor_tensor(a_lo[:, bass.ds(2 * i + s, 1), :], tmp[:, 2 + s:3 + s, :],
                                                a_hi[:, bass.ds(2 * i + s, 1), :].bitcast(F32), ALU.subtract)\
                            .then_inc(alo_ready, 1)
                if f == 1:
                    clear_mixer()
                for q in range(DOWN_UNITS):
                    w_rest(u0 + UP_UNITS + q + 1, (q + 1) % 2, "last_k" if q % 3 == 1 else "full")

            for s in (*acc_free, *aux_free, acc_done, alo_ready, mlo_ready):
                pool.sem_inc(s, 1)
            pool.sem_inc(wlo_ready, 4)
            pool.sem_inc(res_ready, 2 * KD)
            pool.sem_inc(h_ready, 2 * KD)
            pool.sem_inc(sq_ready, KD)
            pool.sem_inc(sq_added, KD - 2)
            pool.sem_inc(xhi_ready, KD)
            pool.sem_inc(layer_go, 1)
            w_rest(0, 0)
            with pool.Fori(0, DEPTH) as layer:
                ffn(0)
                add_results(0)
                for j in range(N_MIX):
                    w_rest(U_MIX + j + 1, (U_MIX + j + 1) % 2)
                    if j == FIRST_FILL + 1:
                        clear_stream()
                for g in range(2 * KB):
                    br_rest(g, yc if g < KB else ya)
                with pool.Fori(0, KD // 2) as i:
                    for s in range(2):
                        for r in range(3):
                            u = U_MERGE + 3 * s + r
                            w_rest(u + 1 + 6 * i, (u + 1) % 2, "branch2" if r == 1 else "full")
                        m = bass.ds(2 * i + s, 1)
                        pool.wait_ge(mhi_ready, 2 * i + s + 1)
                        nc.gpsimd.tensor_tensor(mg_lo[:, m, :], tmp[:, 3 * s:3 * s + 1, :],
                                                mg_hi[:, m, :].bitcast(F32), ALU.subtract).then_inc(mlo_ready, 1)
                for j in range(OUT_UNITS):
                    w_rest(U_OUT + j + 1, (U_OUT + j + 1) % 2)
                add_results(1)
                ffn(1)
                layer_used(pool)
                add_results(2)
                next_layer(pool, layer)

        @block.scalar
        def _(act):
            A = nc.scalar.activation

            def w_round(u, slot, kind="full"):
                act.wait_ge(raw_landed[slot], 32 * (u // 2 + 1) if isinstance(u, int) else u)
                for part in range(2):
                    A(split_part(w_hi, slot, kind, part), split_part(w_raw, slot, kind, part), ACT.Copy).then_inc(whi_ready, 1)

            def w_round_loop(u0, i, per, slot, kind="full", parts=(0, 1)):
                act.wait_ge(raw_landed[slot], 32 * (u0 // 2 + 1) + 16 * per * i)
                for part in parts:
                    A(split_part(w_hi, slot, kind, part), split_part(w_raw, slot, kind, part), ACT.Copy).then_inc(whi_ready, 1)

            def square_h(p, hi, gains):
                turn = IN_TURN[p]
                for k in range(KD):
                    act.wait_ge(h_ready, KD * turn + k + 1)
                    A(hi[:, k, :], h[:, k, :], ACT.Copy, scale=gains[:, k:k + 1]).then_inc(xhi_ready, 1)
                    if k >= 3:
                        act.wait_ge(sq_added, (KD - 2) * turn + k - 2)
                    A(tmp[:, k % 2 if k else 4, :], h[:, k, :], ACT.Square).then_inc(sq_ready, 1)

            def rstd_seed(q, scale=1.0 / D):
                take_aux(act, ("norm", q))
                A(halves(tmp[:, 3, :]), aux_halves(aux_of(("norm", q))), ACT.Ln, scale=scale, bias=eps_col[:, :])\
                    .then_inc(log_ready, 1)
                act.wait_ge(log_ready, q + 1)
                A(tmp[:, 3, :], tmp[:, 3, :], ACT.Exp, scale=-0.5).then_inc(seed_ready, 1)

            def take_y(p, n, m):
                act.wait_ge(acc_done, 1 + n + 1)
                if m >= 3:
                    act.wait_ge(ysum, (KD - 2) * p + m - 2)
                A(halves(tmp[:, 2 + m % 2 if m else 4, :]), acc_halves(SLOT[n]), ACT.Square).then_inc(ysq_ready, 1)
                A(halves(y[:, m, :]), acc_halves(SLOT[n]), ACT.Copy).then_inc(acc_free[SLOT[n]], 1)

            def round_x(chunks):
                for k in chunks:
                    act.wait_ge(xf_ready, k + 1)
                    A(x_hi[:, k, :], tmp[:, k % 2, :], ACT.Copy).then_inc(xnhi_ready, 1)

            def ffn(f):
                u0, n0 = U_FFN[f], A_FFN[f]
                nc.scalar.preload_act_table(ACT.Silu)

                def up_unit(i, s, first=False):
                    nn = n0 + 2 * s
                    if first:
                        for c in range(2):
                            act.wait_ge(acc_done, 1 + nn + c + 1)
                            A(halves(tmp[:, c, :]), acc_halves(SLOT[nn + c]), ACT.Copy).then_inc(acc_free[SLOT[nn + c]], 1)
                        act.wait_ge(first_scaled, 2 * f + 1)
                    else:
                        act.wait_ge(acc_free[SLOT[nn]], USE[nn] + 2 * i + 2)
                    A(tmp[:, s, :], tmp[:, s, :], ACT.Silu).then_inc(silu_ready, 1)
                    act.wait_ge(acc_done, 1 + nn + 4 * i + 2)
                    w_round_loop(u0 + s + 2, i, 2, s)
                    act.wait_ge(act_ready, f * KF + 2 * i + s + 1)
                    A(a_hi[:, bass.ds(2 * i + s, 1), :], tmp[:, 2 + s:3 + s, :], ACT.Copy).then_inc(ahi_ready, 1)

                up_unit(0, 0, first=True)
                up_unit(0, 1)
                with act.Fori(1, UP_UNITS // 2) as i:
                    for s in range(2):
                        up_unit(i, s)
                n1 = n0 + 2 * UP_UNITS

                def down_unit(i, q, skip=False):
                    if q == 0:
                        act.wait_ge(acc_done, 1 + n1 + 4 * i)
                        skip = skip or i == 0
                    elif q == 3:
                        act.wait_ge(acc_done, 1 + n1 + 2 + 4 * i)
                    else:
                        act.wait_ge(part_done, f * KD + 4 * i + {1: 1, 2: 2, 4: 3, 5: 4}[q])
                    if not skip:
                        w_round_loop(u0 + UP_UNITS + q + 1, i, 6, (q + 1) % 2, "last_k" if q % 3 == 1 else "full")
                    if q % 3 == 2:
                        for c in range(2):
                            m = 4 * i + 2 * (q // 3) + c
                            if m == 0:
                                act.wait_ge(alo_ready, 1 + KF * (f + 1))
                            if m == KD - 1:
                                nc.scalar.preload_act_table_set(LN_EXP_SET)
                            take_y(2 * f, n1 + m, m)

                for i in range(KD // 4):
                    for q in range(6):
                        down_unit(i, q)
                rstd_seed(1 + 4 * f)
                if f == 0:
                    mixer_weights(0)

            def evac(n, dst, func=ACT.Copy, **kw):
                act.wait_ge(acc_done, 1 + n + 1)
                A(halves(dst), acc_halves(SLOT[n]), func, **kw).then_inc(acc_free[SLOT[n]], 1)

            def evac_tokens(n, pair, dst):
                act.wait_ge(acc_done, 1 + n + 1)
                for a, b in enumerate(pair):
                    rows = BL[b][1]
                    src, d = dst(b, acc[0:rows, 2 * SLOT[n] + a, :])
                    ins = A(d, src, ACT.Copy)
                ins.then_inc(acc_free[SLOT[n]], 1)

            def mixer_weights(j):
                act.wait_ge(acc_done, 1 + A_UNIT[j])
                w_round(U_MIX + j + 1, (U_MIX + j + 1) % 2)

            def mixer_unit(j):
                mixer_weights(j)
                mixer_out(j)

            def mixer_out(j, chunks=(0, 1)):
                kind, c0, _ = MIX[j]
                n = A_UNIT[j]
                if kind == "qi":
                    for c in range(2):
                        evac(n + c, qi_t[:, c, :])
                elif kind == "k":
                    if 0 in chunks:
                        evac(n, tmp[:, 4, :])
                    if 1 in chunks:
                        act.wait_ge(rstd_ready, 3)
                        evac(n + 1, tmp[:, 3, :])
                elif kind == "q":
                    for c in range(2):
                        evac(n + c, q_t[:, (c0 - C_Q) // P + c, :])
                elif kind in ("v", "mv"):
                    for a, pair in enumerate(((0, 1), (2, 3), (4,))):
                        if kind == "v":
                            evac_tokens(n + a, pair, lambda b, s: (s[:, 0:P], v_tok[0:BL[b][1], b, :]))
                        else:
                            m0 = (c0 - C_MV) // P
                            evac_tokens(n + a, pair, lambda b, s: (
                                s[:, 0:2 * P].rearrange("p (m c) -> p m c", m=2),
                                mv_tok[0:BL[b][1], b, m0:m0 + 2, 0:P]))
                elif kind == "if":
                    for c in range(2):
                        act.wait_ge(acc_done, 1 + n + c + 1)
                        slot = SLOT[n + c]
                        A(tmp[0:NM, 4 + c, :].rearrange("p (a t) -> p a t", a=HALF),
                          acc[0:NM, 2 * slot:2 * slot + 2, 0:TH], ACT.Identity,
                          bias=gate_bias_cur[:, c:c + 1]).then_inc(acc_free[slot], 1)
                elif kind == "mq":
                    for c in range(2):
                        evac(n + c, mq_t[:, (c0 - C_MQ) // P + c, :])
                elif kind == "mk":
                    for c in range(2):
                        evac(n + c, mk_t[:, (c0 - C_MK) // P + c, :], scale=float(P) ** -0.5)

            def filled(g):
                j, c, k = FIRST_FILL + g // (2 * KD), g // KD % 2, g % KD
                kind, c0, _ = MIX[j]
                n = A_UNIT[j] + c
                if c == 0 and k == 0:
                    act.wait_ge(acc_done, 1 + n)
                    w_round(U_MIX + j + 1, (U_MIX + j + 1) % 2)
                if k == KD - 1 and kind == "mo":
                    evac(n, mo_t[:, (c0 - C_MO) // P + c, :], ACT.Tanh, scale=0.5)
                elif k == KD - 1 and kind == "cxc" and c == 0:
                    if j > FIRST_CONV:
                        act.wait_ge(acc_free[0], USE[n])
                    evac(n, cx_t[:, :])

            def index_rel(b, i):
                g = NIDX * (b - 1) + i
                n = BL[b][1]
                key = ("index", b, i)
                act.wait_ge(aux_done, AUX[key] + 1)
                if g == 0:
                    act.wait_ge(rope_done, 2)
                if g >= 2:
                    act.wait_ge(index_step, g - 1)
                A(tmp[0:n, g % 2, 0:KL[b]], aux[0:n, aux_of(key), 0:KL[b]], ACT.Relu, scale=float(DH) ** -0.5)\
                    .then_inc(aux_free[aux_of(key)], 1)

            def attention():
                g = Steps(act, gate_step)
                act.wait_ge(index_step, NIDX * (NB - 1))
                n = A_UNIT[5]
                for c in range(2):
                    act.wait_ge(acc_free[SLOT[n + c]], USE[n + c] + 2)
                g.did(A(tmp[0:NM, 0, :], tmp[0:NM, 5, :], ACT.Abs))
                g.settle()
                g.did(A(tmp[0:NM, 0, :], tmp[0:NM, 0, :], ACT.Exp, scale=-1.0))
                g.settle()
                g.did(A(tmp[0:NM, 0, :], tmp[0:NM, 0, :], ACT.Ln, bias=1.0))
                act.dma_start(sel_sb[:, :, :], sel).then_inc(sel_landed, 16)
                nc.scalar.preload_act_table_set(TANH_SET)
                for t in range(NA + O_LAG):
                    if t:
                        for f in att_fills(t - 1):
                            filled(f)
                    if t < NA:
                        b, hd = divmod(t, NH)
                        n = BL[b][1]
                        act.wait_ge(negmax_ready, t + 1)
                        A(prob[0:n, t % 2, 0:KL[b]], prob[0:n, t % 2, 0:KL[b]], ACT.Exp, bias=neg_max[0:n, t % 2:t % 2 + 1],
                          accum_out=row_sum[0:n, b % 2, hd:hd + 1]).then_inc(p_ready, 1)
                    if 1 <= t <= NA:
                        s = t - 1
                        b = s // NH
                        n = BL[b][1]
                        act.wait_ge(p_turned, s + 1)
                        if s >= 2:
                            act.wait_ge(pv_done, s - 1)
                        ins = A(prob_t[:, s % 2, 0:n], acc[:, 2, 0:n], ACT.Copy)
                        if b:
                            ins = A(prob_t[0:QB, s % 2, n:n * (b + 1)], acc[0:QB, 2, n:n * (b + 1)], ACT.Copy)
                        ins.then_inc(pt_copied, 1)
                    if t >= NH - 1 + O_LAG and (t - O_LAG) % NH == NH - 1:
                        b = (t - O_LAG) // NH
                        t0, n = BL[b]
                        take_aux(act, ("turn", b))
                        A(yb_hi[:, :, t0:t0 + n],
                          aux[:, aux_of(("turn", b)), 0:KB * n].rearrange("p (j t) -> p j t", j=KB),
                          ACT.Copy).then_inc(ybhi_ready, 1)
                    if t == GATE_STEP:
                        take_aux(act, ("gate_cols",))
                        s = aux_of(("gate_cols",))
                        for which, dst, func in ((0, c_tok, ACT.Copy), (1, floor_tok, ACT.Exp)):
                            v = aux[:, s, NB * NM * which:NB * NM * (which + 1)].rearrange("p (b m) -> p b m", m=NM)
                            A(dst[:, 0, :], v[:, 0, :], func)
                            ins = A(dst[0:QB, 1:NB, :], v[0:QB, 1:NB, :], func)
                        ins.then_inc(aux_free[s], 1)

            def mlstm():
                def square(m, b):
                    i = NB * m + b
                    n = BL[b][1]
                    act.wait_ge(num_read, i + 1)
                    if i >= 1:
                        act.wait_ge(mh_squared, i)
                    A(tmp[0:n, 0, 0:P], m_h[0:n, b, m, :], ACT.Square,
                      accum_out=m_ss[0:n, NM * b + m:NM * b + m + 1]).then_inc(mh_squared, 1)

                for step in range(NB * (NM + 1)):
                    m, c = divmod(step, NB)
                    if m < NM:
                        key = ("stab", m)
                        if c == 0:
                            take_aux(act, key)
                            if m >= 2:
                                act.wait_ge(arg_ready, NB * (m - 1))
                            A(tmp[:, 1 + m % 2, :], aux[:, aux_of(key), 0:T], ACT.Copy).then_inc(aux_free[aux_of(key)], 1)
                        k0, nk = BL[c]
                        act.wait_ge(arg_ready, step + 1)
                        A(tmp[0:nk, 3 + step % 2, k0:T], tmp[0:nk, 3 + step % 2, k0:T], ACT.Exp).then_inc(decay_ready, 1)
                    i = step - NB
                    if i >= 0:
                        n = BL[c][1]
                        act.wait_ge(num_done, i + 1)
                        if i >= 2:
                            act.wait_ge(num_read, i - 1)
                        A(den[0:n, i % 2:i % 2 + 1], acc[0:n, 2 + i % 2, P:P + 1], ACT.Abs).then_inc(den_abs, 1)
                    for f in ml_fills(step):
                        filled(f)
                    if i >= 1:
                        square(*divmod(i - 1, NB))
                square(NM - 1, NB - 1)
                nc.scalar.preload_act_table_set(LN_EXP_SET)
                act.wait_ge(mh_step, 1)
                A(m_r[:, :], m_var[:, :], ACT.Ln).then_inc(mh_act, 1)
                act.wait_ge(mh_act, 1)
                A(m_r[:, :], m_r[:, :], ACT.Exp, scale=-0.5).then_inc(mh_act, 1)
                nc.scalar.preload_act_table_set(TANH_SET)
                for m in range(KB):
                    free_aux(act, ("hturn", m))
                    A(yc_hi[:, m, :], tmp[:, 4 + m % 2, :], ACT.Copy).then_inc(brhi_ready, 1)
                act.wait_ge(acc_free[0], USE[A_MERGE - 1] + 2)
                for c in range(KB):
                    A(ya_hi[:, c, :], ya_f[c][:, :], ACT.Copy).then_inc(brhi_ready, 1)

            w_round(0, 0)
            for i in range(SEQ // P):
                for j in range(2):
                    e = 2 * i + j
                    act.wait_ge(io_turned, 2 + e + 1)
                    A(h[:, 4 * j:4 * j + 4, META + i * P:META + (i + 1) * P],
                      acc[:, e % 4, :].rearrange("p (k t) -> p k t", k=4), ACT.Copy).then_inc(io_placed, 1)
            act.wait_ge(layer_go, 1)
            act.wait_ge(io_first, 2)
            act.wait_ge(io_placed, 2 * (SEQ // P))
            square_h(0, x_hi, params)

            with act.Fori(0, DEPTH) as layer:
                nc.scalar.preload_act_table_set(LN_EXP_SET)
                w_round(1, 1)
                rstd_seed(0)
                ffn(0)
                act.wait_ge(cur_ready, N_CUR)
                square_h(1, xu_hi, cur[:, 2 * KD:3 * KD])
                rstd_seed(2)
                mixer_out(0)
                mixer_weights(1)
                round_x(range(KD // 2))
                mixer_out(1, (0,))
                round_x(range(KD // 2, KD))
                mixer_out(1, (1,))
                for j in range(2, 5):
                    mixer_unit(j)
                take_aux(act, ("wi",))
                s = aux_of(("wi",))
                A(wi_tok[0:QB, 1:NB, :], aux[0:QB, s, 0:(NB - 1) * P].rearrange("p (b c) -> p b c", b=NB - 1)[:, :, DH:DH + NIDX],
                  ACT.Copy, scale=float(NIDX) ** -0.5).then_inc(aux_free[s], 1)
                for b in range(1, NB):
                    for i in range(NIDX):
                        index_rel(b, i)
                    for j in UNITS_AFTER[b]:
                        mixer_unit(j)
                attention()
                mlstm()
                with act.Fori(0, KD // 2) as i:
                    for s in range(2):
                        nn = A_MERGE + 6 * s
                        for r in range(3):
                            u = U_MERGE + 3 * s + r
                            act.wait_ge(acc_done, 1 + nn + (0, 2, 5)[r] + 12 * i)
                            w_round_loop(u + 1, i, 6, (u + 1) % 2, "branch2" if r == 1 else "full",
                                         (1,) if r == 2 else (0, 1))
                            for c in ((0, 1), (0,), ())[r]:
                                g = 2 * r + c
                                act.wait_ge(acc_done, 1 + nn + g + 12 * i + 1)
                                act.wait_ge(mlo_ready, 1 + 2 * i + s)
                                A(halves(tmp[:, 3 * s + g, :]), acc_halves(SLOT[nn + g]), ACT.Tanh, scale=0.5)\
                                    .then_inc(acc_free[SLOT[nn + g]], 1)
                            if r == 1:
                                w_round_loop(u + 2, i, 6, u % 2, parts=(0,))
                        act.wait_ge(mf_ready, 2 * i + s + 1)
                        A(mg_hi[:, bass.ds(2 * i + s, 1), :], tmp[:, 3 * s:3 * s + 1, :], ACT.Copy).then_inc(mhi_ready, 1)
                for j in range(OUT_UNITS):
                    n = A_OUT + 2 * j
                    act.wait_ge(acc_done, 1 + n)
                    w_round(U_OUT + j + 1, (U_OUT + j + 1) % 2)
                    if j == 0:
                        act.wait_ge(mlo_ready, 1 + KD)
                    for c in range(2):
                        if 2 * j + c == KD - 1:
                            nc.scalar.preload_act_table_set(LN_EXP_SET)
                        take_y(1, n + c, 2 * j + c)
                rstd_seed(3, 0.25 / D)
                act.wait_ge(acc_done, 1 + A_FFN[1])
                w_round(U_FFN[1] + 1, 1)
                square_h(2, x_hi, cur[:, 4 * KD:5 * KD])
                rstd_seed(4)
                ffn(1)
                layer_used(act)
                square_h(0, x_hi, next_gain)
                next_layer(act, layer)

            for i in range(1, SEQ // P, 2):
                act.wait_ge(out_turned, i + 1)
                A(w_raw[:, i // 2, i % 2, :, :].rearrange("p k c -> p (k c)"), out_tile(i), ACT.Copy).then_inc(out_copied[1], 1)

        @block.vector
        def _(dve):
            V = nc.vector

            def variance(q, scale):
                dve.wait_ge(log_ready, q + 1)
                s = aux_of(("norm", q))
                V.tensor_scalar(halves(tmp[:, 2, :]), aux_halves(s), scale, EPS, ALU.mult, ALU.add).then_inc(aux_free[s], 1)

            def rstd(q):
                key = ("norm", q)
                dve.wait_ge(aux_free[aux_of(key)], AUX[key] // 2 + 2)
                dve.wait_ge(seed_ready, q + 1)
                V.tensor_tensor(tmp[:, 2, :], tmp[:, 2, :], tmp[:, 3, :], ALU.mult).then_inc(newton, 1)
                dve.wait_ge(newton, 2 * q + 1)
                V.scalar_tensor_tensor(tmp[:, 2, :], tmp[:, 2, :], -0.5, tmp[:, 3, :], ALU.mult, ALU.mult).then_inc(newton, 1)
                dve.wait_ge(newton, 2 * q + 2)
                V.scalar_tensor_tensor(tmp[:, 5, :], tmp[:, 2, :], 1.5, tmp[:, 3, :], ALU.add, ALU.mult).then_inc(rstd_ready, 1)
                dve.wait_ge(rstd_ready, q + 1)

            def gain_of(s, k):
                return cur[:, G_NORM + s * KD + k:G_NORM + s * KD + k + 1]

            def result(p, k):
                if k >= 2:
                    dve.wait_ge(h_ready, KD * OUT_TURN[p] + k - 1)
                V.scalar_tensor_tensor(tmp[:, 2 + k % 2, :], y[:, k, :], gain_of(2 * p + 1, k), tmp[:, 5, :],
                                       ALU.mult, ALU.mult).then_inc(res_ready, 1)

            def add_squares(p, k):
                turn = IN_TURN[p]
                dve.wait_ge(sq_ready, KD * turn + k + 1)
                if k >= 2:
                    dve.wait_ge(sq_added, (KD - 2) * turn + k - 1)
                V.tensor_tensor(tmp[:, 4, :], tmp[:, 4, :], tmp[:, k % 2, :], ALU.add).then_inc(sq_added, 1)

            def norm_out(p, scale, p_in):
                variance(2 * p + 1, scale)
                rstd(2 * p + 1)
                if p == 2:
                    layer_used(dve)
                for k in range(KD + 1):
                    if k < KD:
                        result(p, k)
                    if k >= 3:
                        add_squares(p_in, k - 2)

            def norm_in_late(p, hi, lo):
                def rest(chunks):
                    for k in chunks:
                        dve.wait_ge(xhi_ready, KD * IN_TURN[p] + k + 1)
                        V.scalar_tensor_tensor(lo[:, k, :], h[:, k, :], gain_of(2 * p, k), hi[:, k, :].bitcast(F32),
                                               ALU.mult, ALU.subtract).then_inc(xlo_ready, 1)

                rest(range(KD - 1))
                variance(2 * p, 1.0 / D)
                rest(range(KD - 1, KD))
                rstd(2 * p)

            def norm_in(p):
                for k in range(KD + 1):
                    if k < KD:
                        if k >= 2:
                            dve.wait_ge(xnlo_ready, k - 1)
                        V.scalar_tensor_tensor(tmp[:, k % 2, :], h[:, k, :], gain_of(2 * p, k), tmp[:, 5, :],
                                               ALU.mult, ALU.mult).then_inc(xf_ready, 1)
                    if k >= 1:
                        dve.wait_ge(xnhi_ready, k)
                        V.tensor_tensor(x_lo[:, k - 1, :], tmp[:, (k - 1) % 2, :], x_hi[:, k - 1, :].bitcast(F32),
                                        ALU.subtract).then_inc(xnlo_ready, 1)

            def add_y_squares(p):
                for m in range(1, KD - 1):
                    dve.wait_ge(ysq_ready, KD * p + m + 1)
                    if m >= 2:
                        dve.wait_ge(ysum, (KD - 2) * p + m - 1)
                    V.tensor_tensor(tmp[:, 4, :], tmp[:, 4, :], tmp[:, 2 + m % 2, :], ALU.add).then_inc(ysum, 1)

            def ffn(f):
                n0 = A_FFN[f]

                def up_unit(i, s, first=False):
                    nn = n0 + 2 * s
                    g_slot, u_slot = SLOT[nn], SLOT[nn + 1]
                    if first:
                        for c, slot in enumerate((g_slot, u_slot)):
                            dve.wait_ge(acc_free[slot], USE[nn + c] + 2)
                            V.tensor_tensor(tmp[:, c, :], tmp[:, c, :], tmp[:, 5, :], ALU.mult).then_inc(first_scaled, 1)
                        dve.wait_ge(first_scaled, 2 * f + 2)
                        dve.wait_ge(alo_ready, 1 + f * KF)
                        dve.wait_ge(silu_ready, f * KF + 1)
                        V.tensor_tensor(tmp[:, 2, :], tmp[:, 1, :], tmp[:, 0, :], ALU.mult).then_inc(act_ready, 1)
                        dve.wait_ge(act_ready, f * KF + 1)
                        return
                    dve.wait_ge(acc_done, 1 + nn + 4 * i + 1)
                    V.tensor_tensor(halves(tmp[:, s, :]), acc_halves(g_slot), halves(tmp[:, 5, :]), ALU.mult)\
                        .then_inc(acc_free[g_slot], 1)
                    dve.wait_ge(acc_done, 1 + nn + 4 * i + 2)
                    dve.wait_ge(alo_ready, 1 + f * KF + 2 * i + s)
                    V.tensor_tensor(halves(tmp[:, 2 + s, :]), acc_halves(u_slot), halves(tmp[:, 5, :]), ALU.mult)\
                        .then_inc(acc_free[u_slot], 1)
                    dve.wait_ge(acc_free[u_slot], USE[nn + 1] + 2 * i + 2)
                    dve.wait_ge(silu_ready, f * KF + 2 * i + s + 1)
                    V.tensor_tensor(tmp[:, 2 + s, :], tmp[:, 2 + s, :], tmp[:, s, :], ALU.mult).then_inc(act_ready, 1)

                up_unit(0, 0, first=True)
                up_unit(0, 1)
                with dve.Fori(1, UP_UNITS // 2) as i:
                    for s in range(2):
                        up_unit(i, s)
                p = 2 * f
                add_y_squares(p)
                norm_out(p, 1.0 / D, (p + 1) % 3)

            def rope_all():
                r = Steps(dve, rope_step)
                dve.wait_ge(rope_landed, 32)
                dve.wait_ge(xnlo_ready, KD)
                cos, sin = cos_sin[:, 0, :], cos_sin[:, 1, :]
                for table in (cos, sin):
                    r.did(V.tensor_tensor(table, table, tmp[:, 5, :], ALU.mult))
                r.settle()

                def rotated(i):
                    dst = qi_t[:, i, :] if i < 2 else q_t[:, i - 2, :]
                    key = ("rot", i)
                    take_aux(dve, key)
                    V.tensor_tensor(tmp[:, i % 2, :], aux[:, aux_of(key), 0:T], sin, ALU.mult).then_inc(aux_free[aux_of(key)], 1)
                    r.did(V.tensor_tensor(dst, dst, cos, ALU.mult))
                    r.settle()
                    dve.wait_ge(aux_free[aux_of(key)], AUX[key] // 2 + 2)
                    ins = V.tensor_tensor(dst, dst, tmp[:, i % 2, :], ALU.add)
                    if i == 1 + KB:
                        ins.then_inc(rope_done, 1)
                    else:
                        r.did(ins)
                        r.settle()

                rotated(0)
                rotated(1)
                for i in range(3):
                    dst = ki_t[:, :] if i == 0 else k_t[:, i - 1, :]
                    key, key2 = ("dup", i), ("dup_rot", i)
                    take_aux(dve, key)
                    V.tensor_tensor(dst, aux[:, aux_of(key), 0:T], cos, ALU.mult).then_inc(aux_free[aux_of(key)], 1)
                    take_aux(dve, key2)
                    V.tensor_tensor(tmp[:, i % 2, :], aux[:, aux_of(key2), 0:T], sin, ALU.mult).then_inc(aux_free[aux_of(key2)], 1)
                    for kk in (key, key2):
                        dve.wait_ge(aux_free[aux_of(kk)], AUX[kk] // 2 + 2)
                    if i == 0:
                        V.tensor_tensor(tmp[:, 3, :], tmp[:, 3, :], tmp[:, 5, :], ALU.mult).then_inc(wi_scaled, 1)
                    ins = V.tensor_tensor(dst, dst, tmp[:, i % 2, :], ALU.add)
                    if i < 2:
                        r.did(ins)
                        r.settle()
                ins.then_inc(rope_done, 1)
                dve.wait_ge(rope_done, 1)
                for i in range(2, 2 + KB):
                    rotated(i)
                dve.wait_ge(rope_done, 2)
                V.tensor_copy(mask[:, 0:P], causal_bias[:, :]).then_inc(mask_ready, 1)

            def select_keys(b, k):
                n, kl, t0 = BL[b][1], KL[b], BL[b][0]
                score, work = tmp[0:n, 2, 0:kl], tmp[0:n, 3, 0:kl]
                for i in range(NIDX):
                    g = NIDX * (b - 1) + i
                    key = ("index", b, i)
                    dve.wait_ge(aux_free[aux_of(key)], AUX[key] // 2 + 2)
                    if g == 0:
                        s = aux_of(("wi",))
                        dve.wait_ge(aux_free[s], AUX[("wi",)] // 2 + 2)
                    if i == 0:
                        V.tensor_scalar(score, tmp[0:n, g % 2, 0:kl], wi_tok[0:n, b, i:i + 1], None, ALU.mult).then_inc(index_step, 1)
                    else:
                        V.scalar_tensor_tensor(score, tmp[0:n, g % 2, 0:kl], wi_tok[0:n, b, i:i + 1], score,
                                               ALU.mult, ALU.add).then_inc(index_step, 1)
                    dve.wait_ge(index_step, g + 1)
                k.did(V.tensor_tensor(tmp[0:n, 2, t0:kl], tmp[0:n, 2, t0:kl], causal_bias[0:n, 0:n], ALU.add))
                k.settle()
                for i in range(TOPK // 8):
                    src = score if i == 0 else work
                    k.did(V.max(top8[0:n, :], src))
                    k.settle()
                    k.did(V.match_replace(work, top8[0:n, :], src, TAKEN))
                    k.settle()
                V.tensor_scalar(mask[0:n, MO[b]:MO[b] + kl], work, TAKEN / 2, NEG, ALU.is_gt, ALU.mult).then_inc(mask_ready, 1)

            GATE_OPS = 8

            def gate_op(g, i):
                row = lambda r: tmp[0:NM, r, :]
                if i == 0:
                    dve.wait_ge(gate_step, 3)
                    g.did(V.tensor_scalar(row(1), row(5), 0.0, None, ALU.min))
                elif i == 1:
                    g.did(V.tensor_tensor(row(1), row(1), row(0), ALU.subtract))
                elif i == 2:
                    g.did(V.memset(row(0), 1.0))
                elif i == 3:
                    g.did(V.tensor_tensor_scan(row(5), row(0), row(1), 0.0, ALU.mult, ALU.add))
                elif i == 4:
                    g.did(V.tensor_tensor(row(4), row(4), row(5), ALU.subtract))
                elif i == 5:
                    g.did(V.tensor_tensor_scan(row(1), row(4), row(4), 0.0, ALU.max, ALU.max))
                elif i == 6:
                    g.did(V.scalar_tensor_tensor(row(0), row(1), -1.0, row(5), ALU.mult, ALU.subtract))
                else:
                    V.tensor_scalar(row(5), row(1), -1.0, None, ALU.mult).then_inc(gates_ready, 1)
                if i < GATE_OPS - 1:
                    g.settle()

            def filled(g):
                j, c, k = FIRST_FILL + g // (2 * KD), g // KD % 2, g % KD
                if k < KD - 1 or j < FIRST_CONV:
                    return
                n = A_UNIT[j] + c
                pair, of_pair = divmod(j - FIRST_CONV, 3)
                if of_pair < 2 and c == 1:
                    y_c = 2 * pair + of_pair
                    tap = lambda i: cur[:, G_CONV + KB * i + y_c:G_CONV + KB * i + y_c + 1]
                    t = ya_f[y_c][:, :]
                    dve.wait_ge(acc_free[0], USE[n - 1] + 2)
                    dve.wait_ge(acc_done, 1 + n + 1)
                    V.tensor_tensor(halves(conv_u[:, 2:T + 2]), acc_halves(0), halves(cx_t[:, :]), ALU.mult)\
                        .then_inc(acc_free[0], 1)
                    dve.wait_ge(acc_free[0], USE[n] + 2)
                    taps.did(V.tensor_scalar(t, conv_u[:, 0:T], tap(0), None, ALU.mult))
                    taps.settle()
                    taps.did(V.scalar_tensor_tensor(t, conv_u[:, 1:T + 1], tap(1), t, ALU.mult, ALU.add))
                    taps.settle()
                    taps.did(V.scalar_tensor_tensor(t, conv_u[:, 2:T + 2], tap(2), t, ALU.mult, ALU.add))
                    taps.settle()
                elif of_pair == 2:
                    t = ya_f[2 * pair + c][:, :]
                    dve.wait_ge(acc_done, 1 + n + 1)
                    V.tensor_tensor(halves(t), acc_halves(0), halves(t), ALU.mult).then_inc(acc_free[0], 1)

            def attention():
                def finish(b):
                    n = BL[b][1]
                    dve.wait_ge(pv_done, NH * (b + 1))
                    if b:
                        dve.wait_ge(o_read, b)
                    V.reciprocal(row_inv[0:n, :], row_sum[0:n, b % 2, :]).then_inc(inv_ready, 1)
                    dve.wait_ge(inv_ready, b + 1)
                    V.tensor_tensor(tmp[0:n, 2 + b % 2, 0:BW].rearrange("p (h d) -> p h d", h=NH),
                                    acc[0:n, 3, :].rearrange("p (h d) -> p h d", h=NH),
                                    row_inv[0:n, :].unsqueeze(2).to_broadcast([n, NH, DH]), ALU.mult).then_inc(o_read, 1)

                def turned(b):
                    t0, n = BL[b]
                    s = aux_of(("turn", b))
                    dve.wait_ge(ybhi_ready, b + 1)
                    V.tensor_tensor(yb_lo[:, :, t0:t0 + n], aux[:, s, 0:KB * n].rearrange("p (j t) -> p j t", j=KB),
                                    yb_hi[:, :, t0:t0 + n].bitcast(F32), ALU.subtract).then_inc(aux_free[s], 1)

                dve.wait_ge(mask_ready, NB)
                V.memset(conv_u[:, 0:2], 0.0).then_inc(merge_step, 1)
                dve.wait_ge(merge_step, 1)
                g = Steps(dve, gate_rows)
                for t in range(NA + O_LAG):
                    if t:
                        for f in att_fills(t - 1):
                            filled(f)
                    if 1 <= t <= GATE_OPS:
                        gate_op(g, t - 1)
                    if t < NA:
                        b = t // NH
                        n, kl = BL[b][1], KL[b]
                        key = ("score", t)
                        s = aux_of(key)
                        take_aux(dve, key)
                        if t >= 2:
                            dve.wait_ge(p_turned, t - 1)
                            dve.wait_ge(negmax_ready, t - 1)
                        V.tensor_tensor_reduce(prob[0:n, t % 2, 0:kl], aux[0:n, s, 0:kl], mask[0:n, MO[b]:MO[b] + kl],
                                               float(DH) ** -0.5, TAKEN, ALU.add, ALU.max, row_max[0:n, t % 2:t % 2 + 1])\
                            .then_inc(aux_free[s], 1)
                        dve.wait_ge(aux_free[s], AUX[key] // 2 + 2)
                        V.tensor_scalar(neg_max[0:n, t % 2:t % 2 + 1], row_max[0:n, t % 2:t % 2 + 1], -1.0, None, ALU.mult)\
                            .then_inc(negmax_ready, 1)
                    if t >= NH + 1 and (t - 2) % NH == NH - 1:
                        finish((t - 2) // NH)
                    if t >= NH - 1 + O_LAG and (t - O_LAG) % NH == NH - 1:
                        turned((t - O_LAG) // NH)

            def mlstm():
                V.memset(mv_tok[:, :, :, P:P + 1], 1.0).then_inc(cols_ready, 1)
                V.memset(m_ss[:, :], 1.0).then_inc(cols_ready, 1)
                s0 = aux_of(("gate_cols",))
                dve.wait_ge(aux_free[s0], AUX[("gate_cols",)] // 2 + 2)

                def arg(m, c):
                    k0, nk = BL[c]
                    i = NB * m + c
                    if c == 0:
                        key = ("stab", m)
                        dve.wait_ge(aux_free[aux_of(key)], AUX[key] // 2 + 2)
                    V.tensor_scalar(tmp[0:nk, 3 + i % 2, k0:T], tmp[0:nk, 1 + m % 2, k0:T], c_tok[0:nk, c, m:m + 1], 0.0,
                                    ALU.add, ALU.min).then_inc(arg_ready, 1)

                def weights(m, c):
                    k0, nk = BL[c]
                    i = NB * m + c
                    key = ("qk", m, c)
                    sl = aux_of(key)
                    take_aux(dve, key)
                    dve.wait_ge(decay_ready, i + 1)
                    if m >= 2 and c == 0:
                        dve.wait_ge(num_done, NB * (m - 1))
                    wt = m_wt[m % 2]
                    V.tensor_tensor(wt[0:nk, WT[c]:WT[c + 1]], aux[0:nk, sl, 0:T - k0], tmp[0:nk, 3 + i % 2, k0:T], ALU.mult)\
                        .then_inc(aux_free[sl], 1)
                    dve.wait_ge(aux_free[sl], AUX[key] // 2 + 2)
                    diagonal = wt[0:nk, WT[c]:WT[c] + nk]
                    V.tensor_tensor(diagonal, diagonal, causal_keep[0:nk, 0:nk], ALU.mult).then_inc(wt_ready, 1)

                def values(m, b):
                    i = NB * m + b
                    n = BL[b][1]
                    d = den[0:n, i % 2:i % 2 + 1]
                    dve.wait_ge(den_abs, i + 1)
                    V.tensor_tensor(d, d, floor_tok[0:n, b, m:m + 1], ALU.max).then_inc(den_step, 1)
                    dve.wait_ge(den_step, 2 * i + 1)
                    V.reciprocal(d, d).then_inc(den_step, 1)
                    dve.wait_ge(den_step, 2 * i + 2)
                    V.tensor_scalar(m_h[0:n, b, m, :], acc[0:n, 2 + i % 2, 0:P], d, None, ALU.mult).then_inc(num_read, 1)

                for step in range(NB * (NM + 1)):
                    m, c = divmod(step, NB)
                    if m < NM:
                        if c == 0:
                            if m:
                                dve.wait_ge(wt_ready, step)
                            arg(m, 0)
                        if c + 1 < NB:
                            if step >= 1:
                                dve.wait_ge(wt_ready, step)
                            arg(m, c + 1)
                    if step:
                        for f in ml_fills(step - 1):
                            filled(f)
                    if m < NM:
                        weights(m, c)
                    if m >= 1:
                        values(m - 1, c)
                for f in ml_fills(NB * (NM + 1) - 1):
                    filled(f)
                dve.wait_ge(wt_ready, NB * NM)
                s = Steps(dve, mh_step)
                dve.wait_ge(mh_squared, NB * NM)
                s.did(V.tensor_scalar(m_var[:, :], m_ss[:, :], 1.0 / P, EPS, ALU.mult, ALU.add))
                s.settle()
                n = A_UNIT[FIRST_FILL] + 3
                dve.wait_ge(acc_free[0], USE[n] + 2)
                s.did(V.tensor_scalar(mo_t[:, :, :], mo_t[:, :, :], 1.0, None, ALU.add))
                dve.wait_ge(mh_act, 2)
                s.did(V.tensor_tensor(m_var[:, :], m_var[:, :], m_r[:, :], ALU.mult))
                s.settle()
                s.did(V.scalar_tensor_tensor(m_var[:, :], m_var[:, :], -0.5, m_r[:, :], ALU.mult, ALU.mult))
                s.settle()
                s.did(V.scalar_tensor_tensor(m_r[:, :], m_var[:, :], 1.5, m_r[:, :], ALU.add, ALU.mult))
                s.settle()
                for b in range(NB):
                    n = BL[b][1]
                    V.tensor_tensor(m_h[0:n, b, :, :], m_h[0:n, b, :, :],
                                    m_r[0:n, NM * b:NM * b + NM].unsqueeze(2).to_broadcast([n, NM, P]), ALU.mult)\
                        .then_inc(mh_normed, 1)
                for f in range(FILLS - ML_TAIL, FILLS):
                    filled(f)
                for m in range(NM):
                    key = ("hturn", m)
                    sl = aux_of(key)
                    take_aux(dve, key)
                    if m >= 2:
                        dve.wait_ge(brlo_ready, m - 1)
                    gain = cur[:, G_HEAD + m:G_HEAD + m + 1]
                    V.scalar_tensor_tensor(tmp[:, 4 + m % 2, 0:P], aux[:, sl, 0:P], gain, mo_t[:, m, 0:P], ALU.mult, ALU.mult)
                    V.scalar_tensor_tensor(tmp[:, 4 + m % 2, P:T].rearrange("p (b t) -> p b t", t=QB),
                                           aux[:, sl, P:NB * P].rearrange("p (b t) -> p b t", t=P)[:, :, 0:QB], gain,
                                           mo_t[:, m, P:T].rearrange("p (b t) -> p b t", t=QB), ALU.mult, ALU.mult)\
                        .then_inc(aux_free[sl], 1)
                    free_aux(dve, key)

            def merge():
                with dve.Fori(0, KD // 2) as i:
                    for s in range(2):
                        nn = A_MERGE + 6 * s
                        for b in range(3):
                            g = 3 + b
                            sl = SLOT[nn + g]
                            gsl = SLOT[nn + b]
                            dve.wait_ge(acc_free[gsl], USE[nn + b] + 6 * i + 2)
                            dve.wait_ge(acc_done, 1 + nn + g + 12 * i + 1)
                            t = tmp[:, 3 * s + b, :]
                            V.scalar_tensor_tensor(halves(t), halves(t), 1.0, acc_halves(sl), ALU.add, ALU.mult)\
                                .then_inc(acc_free[sl], 1)
                            dve.wait_ge(acc_free[sl], USE[nn + g] + 6 * i + 2)
                            if b == 1:
                                V.tensor_tensor(tmp[:, 3 * s, :], tmp[:, 3 * s, :], t, ALU.add).then_inc(merge_step, 1)
                                dve.wait_ge(merge_step, 2 * i + s + 2)
                        V.tensor_tensor(tmp[:, 3 * s, :], tmp[:, 3 * s, :], tmp[:, 3 * s + 2, :], ALU.add).then_inc(mf_ready, 1)

            dve.wait_ge(io_turned, 1)
            dve.wait_ge(const_landed, 16 * 4)
            V.tensor_copy(params[:, :], aux[:, 0, 0:P]).then_inc(io_first, 1)
            dve.wait_ge(io_turned, 2)
            V.tensor_copy(h[:, :, 0:META], aux[:, 1, 0:KD * META].rearrange("p (k t) -> p k t", k=KD)).then_inc(io_first, 1)
            V.memset(eps_col[:, :], EPS)
            dve.wait_ge(layer_go, 1)
            for k in range(1, KD - 1):
                add_squares(0, k)
            dve.wait_ge(later_landed, 16 * 5)

            with dve.Fori(0, DEPTH) as layer:
                c = Steps(dve, cur_ready)
                c.did(V.tensor_copy(cur[:, G_NORM:G_CONV], params[:, bass.ds(layer * 6 * KD, 6 * KD)]))
                c.did(V.tensor_copy(cur[:, G_CONV:G_HEAD], params[:, bass.ds(layer * 3 * KB + DEPTH * 6 * KD, 3 * KB)]))
                c.did(V.tensor_copy(cur[:, G_HEAD:G_HEAD + NM],
                                    params[:, bass.ds(layer * NM + DEPTH * (6 * KD + 3 * KB), NM)]))
                c.did(V.tensor_copy(gate_bias_cur[:, :].unsqueeze(2), gate_bias[:, :, bass.ds(layer, 1)]))
                c.settle()
                for s in (1, 3, 5):
                    v = cur[:, G_NORM + s * KD:G_NORM + (s + 1) * KD]
                    c.did(V.tensor_scalar(v, v, 0.5, None, ALU.mult))
                v = cur[:, G_HEAD:G_HEAD + NM]
                c.did(V.tensor_scalar(v, v, 0.5, None, ALU.mult))
                c.settle()
                norm_in_late(0, x_hi, x_lo)
                c.did(V.tensor_copy(next_gain[:, :], params[:, bass.ds((DEPTH - 1) * 6 * KD - layer * 6 * KD, KD)]))
                assert c.n == N_CUR
                ffn(0)
                norm_in_late(1, xu_hi, xu_lo)
                norm_in(1)
                rope_all()
                k = Steps(dve, topk_step)
                taps = Steps(dve, conv_step)
                for b in range(1, NB):
                    select_keys(b, k)
                attention()
                mlstm()
                merge()
                add_y_squares(1)
                norm_out(1, 0.25 / D, 2)
                norm_in_late(2, x_hi, x_lo)
                ffn(1)
                next_layer(dve, layer)

            for i in range(0, SEQ // P, 2):
                dve.wait_ge(out_turned, i + 1)
                V.tensor_copy(w_raw[:, i // 2, i % 2, :, :].rearrange("p k c -> p (k c)"), out_tile(i)).then_inc(out_copied[0], 1)

        @block.tensor
        def _(pe):
            MM = nc.tensor.matmul

            def open_acc(n, later=0):
                pe.wait_ge(acc_free[SLOT[n]], USE[n] + later + 1)

            def open_aux(key):
                pe.wait_ge(aux_free[aux_of(key)], AUX[key] // 2 + 1)

            def chunk(slot, wslot, c, xs, k0, kn, wk0=0, first=True, last=True):
                for k in range(kn):
                    lh, ll = w_hi[:, wslot, c, wk0 + k, :], w_lo[:, wslot, c, wk0 + k, :]
                    for j, (w, xx) in enumerate(((lh, xs[0]), (lh, xs[1]), (ll, xs[0]))):
                        for a in range(HALF):
                            ins = MM(acc[:, 2 * slot + a, 0:TH], w, xx[:, k0 + k, a * TH:(a + 1) * TH],
                                     start=(first and k == 0 and j == 0), stop=(last and k == kn - 1 and j == 2))
                return ins

            def token_blocks(n, wslot, pair, cn):
                slot = SLOT[n]
                open_acc(n)
                for a, b in enumerate(pair):
                    t0, rows = BL[b]
                    for k in range(KD):
                        for j in range(3):
                            xx, w = ((x_hi, w_hi), (x_lo, w_hi), (x_hi, w_lo))[j]
                            ins = MM(acc[0:rows, 2 * slot + a, 0:cn * P].rearrange("p (c n) -> p c n", c=cn),
                                     xx[:, k, t0:t0 + rows], w[:, wslot, 0:cn, k, :],
                                     start=(k == 0 and j == 0), stop=(k == KD - 1 and j == 2))
                ins.then_inc(acc_done, 1)

            def norm_sum(q, last, added, add_count, squared, square_count):
                key = ("norm", q)
                open_aux(key)
                pe.wait_ge(added, add_count)
                for a in range(HALF):
                    MM(aux_halves(aux_of(key))[:, a, :], ones[:, :], tmp[:, 4, a * TH:(a + 1) * TH], start=True, stop=False)
                pe.wait_ge(squared, square_count)
                for a in range(HALF):
                    ins = MM(aux_halves(aux_of(key))[:, a, :], ones[:, :], tmp[:, last, a * TH:(a + 1) * TH], start=False, stop=True)
                ins.then_inc(aux_done, 1)

            def y_norm_sum(q, p):
                norm_sum(q, 2 + (KD - 1) % 2, ysum, (KD - 2) * (p + 1), ysq_ready, KD * (p + 1))

            def first_unit(n0, p, hi, lo):
                for c in range(2):
                    open_acc(n0 + c)

                def passes(k, ws_xs, last):
                    for c in range(2):
                        slot = SLOT[n0 + c]
                        for j, (w, xx) in enumerate(ws_xs):
                            for a in range(HALF):
                                ins = MM(acc[:, 2 * slot + a, 0:TH], w[:, 0, c, k, :], xx[:, k, a * TH:(a + 1) * TH],
                                         start=(k == 0 and j == 0 and xx is hi), stop=(last and j == len(ws_xs) - 1))
                        if last:
                            ins.then_inc(acc_done, 1)

                for k in range(KD):
                    pe.wait_ge(xhi_ready, KD * IN_TURN[p] + k + 1)
                    passes(k, ((w_hi, hi), (w_lo, hi)), False)
                turn = IN_TURN[p] + 1
                norm_sum(2 * p, (KD - 1) % 2, sq_added, (KD - 2) * turn, sq_ready, KD * turn)
                for k in range(KD):
                    pe.wait_ge(xlo_ready, KD * p + k + 1)
                    passes(k, ((w_hi, lo),), k == KD - 1)

            def ffn(f):
                u0, n0 = U_FFN[f], A_FFN[f]
                def up_unit(i, s):
                    for c in range(2):
                        pe.wait_ge(wlo_ready, split_wait(u0 + s + 2 * i, c))
                        n = n0 + 2 * s + c
                        open_acc(n, 2 * i)
                        chunk(SLOT[n], s, c, (x_hi, x_lo), 0, KD).then_inc(acc_done, 1)

                pe.wait_ge(wlo_ready, split_wait(u0))
                first_unit(n0, 2 * f, x_hi, x_lo)
                up_unit(0, 1)
                with pe.Fori(1, UP_UNITS // 2) as i:
                    for s in range(2):
                        up_unit(i, s)
                n1 = n0 + 2 * UP_UNITS
                with pe.Fori(0, KD // 4) as i:
                    for q in range(6):
                        kg = q % 3
                        pe.wait_ge(alo_ready, 1 + KF * f + kg * KD + DOWN_K[kg])
                        for c in range(2):
                            pe.wait_ge(wlo_ready, split_wait(u0 + UP_UNITS + q + 6 * i, c))
                            n = n1 + 2 * (q // 3) + c
                            if kg == 0:
                                open_acc(n, 2 * i)
                            ins = chunk(SLOT[n], q % 2, c, (a_hi, a_lo), kg * KD, DOWN_K[kg], 0, kg == 0, kg == 2)
                            if kg == 2:
                                ins.then_inc(acc_done, 1)
                        if kg < 2:
                            ins.then_inc(part_done, 1)
                y_norm_sum(4 * f + 1, 2 * f)

            def mixer_acc(j, c):
                kind, n, ws = MIX[j][0], A_UNIT[j] + c, (U_MIX + j) % 2
                if kind in ("v", "mv"):
                    pe.wait_ge(wlo_ready, split_wait(U_MIX + j))
                    token_blocks(n, ws, ((0, 1), (2, 3), (4,))[c], 1 if kind == "v" else 2)
                else:
                    pe.wait_ge(wlo_ready, split_wait(U_MIX + j, c))
                    open_acc(n)
                    chunk(SLOT[n], ws, c, (xu_hi, xu_lo) if j < N_EARLY else (x_hi, x_lo), 0, KD).then_inc(acc_done, 1)

            def mixer_unit(j):
                for c in range(N_MIXACC[j]):
                    mixer_acc(j, c)

            def over_tokens(key, lhsT, rhs, n0, n1, rows=P):
                s = aux_of(key)
                open_aux(key)
                for a, z in ((0, 512), (512, 1024)):
                    if a < n1 - n0:
                        e = min(z, n1 - n0)
                        ins = MM(aux[0:rows, s, a:e], lhsT, rhs[:, n0 + a:n0 + e], start=True, stop=True)
                ins.then_inc(aux_done, 1)

            def in_sbuf(j):
                for n in (A_UNIT[j], A_UNIT[j] + 1):
                    pe.wait_ge(acc_free[SLOT[n]], USE[n] + 2)

            def rotate(i):
                over_tokens(("rot", i), rope_mats[:, ROT, :], qi_t[:, i, :] if i < 2 else q_t[:, i - 2, :], 0, T)

            def duplicate(i):
                src, d, r = ((3, DUP0, DROT0), (4, DUP0, DROT0), (4, DUP1, DROT1))[i]
                over_tokens(("dup", i), rope_mats[:, d, :], tmp[:, src, :], 0, T)
                over_tokens(("dup_rot", i), rope_mats[:, r, :], tmp[:, src, :], 0, T)

            def early_units():
                mixer_unit(1)
                mixer_acc(2, 0)
                pe.wait_ge(rope_landed, 32)
                in_sbuf(0)
                rotate(0)
                rotate(1)
                mixer_acc(2, 1)
                in_sbuf(1)
                duplicate(0)
                mixer_acc(3, 0)
                duplicate(1)
                mixer_acc(3, 1)
                duplicate(2)
                pe.wait_ge(xnlo_ready, KD)
                mixer_acc(4, 0)
                in_sbuf(2)
                rotate(2)
                rotate(3)
                mixer_acc(4, 1)
                in_sbuf(3)
                rotate(4)
                rotate(5)
                mixer_acc(4, 2)
                pe.wait_ge(wi_scaled, 1)
                key = ("wi",)
                open_aux(key)
                for b in range(1, NB):
                    t0, n = BL[b]
                    ins = nc.tensor.transpose(aux[0:n, aux_of(key), (b - 1) * P:b * P], tmp[:, 3, t0:t0 + n], ident[:, :])
                ins.then_inc(aux_done, 1)

            def fill(g):
                j, c, k = FIRST_FILL + g // (2 * KD), g // KD % 2, g % KD
                n = A_UNIT[j] + c
                if k == 0:
                    pe.wait_ge(wlo_ready, split_wait(U_MIX + j, c))
                    open_acc(n)
                ins = chunk(0, (U_MIX + j) % 2, c, (x_hi, x_lo), k, 1, k, k == 0, k == KD - 1)
                if k == KD - 1:
                    ins.then_inc(acc_done, 1)

            def attention():
                pe.wait_ge(rope_done, 2)
                for c in range(2):
                    n = A_UNIT[FIRST_FILL] - 1 - c
                    pe.wait_ge(acc_free[SLOT[n]], USE[n] + 2)
                for t in range(NA + O_LAG):
                    if t < NA:
                        b, hd = divmod(t, NH)
                        t0, n = BL[b]
                        po = DH * (hd % 2)
                        over_tokens(("score", t), q_t[po:po + DH, hd // 2, t0:t0 + n],
                                    k_t[po:po + DH, hd // (NH // NKV), :], 0, KL[b], n)
                        for f in att_fills(t)[:1]:
                            fill(f)
                    if 1 <= t <= NA:
                        s = t - 1
                        b = s // NH
                        n = BL[b][1]
                        pe.wait_ge(p_ready, s + 1)
                        if s >= 1:
                            pe.wait_ge(pt_copied, s)
                        for c in range(b + 1):
                            k0, nk = BL[c]
                            ins = nc.tensor.transpose(acc[0:nk, 2, c * n:(c + 1) * n], prob[0:n, s % 2, k0:k0 + nk],
                                                      ident[0:n, 0:n])
                        ins.then_inc(p_turned, 1)
                    if 2 <= t <= NA + 1:
                        s = t - 2
                        b, hd = divmod(s, NH)
                        n = BL[b][1]
                        g = hd // (NH // NKV)
                        pe.wait_ge(pt_copied, s + 1)
                        if hd == 0 and b >= 1:
                            pe.wait_ge(o_read, b)
                        for c in range(b + 1):
                            nk = BL[c][1]
                            ins = MM(acc[0:n, 3, hd * DH:(hd + 1) * DH], prob_t[0:nk, s % 2, c * n:(c + 1) * n],
                                     v_tok[0:nk, c, g * DH:(g + 1) * DH], start=(c == 0), stop=(c == b))
                        ins.then_inc(pv_done, 1)
                    if t >= NH - 1 + O_LAG and (t - O_LAG) % NH == NH - 1:
                        b = (t - O_LAG) // NH
                        n = BL[b][1]
                        key = ("turn", b)
                        open_aux(key)
                        pe.wait_ge(o_read, b + 1)
                        for j in range(KB):
                            ins = nc.tensor.transpose(aux[:, aux_of(key), j * n:(j + 1) * n],
                                                      tmp[0:n, 2 + b % 2, j * P:(j + 1) * P], ident[0:n, 0:n])
                        ins.then_inc(aux_done, 1)

                    if t == GATE_STEP:
                        key = ("gate_cols",)
                        open_aux(key)
                        pe.wait_ge(gates_ready, 1)
                        for which, r in ((0, 4), (1, 0)):
                            for b in range(NB):
                                t0, n = BL[b]
                                o = NM * (NB * which + b)
                                ins = nc.tensor.transpose(aux[0:n, aux_of(key), o:o + NM], tmp[0:NM, r, t0:t0 + n],
                                                          ident[0:NM, 0:NM])
                        ins.then_inc(aux_done, 1)
                    for f in att_fills(t)[1 if t < NA else 0:]:
                        fill(f)

            def mlstm():
                pe.wait_ge(sel_landed, 16)
                pe.wait_ge(cols_ready, 2)

                def qk(m, c):
                    k0, nk = BL[c]
                    over_tokens(("qk", m, c), mk_t[:, m, k0:k0 + nk], mq_t[:, m, :], k0, T, nk)

                def stab(m):
                    over_tokens(("stab", m), sel_sb[:, m, :], tmp[0:NM, 5, :], 0, T)

                stab(0)
                for step in range(NB * (NM + 1)):
                    m, b = divmod(step, NB)
                    if m < NM:
                        qk(m, b)
                    i = step - NB
                    if i >= 0:
                        t0, n = BL[b]
                        pe.wait_ge(wt_ready, i + 1)
                        if i >= 2:
                            pe.wait_ge(num_read, i - 1)
                        for c in range(b + 1):
                            k0, nk = BL[c]
                            o = WT[c] + t0 - k0
                            ins = MM(acc[0:n, 2 + i % 2, 0:P + 1], m_wt[(m - 1) % 2][0:nk, o:o + n], mv_tok[0:nk, c, m - 1, :],
                                     start=(c == 0), stop=(c == b))
                        ins.then_inc(num_done, 1)
                    if b == NB - 1 and m + 1 < NM:
                        stab(m + 1)
                    for f in ml_fills(step):
                        fill(f)
                for f in range(FILLS - ML_TAIL, FILLS):
                    fill(f)
                pe.wait_ge(mh_normed, NB)
                for m in range(NM):
                    key = ("hturn", m)
                    open_aux(key)
                    for b in range(NB):
                        n = BL[b][1]
                        ins = nc.tensor.transpose(aux[:, aux_of(key), b * P:b * P + n], m_h[0:n, b, m, :], ident[0:n, 0:n])
                    ins.then_inc(aux_done, 1)
                pe.wait_ge(num_read, NB * NM)

            pe.wait_ge(const_landed, 16 * 4)
            nc.tensor.transpose(aux[:, 0, 0:P], tmp[:, 5, 0:P], ident[:, :]).then_inc(io_turned, 1)
            pe.wait_ge(io_in, 16)
            for k in range(KD):
                ins = nc.tensor.transpose(aux[:, 1, k * META:(k + 1) * META], tmp[0:META, k // 4, (k % 4) * P:(k % 4 + 1) * P],
                                          ident[0:META, 0:META])
            ins.then_inc(io_turned, 1)
            for i in range(SEQ // P):
                pe.wait_ge(x_landed[i], 16)
                for j in range(2):
                    e = 2 * i + j
                    if e >= 4:
                        pe.wait_ge(io_placed, e - 3)
                    for k in range(4):
                        ins = nc.tensor.transpose(acc[:, e % 4, k * P:(k + 1) * P], x_rows[:, i, (4 * j + k) * P:(4 * j + k + 1) * P],
                                                  ident[:, :])
                    ins.then_inc(io_turned, 1)
            pe.wait_ge(io_placed, 2 * (SEQ // P))
            pe.wait_ge(io_first, 2)
            pe.wait_ge(later_landed, 16 * 5)
            pe.wait_ge(layer_go, 1)

            with pe.Fori(0, DEPTH) as layer:
                ffn(0)
                pe.wait_ge(wlo_ready, split_wait(U_MIX))
                first_unit(A_MIX, 1, xu_hi, xu_lo)
                early_units()
                pe.wait_ge(rope_done, 1)
                for b in range(1, NB):
                    t0, n = BL[b]
                    for i in range(NIDX):
                        po = DH * (i % 2)
                        over_tokens(("index", b, i), qi_t[po:po + DH, i // 2, t0:t0 + n], ki_t[po:po + DH, :], 0, KL[b], n)
                    for j in UNITS_AFTER[b]:
                        mixer_unit(j)
                attention()
                mlstm()
                with pe.Fori(0, KD // 2) as i:
                    for s in range(2):
                        nn = A_MERGE + 6 * s
                        u = U_MERGE + 3 * s
                        for r, parts in enumerate((((0, "x", 0), (1, "x", 0)), ((0, "x", 0), (1, ya, 0), (1, yb, KB)),
                                                   ((0, yc, 0),))):
                            for a, (c, xs, wk0) in enumerate(parts):
                                pe.wait_ge(wlo_ready, split_wait(u + r + 6 * i, 1 if r == 2 else c))
                                n = nn + 2 * r + a + (1 if r == 2 else 0)
                                if xs == ya:
                                    pe.wait_ge(brlo_ready, 2 * KB)
                                open_acc(n, 6 * i)
                                full = xs == "x"
                                chunk(SLOT[n], (u + r) % 2, c, (x_hi, x_lo) if full else xs, 0, KD if full else KB, wk0)\
                                    .then_inc(acc_done, 1)
                for j in range(OUT_UNITS):
                    u = U_OUT + j
                    for c in range(2):
                        pe.wait_ge(wlo_ready, split_wait(u, c))
                        n = A_OUT + 2 * j + c
                        open_acc(n)
                        for k in range(KD):
                            if n == A_OUT:
                                pe.wait_ge(mlo_ready, 1 + k + 1)
                            ins = chunk(SLOT[n], u % 2, c, (mg_hi, mg_lo), k, 1, k, k == 0, k == KD - 1)
                        ins.then_inc(acc_done, 1)
                y_norm_sum(3, 1)
                ffn(1)
                layer_used(pe)
                next_layer(pe, layer)

            for k in range(KD):
                pe.wait_ge(h_ready, KD * OUT_TURN[2] + k + 1)
                for i in range(SEQ // P):
                    ins = nc.tensor.transpose(out_tile(i)[:, k * P:(k + 1) * P], h[:, k, META + i * P:META + (i + 1) * P],
                                              ident[:, :])
                    if k == KD - 1:
                        ins.then_inc(out_turned, 1)


def shape_constants(meta_rows, seq, head_dim):
    import numpy as np

    t = meta_rows + seq
    freq = (1.0 / (10000.0 ** (np.arange(0, head_dim, 2, dtype=np.float32) / head_dim))).astype(np.float32)
    angle = np.arange(t, dtype=np.float32)[None, :] * freq[np.arange(P) % (head_dim // 2)][:, None]
    tables = np.stack([np.cos(angle), np.sin(angle)]).astype(np.float32)
    half = head_dim // 2
    i = np.arange(P)
    rot = np.zeros((P, P), np.float32)
    rot[(i + half) % head_dim + i // head_dim * head_dim, i] = np.where(i % head_dim < half, -1.0, 1.0)
    dup = np.zeros((2, P, P), np.float32)
    for g in range(2):
        dup[g, g * head_dim + i % head_dim, i] = 1.0
    tri = i[None, :] <= i[:, None]
    mats = np.stack([np.eye(P), np.ones((P, P)), np.where(tri, 0.0, NEG), tri.T, rot, dup[0], dup[1],
                     dup[0] @ rot, dup[1] @ rot]).astype(np.float32)
    sel = np.zeros((4, 4, P), np.float32)
    sel[np.arange(4), np.arange(4)] = 1.0
    return {"rope_tab": tables, "mats": mats, "sel": sel}


_INS = ["x", "meta", "norm_g", "w_ffn_gu", "w_ffn_down", "w_in", "w_conv", "b_igate", "b_fgate",
        "mh_norm_g", "w_branch", "w_out"]


def kernel(**inputs):
    import numpy as np
    import concourse.bacc as bacc
    from concourse.bass_utils import run_bass_kernel_spmd

    nc = bacc.Bacc("TRN2", target_bir_lowering=False, num_devices=1)
    arrays, args = {}, []
    data = {name: np.ascontiguousarray(inputs[name]) for name in _INS}
    data.update(shape_constants(data["meta"].shape[0], data["x"].shape[1], 64))
    for name, a in data.items():
        arrays[f"in_{name}_dram"] = a
        args.append(nc.dram_tensor(f"in_{name}_dram", a.shape, mybir.dt.from_np(a.dtype), kind="ExternalInput").ap())
    out = nc.dram_tensor("out_dram", data["x"].shape, F32, kind="ExternalOutput").ap()
    trunk_program(nc, *args, out)
    r = run_bass_kernel_spmd(nc, [arrays], core_ids=[0])
    return r.results[0]["out_dram"]
```
